# Optimizing a Trainium2 kernel written in Bass

```python
import math
import jax, jax.numpy as jnp
from jax import lax
import numpy as np

D_MODEL = 1024
BATCH = 1
SEQ = 256
DEPTH = 2

CHUNK = 64
N_BRANCH = 4
BR_WIDTH = D_MODEL // 4
POOL_WINDOWS = (2, 4, 8, 16)
POOL_GROUPS = len(POOL_WINDOWS)
POOL_GW = BR_WIDTH // POOL_GROUPS
DIFF_HEADS = 4
DIFF_QK_DIM = BR_WIDTH // (2 * DIFF_HEADS)
DIFF_V_DIM = 2 * DIFF_QK_DIM
ROPE_THETA = 10000.0
Q_BLOCK = 128
CONV_WIDTH = 31
SGU_LEN = 128
SGU_GROUPS = 4
SGU_GW = BR_WIDTH // SGU_GROUPS
D_FF = 2816
N_EXPERTS = 8
TOP_K = 2
D_FF_EXPERT = 3584
N_DENSE = (DEPTH + 1) // 2
N_MOE = DEPTH // 2
EPS = 1e-6
NEG_INF = -1e30

IN_A = BR_WIDTH
IN_Q = DIFF_HEADS * 2 * DIFF_QK_DIM
IN_K = DIFF_HEADS * 2 * DIFF_QK_DIM
IN_V = DIFF_HEADS * DIFF_V_DIM
IN_C = 2 * BR_WIDTH
IN_D = 2 * BR_WIDTH
D_IN = IN_A + IN_Q + IN_K + IN_V + IN_C + IN_D

kernel_name = "hybrid_gated_pool_diffattn_conv_sgu_moe"

def rmsnorm(x, g):
    xf = x.astype(jnp.float32)
    y = xf * lax.rsqrt(jnp.mean(xf * xf, axis=-1, keepdims=True) + EPS)
    return (y * g.astype(jnp.float32)).astype(x.dtype)

def layernorm(x, g, b):
    xf = x.astype(jnp.float32)
    mu = jnp.mean(xf, axis=-1, keepdims=True)
    xc = xf - mu
    y = xc * lax.rsqrt(jnp.mean(xc * xc, axis=-1, keepdims=True) + EPS)
    return (y * g.astype(jnp.float32) + b.astype(jnp.float32)).astype(x.dtype)

def rope_tables(seq, dim):
    pos = jnp.arange(seq, dtype=jnp.float32)
    inv = 1.0 / (ROPE_THETA ** (jnp.arange(0, dim, 2, dtype=jnp.float32) / dim))
    ang = pos[:, None] * inv[None, :]
    return jnp.cos(ang), jnp.sin(ang)

def apply_rope(x, cos, sin):
    c = cos[None, :, None, None, :].astype(x.dtype)
    s = sin[None, :, None, None, :].astype(x.dtype)
    x1, x2 = jnp.split(x, 2, axis=-1)
    return jnp.concatenate([x1 * c - x2 * s, x2 * c + x1 * s], axis=-1)

def pool_mixer(a, pool_w, pool_scale):
    B, S, C = a.shape
    af = a.astype(jnp.float32)
    cs = jnp.concatenate([jnp.zeros((B, 1, C), jnp.float32), jnp.cumsum(af, axis=1)], axis=1)
    t = jnp.arange(S)
    outs = []
    for g, w in enumerate(POOL_WINDOWS):
        lo = jnp.maximum(t + 1 - w, 0)
        csg = cs[:, :, g * POOL_GW:(g + 1) * POOL_GW]
        win_sum = csg[:, 1:] - csg[:, lo]
        cnt = (t + 1 - lo).astype(jnp.float32)[None, :, None]
        outs.append(win_sum / cnt - af[..., g * POOL_GW:(g + 1) * POOL_GW])
    p = jnp.stack(outs, axis=2).astype(a.dtype)
    y = jnp.einsum('bsgc,gcd->bsgd', p, pool_w)
    return y.reshape(B, S, C) * pool_scale

def diff_attention(q, k, v, qn_g, kn_g, lq1, lk1, lq2, lk2, subln_g, layer_idx, cos, sin):
    B, S, _ = q.shape
    q = q.reshape(B, S, DIFF_HEADS, 2, DIFF_QK_DIM)
    k = k.reshape(B, S, DIFF_HEADS, 2, DIFF_QK_DIM)
    v = v.reshape(B, S, DIFF_HEADS, DIFF_V_DIM).transpose(0, 2, 1, 3)
    q = apply_rope(rmsnorm(q, qn_g), cos, sin).transpose(0, 3, 2, 1, 4)
    k = apply_rope(rmsnorm(k, kn_g), cos, sin).transpose(0, 3, 2, 1, 4)
    lam_init = 0.8 - 0.6 * math.exp(-0.3 * layer_idx)
    lam = (jnp.exp(jnp.sum(lq1.astype(jnp.float32) * lk1.astype(jnp.float32)))
           - jnp.exp(jnp.sum(lq2.astype(jnp.float32) * lk2.astype(jnp.float32))) + lam_init)
    scale = DIFF_QK_DIM ** -0.5
    chunk_id = jnp.arange(S) // CHUNK
    outs = []
    for qb in range(S // Q_BLOCK):
        q0 = qb * Q_BLOCK
        kend = q0 + Q_BLOCK
        s = jnp.einsum('bchqd,bchkd->bchqk', q[:, :, :, q0:kend], k[:, :, :, :kend]).astype(jnp.float32) * scale
        mask = chunk_id[q0:kend, None] >= chunk_id[None, :kend]
        p = jax.nn.softmax(jnp.where(mask, s, NEG_INF), axis=-1)
        a = p[:, 0] - lam * p[:, 1]
        outs.append(jnp.einsum('bhqk,bhkv->bhqv', a.astype(v.dtype), v[:, :, :kend]))
    o = jnp.concatenate(outs, axis=2)
    o = rmsnorm(o, subln_g) * (1.0 - lam_init)
    return o.transpose(0, 2, 1, 3).reshape(B, S, DIFF_HEADS * DIFF_V_DIM)

def conv_module(c_in, conv_w, conv_b, ln_g, ln_b):
    a, gt = jnp.split(c_in, 2, axis=-1)
    u = a * jax.nn.sigmoid(gt)
    y = lax.conv_general_dilated(
        u, conv_w[:, None, :], window_strides=(1,), padding=[(CONV_WIDTH - 1, 0)],
        dimension_numbers=('NWC', 'WIO', 'NWC'), feature_group_count=BR_WIDTH) + conv_b
    return jax.nn.silu(layernorm(y, ln_g, ln_b))

def spatial_gating(d_in, ln_g, ln_b, w_s, b_s):
    z = jax.nn.gelu(d_in, approximate=False)
    u, v = jnp.split(z, 2, axis=-1)
    v = layernorm(v, ln_g, ln_b)
    B, S, _ = v.shape
    v = v.reshape(B, S // SGU_LEN, SGU_LEN, SGU_GROUPS, SGU_GW)
    tri = jnp.tril(jnp.ones((SGU_LEN, SGU_LEN), dtype=bool))
    w = jnp.where(tri[None], w_s, jnp.zeros_like(w_s))
    sv = jnp.einsum('gts,bnsgc->bntgc', w, v) + b_s.T[None, None, :, :, None]
    return u * sv.reshape(B, S, BR_WIDTH)

def swiglu(h, w1, w3, w2):
    return (jax.nn.silu(h @ w1) * (h @ w3)) @ w2

def moe_ffn(h, router, w1, w3, w2):
    B, S, D = h.shape
    t = h.reshape(B * S, D)
    logits = (t @ router).astype(jnp.float32)
    top_v, top_i = lax.top_k(logits, TOP_K)
    top_w = jax.nn.softmax(top_v, axis=-1)
    gates = jnp.sum(jax.nn.one_hot(top_i, N_EXPERTS, dtype=jnp.float32) * top_w[..., None], axis=1)
    gates = gates.astype(t.dtype)
    out = jnp.zeros_like(t)
    for e in range(N_EXPERTS):
        out = out + gates[:, e:e + 1] * swiglu(t, w1[e], w3[e], w2[e])
    return out.reshape(B, S, D)

def setup_inputs(seed: int = 0) -> dict:
    key = jax.random.key(seed)
    ks = iter(jax.random.split(key, 40))

    def nrm(shape, scale):
        return jax.random.normal(next(ks), shape, jnp.float32) * scale

    def gain(shape):
        return 1.0 + nrm(shape, 0.02)

    L = DEPTH
    return {
        "x": nrm((BATCH, SEQ, D_MODEL), 1.0),
        "norm1_g": gain((L, D_MODEL)),
        "w_in": nrm((L, D_MODEL, D_IN), D_MODEL ** -0.5),
        "w_gate": nrm((L, D_MODEL, N_BRANCH * D_MODEL), D_MODEL ** -0.5),
        "b_gate": nrm((L, N_BRANCH * D_MODEL), 0.02),
        "w_branch": nrm((L, N_BRANCH, BR_WIDTH, D_MODEL), BR_WIDTH ** -0.5),
        "w_out": nrm((L, D_MODEL, D_MODEL), D_MODEL ** -0.5),
        "pool_w": nrm((L, POOL_GROUPS, POOL_GW, POOL_GW), POOL_GW ** -0.5),
        "pool_scale": gain((L, BR_WIDTH)),
        "attn_qn_g": gain((L, DIFF_QK_DIM)),
        "attn_kn_g": gain((L, DIFF_QK_DIM)),
        "lam_q1": nrm((L, DIFF_QK_DIM), 0.1),
        "lam_k1": nrm((L, DIFF_QK_DIM), 0.1),
        "lam_q2": nrm((L, DIFF_QK_DIM), 0.1),
        "lam_k2": nrm((L, DIFF_QK_DIM), 0.1),
        "attn_subln_g": gain((L, DIFF_V_DIM)),
        "conv_w": nrm((L, CONV_WIDTH, BR_WIDTH), CONV_WIDTH ** -0.5),
        "conv_b": nrm((L, BR_WIDTH), 0.02),
        "conv_ln_g": gain((L, BR_WIDTH)),
        "conv_ln_b": nrm((L, BR_WIDTH), 0.02),
        "sgu_ln_g": gain((L, BR_WIDTH)),
        "sgu_ln_b": nrm((L, BR_WIDTH), 0.02),
        "sgu_w": nrm((L, SGU_GROUPS, SGU_LEN, SGU_LEN), SGU_LEN ** -0.5),
        "sgu_b": gain((L, SGU_GROUPS, SGU_LEN)),
        "norm2_g": gain((L, D_MODEL)),
        "ffn_w1": nrm((N_DENSE, D_MODEL, D_FF), D_MODEL ** -0.5),
        "ffn_w3": nrm((N_DENSE, D_MODEL, D_FF), D_MODEL ** -0.5),
        "ffn_w2": nrm((N_DENSE, D_FF, D_MODEL), D_FF ** -0.5),
        "moe_router": nrm((N_MOE, D_MODEL, N_EXPERTS), D_MODEL ** -0.5),
        "moe_w1": nrm((N_MOE, N_EXPERTS, D_MODEL, D_FF_EXPERT), D_MODEL ** -0.5),
        "moe_w3": nrm((N_MOE, N_EXPERTS, D_MODEL, D_FF_EXPERT), D_MODEL ** -0.5),
        "moe_w2": nrm((N_MOE, N_EXPERTS, D_FF_EXPERT, D_MODEL), D_FF_EXPERT ** -0.5),
    }

def reference(x, norm1_g, w_in, w_gate, b_gate, w_branch, w_out, pool_w, pool_scale,
              attn_qn_g, attn_kn_g, lam_q1, lam_k1, lam_q2, lam_k2, attn_subln_g,
              conv_w, conv_b, conv_ln_g, conv_ln_b, sgu_ln_g, sgu_ln_b, sgu_w, sgu_b,
              norm2_g, ffn_w1, ffn_w3, ffn_w2, moe_router, moe_w1, moe_w3, moe_w2):
    B, S, D = x.shape
    cos, sin = rope_tables(S, DIFF_QK_DIM)
    o_q = IN_A
    o_k = o_q + IN_Q
    o_v = o_k + IN_K
    o_c = o_v + IN_V
    o_d = o_c + IN_C
    for l in range(DEPTH):
        h = rmsnorm(x, norm1_g[l])
        proj = h @ w_in[l]
        ya = pool_mixer(proj[..., :o_q], pool_w[l], pool_scale[l])
        yb = diff_attention(proj[..., o_q:o_k], proj[..., o_k:o_v], proj[..., o_v:o_c],
                            attn_qn_g[l], attn_kn_g[l], lam_q1[l], lam_k1[l], lam_q2[l], lam_k2[l],
                            attn_subln_g[l], l, cos, sin)
        yc = conv_module(proj[..., o_c:o_d], conv_w[l], conv_b[l], conv_ln_g[l], conv_ln_b[l])
        yd = spatial_gating(proj[..., o_d:], sgu_ln_g[l], sgu_ln_b[l], sgu_w[l], sgu_b[l])
        br = jnp.stack([ya, yb, yc, yd], axis=2)
        br = jnp.einsum('bsic,icd->bsid', br, w_branch[l])
        gates = jax.nn.sigmoid(h @ w_gate[l] + b_gate[l]).reshape(B, S, N_BRANCH, D)
        merged = jnp.sum(gates * br, axis=2)
        x = x + merged @ w_out[l]
        h2 = rmsnorm(x, norm2_g[l])
        if l % 2 == 0:
            i = l // 2
            x = x + swiglu(h2, ffn_w1[i], ffn_w3[i], ffn_w2[i])
        else:
            i = l // 2
            x = x + moe_ffn(h2, moe_router[i], moe_w1[i], moe_w3[i], moe_w2[i])
    return x


_drawn_inputs = setup_inputs


def setup_inputs(seed=0):
    import zlib

    import numpy as np

    out = dict(_drawn_inputs(seed))
    spreads = {}
    factors = {'attn_qn_g': 8.359,
     'sgu_ln_g': 30.813,
     'b_gate': 3.066,
     'pool_scale': 14.71,
     'attn_subln_g': 16.175,
     'conv_b': 2.69,
     'conv_ln_g': 16.946,
     'conv_ln_b': 17.679,
     'sgu_ln_b': 28.641,
     'sgu_b': 19.848,
     'attn_kn_g': 2.875,
     'lam_k2': 3.811,
     'norm2_g': 4.969}
    for name, (base, spread) in spreads.items():
        noise = np.random.default_rng([zlib.crc32(name.encode()), seed]).standard_normal(out[name].shape)
        drawn = base * np.exp(spread * noise) if base else spread * noise
        out[name] = __import__('jax').numpy.asarray(drawn.astype(out[name].dtype))
    for name, factor in factors.items():
        out[name] = (out[name] * factor).astype(out[name].dtype)
    return out
```

```python
import math
from contextlib import ExitStack

import numpy as np
import concourse.bass as bass
from concourse import mybir

F32 = mybir.dt.float32
I32 = mybir.dt.int32
ALU = mybir.AluOpType
ACT = mybir.ActivationFunctionType
AX = mybir.AxisListType.X

P = 128
D = 1024
T = 256
TT = T // P
KT = D // P
L = 2
BR = D // 4
CT = BR // P
HEADS = 4
QK = 32
MAPS = 2 * HEADS
VD = 64
TAPS = 31
PAD = TAPS - 1
PPAD = 16
NGATE = 4
FF = 2816
FE = 3584
E = 8
US = 256
S_DENSE = FF // US
S_MOE = FE // US
SLOTS = 7
EPS = 1e-6
MASKED = -1e30
SCALE = QK ** -0.5

IN_COL = {"pa": 0, "q": 256, "k": 512, "v": 768, "ca": 1024, "cg": 1280, "du": 1536, "dv": 1792}
IN_ORDER = ["q", "k", "v", "cg", "ca", "dv", "du", "pa"]
TOK_PARTS = ("q", "k", "v", "dv")
BR_ORDER = [0, 3, 2, 1]

PC_N1, PC_N2, PC_BG, PC_PS, PC_CB, PC_CG, PC_CBB, PC_CW = 0, 8, 16, 48, 50, 52, 54, 56
PC = PC_CW + 2 * TAPS

C_ID, C_TRI, C_COS, C_SIN, C_INV, C_IOTA = 0, 128, 256, 288, 320, 832
C_N = C_IOTA + 128


def shape_constants():
    c = np.zeros((P, C_N), np.float32)
    c[:, C_ID:C_ID + P] = np.eye(P, dtype=np.float32)
    c[:, C_TRI:C_TRI + P] = np.triu(np.ones((P, P), np.float32), 1)
    pos = np.arange(T, dtype=np.float32)
    inv = (1.0 / (np.float32(10000.0) ** (np.arange(0, QK, 2, dtype=np.float32) / np.float32(QK)))).astype(np.float32)
    ang = (pos[:, None] * inv[None, :]).astype(np.float32)
    for t in range(TT):
        c[:, C_COS + 16 * t:C_COS + 16 * t + 16] = np.cos(ang[P * t:P * t + P])
        c[:, C_SIN + 16 * t:C_SIN + 16 * t + 16] = np.sin(ang[P * t:P * t + P])
    for g, w in enumerate((2, 4, 8, 16)):
        row = 1.0 / np.minimum(np.arange(T) + 1, w).astype(np.float32)
        c[64 * (g % 2):64 * (g % 2) + 64, C_INV + T * (g // 2):C_INV + T * (g // 2) + T] = row
    c[:, C_IOTA:C_IOTA + P] = np.arange(P)
    return c


class Plan:

    def __init__(self):
        self.jobs, self.uses = {}, [0] * 8
        self.units, self.index = [], {}
        self.acc_units = 0

    def job(self, key, bank, stride=0):
        self.jobs[key] = (bank, self.uses[bank], stride)
        self.uses[bank] += 1

    def unit(self, key, freed):
        self.index[key] = len(self.units)
        self.units.append((key, freed))

    def acc(self, stride=0):
        self.acc_units += 1
        return ("acc", self.acc_units, stride)


def make_plan():
    p = Plan()
    for l in range(L):
        p.job(("par", l), 1 + l)
    p.job(("wsT", 0), 0)
    p.job(("wsT", 1), 3)

    def ffn(key, steps, se=0, sh=0, sy=0):
        for b in range(4):
            p.job(("y", key, b), b, sy)
        for s in range(steps + 1):
            if s < steps:
                for j, w in enumerate(("h1", "h3")):
                    p.job((w, key, s), 4 + 2 * (s % 2) + j, sh)
                    p.unit((w, key, s), ("ready", (w, key, s)))
            if s >= 1:
                p.unit(("w2", key, s - 1), ("ready", ("y", key, 3)) if s == steps else p.acc(se))

    for l in range(L):
        for j in range(4):
            p.job(("n1", l, j), 4 + j)
        for i, w in enumerate(IN_ORDER):
            p.job((w, l), 4 + i % 4)
            p.unit(("in", l, w), ("ready", (w, l)))
        p.job(("qT", l), 0)
        p.job(("kT", l), 1)
        for g in range(16):
            p.job(("g", l, g), 4 + g % 4)
            p.unit(("gate", l, g), ("ready", ("g", l, g)))
        for qb in (1, 0):
            for b in range(4):
                p.job(("s", l, qb, b), b)
        p.job(("pool", l), 0)
        p.job(("sv", l), 1)
        p.job(("mean", l), 2)
        p.job(("var", l), 3)
        for b in range(3):
            p.job(("aT", l, b), b)
        p.job(("o", l), 3)
        p.job(("ybT", l), 0)
        for i in BR_ORDER:
            for q in range(4):
                p.job(("br", l, i, q), 4 + q)
            p.unit(("branch", l, i), ("ready", ("br", l, i, 3)))
        for b in range(4):
            p.job(("y", ("out", l), b), b)
        for u in range(4):
            p.unit(("out", l, u), ("ready", ("y", ("out", l), 3)) if u == 3 else p.acc())
        for j in range(4):
            p.job(("n2", l, j), 4 + j)
        if l == 0:
            ffn("dense", S_DENSE)
    p.job("logits", 0)
    p.moe_base = len(p.units)
    ffn("moe", S_MOE, se=S_MOE - 1, sh=S_MOE // 2, sy=1)
    p.moe_units = len(p.units) - p.moe_base
    assert p.moe_units % SLOTS == 0
    return p


def trunk_kernel(nc, x, norm1_g, w_in, w_gate, b_gate, w_branch, w_out, pool_w, pool_scale,
                 attn_qn_g, attn_kn_g, lam_q1, lam_k1, lam_q2, lam_k2, attn_subln_g,
                 conv_w, conv_b, conv_ln_g, conv_ln_b, sgu_ln_g, sgu_ln_b, sgu_w, sgu_b,
                 norm2_g, ffn_w1, ffn_w3, ffn_w2, moe_router, moe_w1, moe_w3, moe_w2, table, out):
    plan = make_plan()
    lam_init = [0.8 - 0.6 * math.exp(-0.3 * l) for l in range(L)]

    with ExitStack() as ctx:
        def sb(name, shape, dt=F32):
            return ctx.enter_context(nc.sbuf_tensor(name, shape, dt))

        def sem(name):
            return ctx.enter_context(nc.semaphore(name))

        bank = [ctx.enter_context(nc.psum_tensor(f"bank{b}", [P, 512], F32)) for b in range(8)]

        ring = sb("ring", [P, SLOTS, 2048])
        x_tok = sb("x_tok", [P, TT, D])
        shared8k = sb("shared8k", [P, 2048])
        xn = shared8k[:, :].rearrange("p (t d) -> p t d", t=TT)
        sc1 = shared8k[:, :].rearrange("p (m k) -> p m k", m=MAPS)
        merged = shared8k[:, :].rearrange("p (k t) -> p k t", k=KT)
        hT = sb("hT", [P, KT, T])
        gates = sb("gates", [P, 4 * KT, T])
        junk = sb("junk", [P, D])
        eps = sb("eps", [P, 1])
        ssq = sb("ssq", [P, TT])
        rms = sb("rms", [P, TT])
        rstd = sb("rstd", [P, TT])
        const = sb("const", [P, C_N])
        par_rows = sb("par_rows", [PC, L, P])
        par = sb("par", [P, L, PC])
        router = sb("router", [P, KT, E])
        ident = const[:, C_ID:C_ID + P]
        tri = const[:, C_TRI:C_TRI + P]
        cos = const[:, C_COS:C_COS + 32].rearrange("p (t d) -> p t d", t=TT)
        sin = const[:, C_SIN:C_SIN + 32].rearrange("p (t d) -> p t d", t=TT)
        invcnt = const[:, C_INV:C_INV + 512].rearrange("p (c t) -> p c t", c=CT)

        qkg = sb("qkg", [P, L, 2, QK])
        lamv = sb("lamv", [P, L, 2, 2, QK])
        lamp = sb("lamp", [P, 2, QK])
        lams = sb("lams", [P, 2])
        lame = sb("lame", [P, 2])
        neglam = sb("neglam", [P, L])
        subg = sb("subg", [P, L, VD])
        qk_raw = sb("qk_raw", [P, TT, 2, BR])
        qk_n = sb("qk_n", [P, TT, 2, BR])
        att8k = sb("att8k", [P, 2048])
        qk_sq = att8k[:, 0:1024].rearrange("p (m d) -> p m d", d=QK)
        rot = att8k[:, 1024:2048].rearrange("p (t i c) -> p t i c", t=TT, i=2)
        aT = att8k[:, 0:12 * P].rearrange("p (n k) -> p n k", n=12)
        qk_ss = sb("qk_ss", [P, TT * 2 * MAPS])
        qk_rms = sb("qk_rms", [P, TT * 2 * MAPS])
        qk_rstd = sb("qk_rstd", [P, TT * 2 * MAPS])
        prod = sb("prod", [P, 2, 512])
        ra, rb = (prod[:, i, :].rearrange("p (t m d) -> p t m d", t=TT, m=16) for i in range(2))
        v_tok = sb("v_tok", [P, TT, BR])
        qT = sb("qT", [P, CT, T])
        kT = sb("kT", [P, CT, T])
        sc0 = sb("sc0", [P, MAPS, P])
        smax = sb("smax", [P, 2, MAPS])
        nmax = sb("nmax", [P, 2, MAPS])
        esum = sb("esum", [P, 2, MAPS])
        erec = sb("erec", [P, 2, MAPS])
        elam = sb("elam", [P, 2, MAPS])
        osq = junk[:, 0:512].rearrange("p (m d) -> p m d", d=VD)
        oss = sb("oss", [P, MAPS])
        orms = sb("orms", [P, MAPS])
        orstd = sb("orstd", [P, MAPS])
        o_n = sb("o_n", [P, MAPS, VD])

        sig = sb("sig", [P, CT, T])
        u_pad = sb("u_pad", [P, CT, PAD + T])
        cy = sb("cy", [P, CT, T])
        csq = junk[:, 512:1024].rearrange("p (c t) -> p c t", c=CT)
        crms = sb("crms", [P, T])
        mean_w = sb("mean_w", [P, P])

        ws = sb("ws", [P, L, 4, P])
        wT = sb("wT", [P, L, 4, P])
        sgub = sb("sgub", [P, L, CT, P])
        slg = sb("slg", [P, L, BR])
        slb = sb("slb", [P, L, BR])
        zu = sb("zu", [P, CT, T])
        zv = sb("zv", [P, TT, BR])
        zsum = sb("zsum", [P, TT])
        znm = sb("znm", [P, TT])
        zss = sb("zss", [P, TT])
        zrms = sb("zrms", [P, TT])
        zrstd = sb("zrstd", [P, TT])

        pool_bd = sb("pool_bd", [P, L, CT, P])
        w1s, w2s, w4s, w8s, w16s = (sb(f"w{w}s", [P, CT, PPAD + T]) for w in (1, 2, 4, 8, 16))
        pooled = sb("pooled", [P, CT, T])

        yT = [sb(f"yT{i}", [P, CT, T]) for i in range(4)]

        sil = qk_raw[:, :, :, :].rearrange("p t i c -> p t (i c)")
        act = qk_n[:, :, :, :].rearrange("p t i c -> p t (i c)")

        lg = sb("lg", [P, TT, E])
        top1 = sb("top1", [P, TT])
        top2 = sb("top2", [P, TT])
        eq = sb("eq", [P, TT, E])
        rank = sb("rank", [P, TT, E])
        best = sb("best", [P, TT])
        hot1 = sb("hot1", [P, TT, E])
        hot2 = sb("hot2", [P, TT, E])
        lg2 = sb("lg2", [P, TT, E])
        diff = sb("diff", [P, TT])
        ed = sb("ed", [P, TT])
        den = sb("den", [P, TT])
        wt1 = sb("wt1", [P, TT])
        wt2 = sb("wt2", [P, TT])
        gate = sb("gate", [P, TT, E])

        loaded = [sem(f"slot{i}_loaded") for i in range(SLOTS)]
        ready = [sem(f"bank{b}_ready") for b in range(8)]
        drained = [sem(f"bank{b}_drained") for b in range(8)]
        acc_unit_used = sem("acc_unit_used")
        x_loaded = sem("x_loaded")
        const_loaded = sem("const_loaded")
        rows_loaded = sem("rows_loaded")
        bcast_loaded = sem("bcast_loaded")
        ws_loaded = sem("ws_loaded")
        bd_loaded = sem("bd_loaded")
        pool_step = sem("pool_step")
        dve_step = sem("dve_step")
        act_step = sem("act_step")
        pads_zero = sem("pads_zero")
        eps_set = sem("eps_set")
        bd_zero = sem("bd_zero")
        ws_lower = sem("ws_lower")
        x_updated = sem("x_updated")
        rms_ready = sem("rms_ready")
        xn_ready = sem("xn_ready")
        qk_squared = sem("qk_squared")
        qk_summed = sem("qk_summed")
        qk_rooted = sem("qk_rooted")
        rot_ready = sem("rot_ready")
        z_shifted = sem("z_shifted")
        z_rooted = sem("z_rooted")
        z_normed = sem("z_normed")
        zu_ready = sem("zu_ready")
        lam_summed = sem("lam_summed")
        lam_exped = sem("lam_exped")
        nmax_ready = sem("nmax_ready")
        exp_ready = sem("exp_ready")
        a_ready = sem("a_ready")
        o_squared = sem("o_squared")
        o_summed = sem("o_summed")
        o_rooted = sem("o_rooted")
        o_normed = sem("o_normed")
        conv_ready = sem("conv_ready")
        c_shifted = sem("c_shifted")
        c_squared = sem("c_squared")
        c_normed = sem("c_normed")
        yc_ready = sem("yc_ready")
        pooled_ready = sem("pooled_ready")
        merged_ready = sem("merged_ready")
        diff_ready = sem("diff_ready")
        ed_ready = sem("ed_ready")
        gate_ready = sem("gate_ready")
        out_stored = sem("out_stored")

        def val(base, stride, e):
            return base if e is None else base + stride * e

        def wait_free(pe, key, e=None):
            b, n, stride = plan.jobs[key]
            if n > 0:
                pe.wait_ge(drained[b], val(n, stride, e))

        def wait_ready(eng, key, e=None):
            b, n, stride = plan.jobs[key]
            eng.wait_ge(ready[b], val(n + 1, stride, e))

        def wait_drained(eng, key, e=None):
            b, n, stride = plan.jobs[key]
            eng.wait_ge(drained[b], val(n + 1, stride, e))

        def bank_of(key):
            return bank[plan.jobs[key][0]]

        def signals(ins, sems, key):
            ins.then_inc(sems[plan.jobs[key][0]], 1)

        def wait_unit(pe, key, e=None):
            n = plan.index[key]
            per = plan.moe_units // SLOTS
            pe.wait_ge(loaded[n % SLOTS], val(16 * (n // SLOTS + 1), 16 * per, e))
            return ring[:, n % SLOTS, :]

        def drams(key, e=None):
            kind = key[0]
            if kind == "in":
                _, l, w = key
                return w_in[l].rearrange("(k p) c -> p k c", p=P)[:, :, IN_COL[w]:IN_COL[w] + US]
            if kind == "gate":
                _, l, g = key
                return w_gate[l].rearrange("(k p) c -> p k c", p=P)[:, :, US * g:US * g + US]
            if kind == "branch":
                _, l, i = key
                return w_branch[l, i].rearrange("(k p) d -> p k d", p=P)
            if kind == "out":
                _, l, u = key
                return w_out[l, US * u:US * u + US, :].rearrange("(k p) d -> p k d", p=P)
            _, which, s = key
            w = {"dense": {"h1": ffn_w1, "h3": ffn_w3, "w2": ffn_w2},
                 "moe": {"h1": moe_w1, "h3": moe_w3, "w2": moe_w2}}[which][kind]
            if which == "dense":
                w = w[0:1]
            else:
                w = w[0, bass.ds(e, 1)]
            if kind == "w2":
                return w[:, US * s:US * s + US, :].rearrange("e (k p) d -> p (e k) d", p=P)
            return w[:, :, US * s:US * s + US].rearrange("e (k p) f -> p (e k) f", p=P)

        BCASTS = 1 + L * (2 + 4 + 1 + 2 + 4)

        block = ctx.enter_context(nc.Block())

        @block.sync
        def _(sp):
            def wait_slot(n, e=None):
                _, freed = plan.units[n]
                if freed[0] == "ready":
                    wait_ready(sp, freed[1], e)
                else:
                    sp.wait_ge(acc_unit_used, val(freed[1], freed[2], e))

            def load(n, e=None):
                key, _ = plan.units[n]
                src = drams(key, e)
                dst = ring[:, n % SLOTS, :].rearrange("p (k c) -> p k c", k=src.shape[1])
                sp.dma_start(dst, src).then_inc(loaded[n % SLOTS], 16)

            for t in range(TT):
                sp.dma_start(x_tok[:, t, :], x[0, P * t:P * t + P, :]).then_inc(x_loaded, 16)
            for n in range(plan.moe_base):
                if n >= SLOTS:
                    wait_slot(n - SLOTS)
                load(n)
            base, per = plan.moe_base, plan.moe_units
            for i in range(per):
                wait_slot(base + i - SLOTS, None if i < SLOTS else 0)
                load(base + i, 0)
            with sp.Fori(1, E) as e:
                for i in range(per):
                    if i < SLOTS:
                        wait_slot(base + per + i - SLOTS, e - 1)
                    else:
                        wait_slot(base + i - SLOTS, e)
                    load(base + i, e)
            sp.wait_ge(x_updated, TT * (L + 1 + E))
            for t in range(TT):
                sp.dma_start(out[0, P * t:P * t + P, :], x_tok[:, t, :]).then_inc(out_stored, 16)
            sp.wait_ge(out_stored, 16 * TT)

        @block.gpsimd
        def _(pool):
            steps = [0]

            def step(ins):
                steps[0] += 1
                ins.then_inc(pool_step, 1)
                pool.wait_ge(pool_step, steps[0])

            pool.memset(u_pad[:, :, 0:PAD], 0.0)
            for w in (w1s, w2s, w4s, w8s):
                pool.memset(w[:, :, 0:PPAD], 0.0)
            pool.memset(mean_w[:, :], 1.0 / BR).then_inc(pads_zero, 1)
            pool.memset(pool_bd[:, :, :, :], 0.0).then_inc(bd_zero, 1)
            pool.wait_ge(pads_zero, 1)
            pool.wait_ge(ws_loaded, 16 * L)
            for l in range(L):
                pool.affine_select(out=ws[:, l, :, :], in_=ws[:, l, :, :], compare_op=ALU.is_ge, fill=0.0, base=0,
                                   pattern=[[0, 4], [-1, P]], channel_multiplier=1).then_inc(ws_lower, 1)
            pool.wait_ge(const_loaded, 16)
            now = slice(PPAD, PPAD + T)
            for l in range(L):
                wait_drained(pool, ("pa", l))
                for a, b, back in ((w1s, w2s, 1), (w2s, w4s, 2), (w4s, w8s, 4), (w8s, w16s, 8)):
                    step(pool.tensor_tensor(b[:, :, now], a[:, :, now], a[:, :, PPAD - back:PPAD - back + T], ALU.add))
                for g, w in enumerate((w2s, w4s, w8s, w16s)):
                    rows = slice(64 * (g % 2), 64 * (g % 2) + 64)
                    last = pool.tensor_tensor(pooled[rows, g // 2, :], w[rows, g // 2, now], invcnt[rows, g // 2, :], ALU.mult)
                step(last)
                pool.tensor_tensor(pooled[:, :, :], pooled[:, :, :], w1s[:, :, now], ALU.subtract).then_inc(pooled_ready, 1)

        @block.tensor
        def _(pe):
            def transposes(key, pairs):
                wait_free(pe, key)
                for o, i in pairs:
                    n = i.shape[0]
                    last = pe.transpose(o, i, ident[0:n, 0:n])
                signals(last, ready, key)

            def norm_transposes(l, which):
                for t in range(TT):
                    pe.wait_ge(xn_ready, TT * (2 * l + (which == "n2")) + t + 1)
                    for j in range(4):
                        if t == 0:
                            wait_free(pe, (which, l, j))
                        for k in (2 * j, 2 * j + 1):
                            last = pe.transpose(bank_of((which, l, j))[:, T * (k % 2) + P * t:T * (k % 2) + P * t + P],
                                                xn[:, t, P * k:P * k + P], ident)
                        if t == TT - 1:
                            signals(last, ready, (which, l, j))

            def feat_unit(key, ukey, k_guard=None, e=None):
                w = wait_unit(pe, ukey, e).rearrange("p (k c) -> p k c", k=KT)
                wait_free(pe, key, e)
                for c in range(2):
                    for k in range(KT):
                        if k_guard and c == 0 and k % 2 == 0:
                            wait_drained(pe, (*k_guard, k // 2))
                        last = pe.matmul(bank_of(key)[:, T * c:T * c + T], w[:, k, P * c:P * c + P], hT[:, k, :],
                                         start=(k == 0), stop=(k == KT - 1))
                signals(last, ready, key)

            def tok_unit(key, ukey, k_guard=None):
                w = wait_unit(pe, ukey).rearrange("p (k c) -> p k c", k=KT)
                wait_free(pe, key)
                for t in range(TT):
                    for k in range(KT):
                        if k_guard and t == 0 and k % 2 == 0:
                            wait_drained(pe, (*k_guard, k // 2))
                        last = pe.matmul(bank_of(key)[:, T * t:T * t + US], hT[:, k, P * t:P * t + P], w[:, k, :],
                                         start=(k == 0), stop=(k == KT - 1))
                signals(last, ready, key)

            def acc_unit(ukey, ykey, lhs, first, final, e=None):
                w = wait_unit(pe, ukey, e).rearrange("p (k d) -> p k d", k=2)
                for t in range(TT):
                    for n in range(2):
                        b = 2 * t + n
                        if first:
                            wait_free(pe, ("y", ykey, b), e)
                        for k in range(2):
                            last = pe.matmul(bank[b][:, :], lhs(k, t), w[:, k, 512 * n:512 * n + 512],
                                             start=(first and k == 0), stop=(final and k == 1))
                        if final:
                            signals(last, ready, ("y", ykey, b))
                if not final:
                    last.then_inc(acc_unit_used, 1)

            def ffn(key, steps, e=None, k_guard=None):
                for s in range(steps + 1):
                    if s < steps:
                        feat_unit(("h1", key, s), ("h1", key, s), k_guard if s == 0 else None, e)
                        feat_unit(("h3", key, s), ("h3", key, s), None, e)
                    if s >= 1:
                        wait_drained(pe, ("h3", key, s - 1), e)
                        acc_unit(("w2", key, s - 1), key,
                                 lambda k, t: act[:, (s - 1) % 2, T * k + P * t:T * k + P * t + P],
                                 s == 1, s == steps, e)

            def scores(l, qb):
                for b in range(4):
                    wait_free(pe, ("s", l, qb, b))
                keys = P * (qb + 1)
                for c in range(CT):
                    for b in range(4):
                        rows = slice(QK * b, QK * b + QK)
                        last = pe.matmul(bank[b][:, T * c:T * c + keys], qT[rows, c, P * qb:P * qb + P],
                                         kT[rows, c, 0:keys], start=True, stop=True)
                        if c == CT - 1:
                            signals(last, ready, ("s", l, qb, b))

            def hooks(l, g):
                if g == -1:
                    pe.wait_ge(rot_ready, l + 1)
                    for i, dst in enumerate(("qT", "kT")):
                        transposes((dst, l), [(bank_of((dst, l))[:, T * c + P * t:T * c + P * t + P],
                                               rot[:, t, i, P * c:P * c + P]) for c in range(CT) for t in range(TT)])
                if g == 0:
                    wait_drained(pe, ("qT", l))
                    wait_drained(pe, ("kT", l))
                    scores(l, 1)
                if g == 1:
                    scores(l, 0)
                if g == 3:
                    pe.wait_ge(pooled_ready, l + 1)
                    pe.wait_ge(bd_loaded, 16 * 4 * L)
                    wait_free(pe, ("pool", l))
                    for c in range(CT):
                        last = pe.matmul(bank_of(("pool", l))[:, T * c:T * c + T], pool_bd[:, l, c, :], pooled[:, c, :],
                                         start=True, stop=True)
                    signals(last, ready, ("pool", l))
                if g == 4:
                    pe.wait_ge(z_normed, l + 1)
                    wait_drained(pe, ("wsT", l))
                    wait_free(pe, ("sv", l))
                    for c in range(CT):
                        for n in range(TT):
                            for half in range(2):
                                grp = 2 * c + half
                                last = pe.matmul(bank_of(("sv", l))[64 * half:64 * half + 64, T * c + P * n:T * c + P * n + P],
                                                 zv[:, n, 64 * grp:64 * grp + 64], wT[:, l, grp, :],
                                                 start=True, stop=True, skip_group_check=True)
                    signals(last, ready, ("sv", l))
                if g == 8:
                    pe.wait_ge(conv_ready, l + 1)
                    pe.wait_ge(pads_zero, 1)
                    wait_free(pe, ("mean", l))
                    for c in range(CT):
                        last = pe.matmul(bank_of(("mean", l))[:, 0:T], mean_w[:, :], cy[:, c, :], start=(c == 0), stop=(c == CT - 1))
                    signals(last, ready, ("mean", l))
                if g == 9:
                    pe.wait_ge(c_squared, l + 1)
                    wait_free(pe, ("var", l))
                    for c in range(CT):
                        last = pe.matmul(bank_of(("var", l))[:, 0:T], mean_w[:, :], csq[:, c, :], start=(c == 0), stop=(c == CT - 1))
                    signals(last, ready, ("var", l))
                if g == 10:
                    pe.wait_ge(a_ready, l + 1)
                    for b in range(2):
                        transposes(("aT", l, b), [(bank[b][:, P * (2 * h + kb):P * (2 * h + kb) + P],
                                                   sc1[:, 2 * (2 * b + h), P * kb:P * kb + P]) for h in range(2) for kb in range(2)])
                    transposes(("aT", l, 2), [(bank[2][:, P * h:P * h + P], sc0[:, 2 * h, :]) for h in range(HEADS)])
                if g == 11:
                    for b in range(3):
                        wait_drained(pe, ("aT", l, b))
                    wait_free(pe, ("o", l))
                    for qb in range(2):
                        for h in range(HEADS):
                            for kb in range(qb + 1):
                                a = aT[:, 2 * h + kb if qb else 8 + h, :]
                                last = pe.matmul(bank_of(("o", l))[:, VD * (4 * qb + h):VD * (4 * qb + h) + VD], a,
                                                 v_tok[:, kb, VD * h:VD * h + VD], start=(kb == 0), stop=(kb == qb))
                    signals(last, ready, ("o", l))
                if g == 14:
                    pe.wait_ge(o_normed, l + 1)
                    flat = o_n[:, :, :].rearrange("p m d -> p (m d)")
                    transposes(("ybT", l), [(bank_of(("ybT", l))[:, T * c + P * t:T * c + P * t + P],
                                             flat[:, BR * t + P * c:BR * t + P * c + P]) for c in range(CT) for t in range(TT)])

            def branch(l, i):
                if i == 0:
                    wait_drained(pe, ("pool", l))
                elif i == 1:
                    wait_drained(pe, ("ybT", l))
                elif i == 2:
                    pe.wait_ge(yc_ready, l + 1)
                else:
                    wait_drained(pe, ("sv", l))
                w = wait_unit(pe, ("branch", l, i)).rearrange("p (k d) -> p k d", k=CT)
                for q in range(4):
                    key = ("br", l, i, q)
                    wait_free(pe, key)
                    for half in range(2):
                        d = 2 * q + half
                        for c in range(CT):
                            last = pe.matmul(bank_of(key)[:, T * half:T * half + T], w[:, c, P * d:P * d + P], yT[i][:, c, :],
                                             start=(c == 0), stop=(c == CT - 1))
                    signals(last, ready, key)

            pe.wait_ge(const_loaded, 16)
            pe.wait_ge(rows_loaded, 16 * 8 * L)
            for l in range(L):
                transposes(("par", l), [(bank_of(("par", l))[:, 0:PC], par_rows[:, l, :])])
            for l in range(L):
                norm_transposes(l, "n1")
                for i, w in enumerate(IN_ORDER):
                    (tok_unit if w in TOK_PARTS else feat_unit)((w, l), ("in", l, w), ("n1", l) if i == 0 else None)
                    if l == 0 and i == 0:
                        pe.wait_ge(ws_lower, L)
                        for j in range(L):
                            transposes(("wsT", j), [(bank_of(("wsT", j))[:, P * g:P * g + P], ws[:, j, g, :]) for g in range(4)])
                hooks(l, -1)
                for g in range(16):
                    feat_unit(("g", l, g), ("gate", l, g))
                    hooks(l, g)
                for i in BR_ORDER:
                    branch(l, i)
                for u in range(4):
                    pe.wait_ge(merged_ready, 4 * l + u + 1)
                    acc_unit(("out", l, u), ("out", l), lambda k, t: merged[:, 2 * u + k, P * t:P * t + P], u == 0, u == 3)
                norm_transposes(l, "n2")
                if l == 0:
                    ffn("dense", S_DENSE, k_guard=("n2", 0))
            for j in range(4):
                wait_drained(pe, ("n2", 1, j))
            pe.wait_ge(bcast_loaded, 16 * BCASTS)
            wait_free(pe, "logits")
            for t in range(TT):
                for k in range(KT):
                    last = pe.matmul(bank_of("logits")[:, E * t:E * t + E], hT[:, k, P * t:P * t + P], router[:, k, :],
                                     start=(k == 0), stop=(k == KT - 1))
            signals(last, ready, "logits")
            with pe.Fori(0, E) as e:
                ffn("moe", S_MOE, e)

        @block.scalar
        def _(act_e):
            steps = [0]

            def step(ins):
                steps[0] += 1
                ins.then_inc(act_step, 1)
                act_e.wait_ge(act_step, steps[0])

            fn = act_e.activation
            act_e.dma_start(const[:, :], table).then_inc(const_loaded, 16)
            for l in range(L):
                for c0, n, src in ((PC_N1, 8, norm1_g[l].rearrange("(k p) -> k p", p=P)),
                                   (PC_N2, 8, norm2_g[l].rearrange("(k p) -> k p", p=P)),
                                   (PC_BG, 32, b_gate[l].rearrange("(k p) -> k p", p=P)),
                                   (PC_PS, 2, pool_scale[l].rearrange("(k p) -> k p", p=P)),
                                   (PC_CB, 2, conv_b[l].rearrange("(k p) -> k p", p=P)),
                                   (PC_CG, 2, conv_ln_g[l].rearrange("(k p) -> k p", p=P)),
                                   (PC_CBB, 2, conv_ln_b[l].rearrange("(k p) -> k p", p=P)),
                                   (PC_CW, 2 * TAPS, conv_w[l].rearrange("t (h p) -> (t h) p", p=P))):
                    act_e.dma_start(par_rows[c0:c0 + n, l, :], src).then_inc(rows_loaded, 16)
            for l in range(L):
                act_e.dma_start(ws[:, l, :, :], sgu_w[l].rearrange("g t s -> t g s")).then_inc(ws_loaded, 16)

            act_e.dma_start(router[:, :, :], moe_router[0].rearrange("(k p) e -> p k e", p=P)).then_inc(bcast_loaded, 16)
            for l in range(L):
                for dst, src in ((qkg[:, l, 0, :], attn_qn_g[l]), (qkg[:, l, 1, :], attn_kn_g[l]),
                                 (lamv[:, l, 0, 0, :], lam_q1[l]), (lamv[:, l, 0, 1, :], lam_k1[l]),
                                 (lamv[:, l, 1, 0, :], lam_q2[l]), (lamv[:, l, 1, 1, :], lam_k2[l]),
                                 (subg[:, l, :], attn_subln_g[l]), (slg[:, l, :], sgu_ln_g[l]), (slb[:, l, :], sgu_ln_b[l])):
                    act_e.dma_start(dst, src.partition_broadcast(P)).then_inc(bcast_loaded, 16)
                for g in range(4):
                    h = 64 * (g % 2)
                    act_e.dma_start(sgub[h:h + 64, l, g // 2, :], sgu_b[l, g].partition_broadcast(64)).then_inc(bcast_loaded, 16)
            act_e.wait_ge(bd_zero, 1)
            for l in range(L):
                for g in range(4):
                    h = 64 * (g % 2)
                    act_e.dma_start(pool_bd[h:h + 64, l, g // 2, h:h + 64], pool_w[l, g]).then_inc(bd_loaded, 16)

            def copy_out(key, dst, func=ACT.Identity, **kw):
                wait_ready(act_e, key)
                signals(fn(dst, bank_of(key)[:, 0:dst.free_size()] if len(dst.shape) == 2 else
                           bank_of(key)[:, 0:dst.shape[1] * dst.shape[2]].rearrange("p (a b) -> p a b", a=dst.shape[1]),
                           func, **kw), drained, key)

            def norm(l, which):
                n = 2 * l + (which == "n2")
                for t in range(TT):
                    if n == 0:
                        act_e.wait_ge(x_loaded, 16 * TT)
                    else:
                        act_e.wait_ge(x_updated, TT * (n - 1) + t + 1)
                    step(fn(junk[:, :], x_tok[:, t, :], ACT.Square, accum_out=ssq[:, t:t + 1]))
                    fn(rms[:, t:t + 1], ssq[:, t:t + 1], ACT.Sqrt, scale=1.0 / D, bias=eps[:, :]).then_inc(rms_ready, 1)
                for j in (0, 2):
                    norm_out(act_e, l, which, j)

            def norm_out(eng, l, which, j):
                wait_ready(eng, (which, l, j))
                for k in (2 * j, 2 * j + 1):
                    c = (PC_N1 if which == "n1" else PC_N2) + k
                    last = fn(hT[:, k, :], bank_of((which, l, j))[:, T * (k % 2):T * (k % 2) + T], ACT.Copy,
                              scale=par[:, l, c:c + 1])
                signals(last, drained, (which, l, j))

            def hooks(l, g):
                if g == -1:
                    act_e.wait_ge(z_shifted, l + 1)
                    for t in range(TT):
                        last = fn(junk[:, BR * t:BR * t + BR], zv[:, t, :], ACT.Square, accum_out=zss[:, t:t + 1])
                    step(last)
                    fn(zrms[:, :], zss[:, :], ACT.Sqrt, scale=1.0 / BR, bias=eps[:, :]).then_inc(z_rooted, 1)
                    act_e.wait_ge(lam_summed, l + 1)
                    fn(lame[:, :], lams[:, :], ACT.Exp).then_inc(lam_exped, 1)
                    copy_out(("qT", l), qT[:, :, :])
                if g == 0:
                    for b in range(4):
                        copy_out(("s", l, 1, b), sc1[:, b::4, :])
                if g == 1:
                    for b in range(4):
                        wait_ready(act_e, ("s", l, 0, b))
                        signals(fn(sc0[:, b::4, :], bank[b][:, :].rearrange("p (c k) -> p c k", c=CT)[:, :, 0:P], ACT.Identity),
                                drained, ("s", l, 0, b))
                if g in (2, 3):
                    qb = 3 - g
                    sc = sc1 if qb else sc0
                    act_e.wait_ge(nmax_ready, 2 * l + g - 1)
                    for m in range(MAPS):
                        last = fn(sc[:, m, :], sc[:, m, :], ACT.Exp, scale=SCALE, bias=nmax[:, qb, m:m + 1],
                                  accum_out=esum[:, qb, m:m + 1])
                    last.then_inc(exp_ready, 1)
                if g == 3:
                    wait_ready(act_e, ("pool", l))
                    for c in range(CT):
                        last = fn(yT[0][:, c, :], bank_of(("pool", l))[:, T * c:T * c + T], ACT.Copy,
                                  scale=par[:, l, PC_PS + c:PC_PS + c + 1])
                    signals(last, drained, ("pool", l))
                if g == 9 - 1:
                    act_e.wait_ge(c_shifted, l + 1)
                    fn(csq[:, :, :], cy[:, :, :], ACT.Square).then_inc(c_squared, 1)
                if g == 9:
                    wait_ready(act_e, ("var", l))
                    signals(fn(crms[:, :], bank_of(("var", l))[:, 0:T], ACT.Sqrt, bias=eps[:, :]), drained, ("var", l))
                if g == 10:
                    for b in (0, 2):
                        copy_out(("aT", l, b), aT[:, 4 * b:4 * b + 4, :])
                    act_e.wait_ge(c_normed, l + 1)
                    for c in range(CT):
                        last = fn(yT[2][:, c, :], cy[:, c, :], ACT.Silu, scale=par[:, l, PC_CG + c:PC_CG + c + 1],
                                  bias=par[:, l, PC_CBB + c:PC_CBB + c + 1])
                    last.then_inc(yc_ready, 1)
                if g == 11:
                    wait_ready(act_e, ("o", l))
                    fn(osq[:, :, :], bank_of(("o", l))[:, :].rearrange("p (m d) -> p m d", m=MAPS), ACT.Square).then_inc(o_squared, 1)
                    act_e.wait_ge(o_summed, l + 1)
                    fn(orms[:, :], oss[:, :], ACT.Sqrt, scale=1.0 / VD, bias=eps[:, :]).then_inc(o_rooted, 1)
                if g == 14:
                    copy_out(("ybT", l), yT[1][:, :, :])

            def ffn(key, nsteps, e=None):
                for s in range(nsteps):
                    wait_ready(act_e, ("h1", key, s), e)
                    if s >= 2:
                        wait_drained(act_e, ("h3", key, s - 2), e)
                    signals(fn(sil[:, s % 2, :], bank_of(("h1", key, s))[:, :], ACT.Silu), drained, ("h1", key, s))

            act_e.wait_ge(eps_set, 1)
            for l in range(L):
                copy_out(("par", l), par[:, l, :], ACT.Identity)
            for l in range(L):
                wait_drained(act_e, ("par", l))
            for l in range(L):
                norm(l, "n1")
                for w in IN_ORDER:
                    key = (w, l)
                    if w in ("q", "k"):
                        copy_out(key, qk_raw[:, :, int(w == "k"), :])
                        if w == "k":
                            wait_drained(act_e, key)
                            wait_drained(act_e, ("q", l))
                            fn(qk_sq[:, :, :].rearrange("p m d -> p (m d)"), qk_raw[:, :, :, :].rearrange("p t i c -> p (t i c)"),
                               ACT.Square).then_inc(qk_squared, 1)
                    elif w == "v":
                        copy_out(key, v_tok[:, :, :])
                        act_e.wait_ge(qk_summed, l + 1)
                        fn(qk_rms[:, :], qk_ss[:, :], ACT.Sqrt, scale=1.0 / QK, bias=eps[:, :]).then_inc(qk_rooted, 1)
                        if l == 0:
                            for j in range(L):
                                copy_out(("wsT", j), wT[:, j, :, :])
                    elif w == "cg":
                        copy_out(key, sig[:, :, :], ACT.Sigmoid)
                    elif w == "dv":
                        wait_ready(act_e, key)
                        for t in range(TT):
                            last = fn(zv[:, t, :], bank_of(key)[:, T * t:T * t + BR], ACT.Gelu, accum_out=zsum[:, t:t + 1])
                        signals(last, drained, key)
                    elif w == "du":
                        copy_out(key, zu[:, :, :], ACT.Gelu)
                    elif w == "pa":
                        copy_out(key, w1s[:, :, PPAD:PPAD + T])
                hooks(l, -1)
                for g in range(16):
                    wait_ready(act_e, ("g", l, g))
                    for c in range(2):
                        d = 2 * g + c
                        last = fn(gates[:, d, :], bank_of(("g", l, g))[:, T * c:T * c + T], ACT.Sigmoid,
                                  bias=par[:, l, PC_BG + d:PC_BG + d + 1])
                    signals(last, drained, ("g", l, g))
                    hooks(l, g)
                norm(l, "n2")
                if l == 0:
                    ffn("dense", S_DENSE)
            act_e.wait_ge(diff_ready, 1)
            fn(ed[:, :], diff[:, :], ACT.Exp).then_inc(ed_ready, 1)
            with act_e.Fori(0, E) as e:
                ffn("moe", S_MOE, e)

        @block.vector
        def _(dve):
            steps = [0]
            tt, ts, stt = dve.tensor_tensor, dve.tensor_scalar, dve.scalar_tensor_tensor

            def step(ins):
                steps[0] += 1
                ins.then_inc(dve_step, 1)
                dve.wait_ge(dve_step, steps[0])

            def norm(l, which):
                n = 2 * l + (which == "n2")
                for t in range(TT):
                    dve.wait_ge(rms_ready, TT * n + t + 1)
                    step(dve.reciprocal(rstd[:, t:t + 1], rms[:, t:t + 1]))
                    ts(xn[:, t, :], x_tok[:, t, :], rstd[:, t:t + 1], None, ALU.mult).then_inc(xn_ready, 1)
                for j in (1, 3):
                    wait_ready(dve, (which, l, j))
                    for k in (2 * j, 2 * j + 1):
                        c = (PC_N1 if which == "n1" else PC_N2) + k
                        last = ts(hT[:, k, :], bank_of((which, l, j))[:, T * (k % 2):T * (k % 2) + T], par[:, l, c:c + 1], None, ALU.mult)
                    signals(last, drained, (which, l, j))

            def add_y(key, e=None, scale=None):
                for t in range(TT):
                    for n in range(2):
                        k = ("y", key, 2 * t + n)
                        xs = x_tok[:, t, 512 * n:512 * n + 512]
                        wait_ready(dve, k, e)
                        if scale is None:
                            tt(xs, bank_of(k)[:, :], xs, ALU.add).then_inc(drained[2 * t + n], 1)
                        else:
                            stt(out=xs, in0=bank_of(k)[:, :], scalar=scale(t), in1=xs, op0=ALU.mult, op1=ALU.add)\
                                .then_inc(drained[2 * t + n], 1)
                    wait_drained(dve, ("y", key, 2 * t), e)
                    wait_drained(dve, ("y", key, 2 * t + 1), e)
                    dve.sem_inc(x_updated, 1)

            def rope(l):
                dve.wait_ge(qk_squared, l + 1)
                dve.tensor_reduce(qk_ss[:, :], qk_sq[:, :, :], AX, ALU.add).then_inc(qk_summed, 1)
                dve.wait_ge(qk_rooted, l + 1)
                step(dve.reciprocal(qk_rstd[:, :], qk_rms[:, :]))
                flat = "p t i (m d) -> p (t i m) d"
                step(tt(qk_n[:, :, :, :].rearrange(flat, d=QK), qk_raw[:, :, :, :].rearrange(flat, d=QK),
                        qk_rstd[:, :].unsqueeze(2).to_broadcast([P, TT * 2 * MAPS, QK]), ALU.mult))
                for i in range(2):
                    v = qk_n[:, :, i, :].rearrange("p t (m d) -> p t m d", d=QK)
                    last = tt(v, v, qkg[:, l, i, :].unsqueeze(1).unsqueeze(1).to_broadcast([P, TT, MAPS, QK]), ALU.mult)
                step(last)
                v = qk_n[:, :, :, :].rearrange("p t i (m d) -> p t (i m) d", d=QK)
                r = rot[:, :, :, :].rearrange("p t i (m d) -> p t (i m) d", d=QK)
                lo, hi = slice(0, 16), slice(16, 32)
                c = cos.unsqueeze(2).to_broadcast([P, TT, 16, 16])
                s = sin.unsqueeze(2).to_broadcast([P, TT, 16, 16])
                tt(ra[:, :, :, :], v[:, :, :, lo], c, ALU.mult)
                step(tt(rb[:, :, :, :], v[:, :, :, hi], s, ALU.mult))
                step(tt(r[:, :, :, lo], ra[:, :, :, :], rb[:, :, :, :], ALU.subtract))
                tt(ra[:, :, :, :], v[:, :, :, hi], c, ALU.mult)
                step(tt(rb[:, :, :, :], v[:, :, :, lo], s, ALU.mult))
                tt(r[:, :, :, hi], ra[:, :, :, :], rb[:, :, :, :], ALU.add).then_inc(rot_ready, 1)

            def lam(l):
                step(tt(lamp[:, :, :], lamv[:, l, :, 0, :], lamv[:, l, :, 1, :], ALU.mult))
                dve.tensor_reduce(lams[:, :], lamp[:, :, :], AX, ALU.add).then_inc(lam_summed, 1)

            def z_norm_shift(l):
                wait_drained(dve, ("dv", l))
                step(ts(znm[:, :], zsum[:, :], -1.0 / BR, None, ALU.mult))
                for t in range(TT):
                    last = ts(zv[:, t, :], zv[:, t, :], znm[:, t:t + 1], None, ALU.add)
                last.then_inc(z_shifted, 1)

            def z_norm_scale(l):
                dve.wait_ge(z_rooted, l + 1)
                step(dve.reciprocal(zrstd[:, :], zrms[:, :]))
                for t in range(TT):
                    last = stt(out=zv[:, t, :], in0=zv[:, t, :], scalar=zrstd[:, t:t + 1], in1=slg[:, l, :],
                               op0=ALU.mult, op1=ALU.mult)
                step(last)
                tt(zv[:, :, :], zv[:, :, :], slb[:, l, :].unsqueeze(1).to_broadcast([P, TT, BR]), ALU.add).then_inc(z_normed, 1)

            def row_max(l, qb):
                sc = sc1 if qb else sc0
                keys = P * (qb + 1)
                for b in range(4):
                    wait_drained(dve, ("s", l, qb, b))
                step(dve.memset(sc[0:64, :, keys - 64:keys], MASKED))
                step(dve.tensor_reduce(smax[:, qb, :], sc[:, :, :], AX, ALU.max))
                ts(nmax[:, qb, :], smax[:, qb, :], -SCALE, None, ALU.mult).then_inc(nmax_ready, 1)

            def conv(l):
                for k in range(TAPS):
                    for c in range(CT):
                        col = PC_CW + 2 * k + c
                        if k == 0:
                            ins = ts(cy[:, c, :], u_pad[:, c, 0:T], par[:, l, col:col + 1],
                                     par[:, l, PC_CB + c:PC_CB + c + 1], ALU.mult, ALU.add)
                        else:
                            dve.wait_ge(dve_step, steps[0] - 1)
                            ins = stt(out=cy[:, c, :], in0=u_pad[:, c, k:k + T], scalar=par[:, l, col:col + 1],
                                      in1=cy[:, c, :], op0=ALU.mult, op1=ALU.add)
                        if k == TAPS - 1 and c == CT - 1:
                            ins.then_inc(conv_ready, 1)
                        else:
                            steps[0] += 1
                            ins.then_inc(dve_step, 1)

            def combine(l):
                dve.wait_ge(exp_ready, 2 * l + 2)
                step(dve.reciprocal(erec[:, :, :], esum[:, :, :]))
                step(ts(elam[:, :, :], erec[:, :, :], neglam[:, l:l + 1], None, ALU.mult))
                for sc, qb in ((sc1, 1), (sc0, 0)):
                    for h in range(HEADS):
                        last = ts(sc[:, 2 * h + 1, :], sc[:, 2 * h + 1, :], elam[:, qb, 2 * h + 1:2 * h + 2], None, ALU.mult)
                step(last)
                for sc, qb in ((sc1, 1), (sc0, 0)):
                    for h in range(HEADS):
                        last = stt(out=sc[:, 2 * h, :], in0=sc[:, 2 * h, :], scalar=erec[:, qb, 2 * h:2 * h + 1],
                                   in1=sc[:, 2 * h + 1, :], op0=ALU.mult, op1=ALU.add)
                last.then_inc(a_ready, 1)

            def o_norm(l):
                dve.wait_ge(o_squared, l + 1)
                dve.tensor_reduce(oss[:, :], osq[:, :, :], AX, ALU.add).then_inc(o_summed, 1)
                dve.wait_ge(o_rooted, l + 1)
                step(dve.reciprocal(orstd[:, :], orms[:, :]))
                wait_ready(dve, ("o", l))
                signals(tt(o_n[:, :, :], bank_of(("o", l))[:, :].rearrange("p (m d) -> p m d", m=MAPS),
                           orstd[:, :].unsqueeze(2).to_broadcast([P, MAPS, VD]), ALU.mult), drained, ("o", l))
                wait_drained(dve, ("o", l))
                tt(o_n[:, :, :], o_n[:, :, :], subg[:, l, :].unsqueeze(1).to_broadcast([P, MAPS, VD]), ALU.mult)\
                    .then_inc(o_normed, 1)

            def ffn(key, nsteps, e=None):
                for s in range(nsteps):
                    wait_drained(dve, ("h1", key, s), e)
                    wait_ready(dve, ("h3", key, s), e)
                    if s >= 3:
                        dve.wait_ge(acc_unit_used, acc_at(key, s - 2, e))
                    elif s == 2:
                        dve.wait_ge(acc_unit_used, acc_at(key, 0, e))
                    signals(tt(act[:, s % 2, :], bank_of(("h3", key, s))[:, :], sil[:, s % 2, :], ALU.mult), drained, ("h3", key, s))

            def acc_at(key, s, e):
                freed = plan.units[plan.index[("w2", key, s)]][1]
                return val(freed[1], freed[2], e)

            dve.memset(eps[:, :], EPS).then_inc(eps_set, 1)
            dve.wait_ge(bcast_loaded, 16 * BCASTS)
            dve.wait_ge(const_loaded, 16)
            for l in range(L):
                step(ts(subg[:, l, :], subg[:, l, :], 1.0 - lam_init[l], None, ALU.mult))
            dve.wait_ge(x_loaded, 16 * TT)
            wait_drained(dve, ("par", 0))
            wait_drained(dve, ("par", 1))
            dve.wait_ge(pads_zero, 1)
            for l in range(L):
                norm(l, "n1")
                lam(l)
                rope(l)
                wait_ready(dve, ("ca", l))
                wait_drained(dve, ("cg", l))
                signals(tt(u_pad[:, :, PAD:PAD + T], bank_of(("ca", l))[:, :].rearrange("p (c t) -> p c t", c=CT), sig[:, :, :], ALU.mult),
                        drained, ("ca", l))
                z_norm_shift(l)
                z_norm_scale(l)
                dve.wait_ge(lam_exped, l + 1)
                step(stt(out=neglam[:, l:l + 1], in0=lame[:, 1:2], scalar=-lam_init[l], in1=lame[:, 0:1],
                         op0=ALU.add, op1=ALU.subtract))
                wait_ready(dve, ("kT", l))
                signals(dve.tensor_copy(kT[:, :, :], bank_of(("kT", l))[:, :].rearrange("p (c t) -> p c t", c=CT)), drained, ("kT", l))
                row_max(l, 1)
                row_max(l, 0)
                wait_drained(dve, ("ca", l))
                conv(l)
                combine(l)
                wait_ready(dve, ("sv", l))
                wait_drained(dve, ("du", l))
                step(tt(yT[3][:, :, :].rearrange("p c (n t) -> p c n t", n=TT),
                        bank_of(("sv", l))[:, :].rearrange("p (c n t) -> p c n t", c=CT, n=TT),
                        sgub[:, l, :, :].unsqueeze(2).to_broadcast([P, CT, TT, P]), ALU.add))
                signals(tt(yT[3][:, :, :], yT[3][:, :, :], zu[:, :, :], ALU.mult), drained, ("sv", l))
                wait_ready(dve, ("mean", l))
                dve.wait_ge(conv_ready, l + 1)
                mean = bank_of(("mean", l))[:, 0:T].unsqueeze(1).to_broadcast([P, CT, T])
                tt(cy[:, :, :], cy[:, :, :], mean, ALU.subtract).then_inc(c_shifted, 1)
                dve.wait_ge(c_shifted, l + 1)
                dve.sem_inc(drained[plan.jobs[("mean", l)][0]], 1)
                wait_drained(dve, ("var", l))
                step(dve.reciprocal(crms[:, :], crms[:, :]))
                tt(cy[:, :, :], cy[:, :, :], crms[:, :].unsqueeze(1).to_broadcast([P, CT, T]), ALU.mult).then_inc(c_normed, 1)
                wait_ready(dve, ("aT", l, 1))
                signals(dve.tensor_copy(aT[:, 4:8, :], bank[1][:, :].rearrange("p (a b) -> p a b", a=4)), drained, ("aT", l, 1))
                o_norm(l)
                for n, i in enumerate(BR_ORDER):
                    for q in range(4):
                        key = ("br", l, i, q)
                        wait_ready(dve, key)
                        m = merged[:, 2 * q:2 * q + 2, :].rearrange("p k t -> p (k t)")
                        gt = gates[:, KT * i + 2 * q:KT * i + 2 * q + 2, :].rearrange("p k t -> p (k t)")
                        if n == 0:
                            signals(tt(m, bank_of(key)[:, :], gt, ALU.mult), drained, key)
                        else:
                            signals(tt(prod[:, q % 2, :], bank_of(key)[:, :], gt, ALU.mult), drained, key)
                            wait_drained(dve, key)
                            ins = tt(m, m, prod[:, q % 2, :], ALU.add)
                            if n == 3:
                                ins.then_inc(merged_ready, 1)
                            else:
                                step(ins)
                add_y(("out", l))
                norm(l, "n2")
                if l == 0:
                    ffn("dense", S_DENSE)
                    add_y("dense")

            wait_ready(dve, "logits")
            signals(dve.tensor_copy(lg[:, :, :], bank_of("logits")[:, 0:TT * E].rearrange("p (t e) -> p t e", t=TT)), drained, "logits")
            wait_drained(dve, "logits")
            for e in range(E):
                last = dve.memset(rank[:, :, e:e + 1], float(E - e))
            step(last)

            def wide(col):
                return col.unsqueeze(2).to_broadcast([P, TT, E])

            def first_max(src, top, hot):
                step(dve.tensor_reduce(top[:, :], src[:, :, :], AX, ALU.max))
                step(tt(eq[:, :, :], src[:, :, :], wide(top[:, :]), ALU.is_equal))
                step(tt(eq[:, :, :], eq[:, :, :], rank[:, :, :], ALU.mult))
                step(dve.tensor_reduce(best[:, :], eq[:, :, :], AX, ALU.max))
                step(tt(hot[:, :, :], rank[:, :, :], wide(best[:, :]), ALU.is_equal))

            first_max(lg, top1, hot1)
            step(stt(out=lg2[:, :, :].rearrange("p t e -> p (t e)"), in0=hot1[:, :, :].rearrange("p t e -> p (t e)"), scalar=-3e38,
                     in1=lg[:, :, :].rearrange("p t e -> p (t e)"), op0=ALU.mult, op1=ALU.add))
            first_max(lg2, top2, hot2)
            tt(diff[:, :], top2[:, :], top1[:, :], ALU.subtract).then_inc(diff_ready, 1)
            dve.wait_ge(ed_ready, 1)
            step(ts(den[:, :], ed[:, :], 1.0, None, ALU.add))
            step(dve.reciprocal(wt1[:, :], den[:, :]))
            step(tt(wt2[:, :], ed[:, :], wt1[:, :], ALU.mult))
            step(tt(hot1[:, :, :], hot1[:, :, :], wide(wt1[:, :]), ALU.mult))
            step(tt(hot2[:, :, :], hot2[:, :, :], wide(wt2[:, :]), ALU.mult))
            tt(gate[:, :, :], hot1[:, :, :], hot2[:, :, :], ALU.add).then_inc(gate_ready, 1)
            dve.wait_ge(gate_ready, 1)
            with dve.Fori(0, E) as e:
                ffn("moe", S_MOE, e)
                add_y("moe", e, lambda t: gate[:, t, bass.ds(e, 1)])


_INS = ['x', 'norm1_g', 'w_in', 'w_gate', 'b_gate', 'w_branch', 'w_out', 'pool_w', 'pool_scale', 'attn_qn_g', 'attn_kn_g',
        'lam_q1', 'lam_k1', 'lam_q2', 'lam_k2', 'attn_subln_g', 'conv_w', 'conv_b', 'conv_ln_g', 'conv_ln_b', 'sgu_ln_g',
        'sgu_ln_b', 'sgu_w', 'sgu_b', 'norm2_g', 'ffn_w1', 'ffn_w3', 'ffn_w2', 'moe_router', 'moe_w1', 'moe_w3', 'moe_w2']


def kernel(**inputs):
    import concourse.bacc as _bacc
    from concourse.bass_utils import run_bass_kernel_spmd as _run

    nc = _bacc.Bacc("TRN2", target_bir_lowering=False, num_devices=1)
    arrays, args = {}, []
    for name in _INS:
        a = np.ascontiguousarray(inputs[name])
        arrays[f"in_{name}"] = a
        args.append(nc.dram_tensor(f"in_{name}", a.shape, mybir.dt.from_np(a.dtype), kind="ExternalInput").ap())
    arrays["in_table"] = shape_constants()
    args.append(nc.dram_tensor("in_table", (P, C_N), F32, kind="ExternalInput").ap())
    args.append(nc.dram_tensor("out_y", (1, T, D), F32, kind="ExternalOutput").ap())
    trunk_kernel(nc, *args)
    r = _run(nc, [arrays], core_ids=[0])
    return r.results[0]["out_y"]
```

```python
import math
from contextlib import ExitStack

import numpy as np
import concourse.bass as bass
from concourse import mybir

F32 = mybir.dt.float32
I32 = mybir.dt.int32
ALU = mybir.AluOpType
ACT = mybir.ActivationFunctionType
AX = mybir.AxisListType.X

P = 128
D = 1024
T = 256
TT = T // P
KT = D // P
L = 2
BR = D // 4
CT = BR // P
HEADS = 4
QK = 32
MAPS = 2 * HEADS
VD = 64
TAPS = 31
PAD = TAPS - 1
PPAD = 16
NGATE = 4
FF = 2816
FE = 3584
E = 8
US = 256
S_DENSE = FF // US
S_MOE = FE // US
SLOTS = 7
MORE = 7
CAP = 128
EPS = 1e-6
MASKED = -1e30
SCALE = QK ** -0.5

IN_COL = {"pa": 0, "q": 256, "k": 512, "v": 768, "ca": 1024, "cg": 1280, "du": 1536, "dv": 1792}
IN_ORDER = ["q", "k", "v", "cg", "ca", "dv", "du", "pa"]
TOK_PARTS = ("q", "k", "v", "dv")
BR_ORDER = [0, 3, 2, 1]

PC_N1, PC_N2, PC_BG, PC_PS, PC_CB, PC_CG, PC_CBB, PC_CW = 0, 8, 16, 48, 50, 52, 54, 56
PC = PC_CW + 2 * TAPS

C_ID, C_TRI, C_COS, C_SIN, C_INV, C_IOTA = 0, 128, 256, 288, 320, 832
C_N = C_IOTA + 128

ARENA = 18176


def shape_constants():
    c = np.zeros((P, C_N), np.float32)
    c[:, C_ID:C_ID + P] = np.eye(P, dtype=np.float32)
    c[:, C_TRI:C_TRI + P] = np.triu(np.ones((P, P), np.float32), 1)
    pos = np.arange(T, dtype=np.float32)
    inv = (1.0 / (np.float32(10000.0) ** (np.arange(0, QK, 2, dtype=np.float32) / np.float32(QK)))).astype(np.float32)
    ang = (pos[:, None] * inv[None, :]).astype(np.float32)
    for t in range(TT):
        c[:, C_COS + 16 * t:C_COS + 16 * t + 16] = np.cos(ang[P * t:P * t + P])
        c[:, C_SIN + 16 * t:C_SIN + 16 * t + 16] = np.sin(ang[P * t:P * t + P])
    for g, w in enumerate((2, 4, 8, 16)):
        row = 1.0 / np.minimum(np.arange(T) + 1, w).astype(np.float32)
        c[64 * (g % 2):64 * (g % 2) + 64, C_INV + T * (g // 2):C_INV + T * (g // 2) + T] = row
    c[:, C_IOTA:C_IOTA + P] = np.arange(P)
    return c


class Plan:

    def __init__(self):
        self.jobs, self.uses = {}, [0] * 8
        self.units, self.index = [], {}
        self.acc_units = 0

    def job(self, key, bank, stride=0):
        self.jobs[key] = (bank, self.uses[bank], stride)
        self.uses[bank] += 1

    def unit(self, key, freed):
        self.index[key] = len(self.units)
        self.units.append((key, freed))

    def acc(self, stride=0):
        self.acc_units += 1
        return ("acc", self.acc_units, stride)


def make_plan():
    p = Plan()
    for l in range(L):
        p.job(("par", l), 1 + l)
    p.job(("wsT", 0), 0)
    p.job(("wsT", 1), 3)

    def ffn(key, steps):
        for b in range(4):
            p.job(("y", key, b), b)
        for s in range(steps + 1):
            if s < steps:
                for j, w in enumerate(("h1", "h3")):
                    p.job((w, key, s), 4 + 2 * (s % 2) + j)
                    p.unit((w, key, s), ("ready", (w, key, s)))
            if s >= 1:
                p.unit(("w2", key, s - 1), ("ready", ("y", key, 3)) if s == steps else p.acc())

    for l in range(L):
        for j in range(4):
            p.job(("n1", l, j), 4 + j)
        for i, w in enumerate(IN_ORDER):
            p.job((w, l), 4 + i % 4)
            p.unit(("in", l, w), ("ready", (w, l)))
        p.job(("qT", l), 0)
        p.job(("kT", l), 1)
        for g in range(16):
            p.job(("g", l, g), 4 + g % 4)
            p.unit(("gate", l, g), ("ready", ("g", l, g)))
        for qb in (1, 0):
            for b in range(4):
                p.job(("s", l, qb, b), b)
        p.job(("pool", l), 0)
        p.job(("sv", l), 1)
        p.job(("mean", l), 2)
        p.job(("var", l), 3)
        for b in range(3):
            p.job(("aT", l, b), b)
        p.job(("o", l), 3)
        p.job(("ybT", l), 0)
        for i in BR_ORDER:
            for q in range(4):
                p.job(("br", l, i, q), 4 + q)
            p.unit(("branch", l, i), ("ready", ("br", l, i, 3)))
        for b in range(4):
            p.job(("y", ("out", l), b), b)
        for u in range(4):
            p.unit(("out", l, u), ("ready", ("y", ("out", l), 3)) if u == 3 else p.acc())
        for j in range(4):
            p.job(("n2", l, j), 4 + j)
        if l == 0:
            ffn("dense", S_DENSE)
    p.job("logits", 0)
    p.job("places", 1)

    p.moe_base = len(p.units)
    for s in range(S_MOE + 1):
        if s < S_MOE:
            for j, w in enumerate(("h1", "h3")):
                p.job((w, "moe", s), 4 + 2 * (s % 2) + j, S_MOE // 2)
                p.unit((w, "moe", s), ("ready", (w, "moe", s)))
        if s >= 1:
            p.unit(("w2", "moe", s - 1), p.acc(S_MOE))
    p.moe_units = len(p.units) - p.moe_base
    assert p.moe_units % (SLOTS + MORE) == 0
    before = list(p.uses)

    for b in range(4):
        p.job(("y", "moe", b), b, 1)

    p.uses = before
    for b in (2, 3):
        p.job(("gather", "first", b), b)
    for b in range(2):
        p.job(("yT", b), b, 1)
    per = 5
    p.job(("turn", 0), 2, per)
    p.job(("turn", 1), 3, per)
    for t in range(TT):
        for n in range(2):
            p.job(("spread", t, n), 2 + n, per)
    p.job(("gates", "T"), 2, per)
    for b in (2, 3):
        p.job(("gather", "next", b), b, per)
    for key, (b, n, stride) in list(p.jobs.items()):
        if b == 3 and stride == per:
            p.jobs[key] = (b, n, per - 1)
    for key in (("turn", 0), ("turn", 1), *(("spread", t, n) for t in range(TT) for n in range(2))):
        b, n, stride = p.jobs[key]
        p.jobs[(*key, "end")] = (b, n + E * stride, 0)
    return p


def trunk_kernel(nc, x, norm1_g, w_in, w_gate, b_gate, w_branch, w_out, pool_w, pool_scale,
                 attn_qn_g, attn_kn_g, lam_q1, lam_k1, lam_q2, lam_k2, attn_subln_g,
                 conv_w, conv_b, conv_ln_g, conv_ln_b, sgu_ln_g, sgu_ln_b, sgu_w, sgu_b,
                 norm2_g, ffn_w1, ffn_w3, ffn_w2, moe_router, moe_w1, moe_w3, moe_w2, table, out):
    plan = make_plan()
    lam_init = [0.8 - 0.6 * math.exp(-0.3 * l) for l in range(L)]

    with ExitStack() as ctx:
        def sb(name, shape, dt=F32):
            return ctx.enter_context(nc.sbuf_tensor(name, shape, dt))

        def sem(name):
            return ctx.enter_context(nc.semaphore(name))

        bank = [ctx.enter_context(nc.psum_tensor(f"bank{b}", [P, 512], F32)) for b in range(8)]

        ring = sb("ring", [P, SLOTS, 2048])
        x_tok = sb("x_tok", [P, TT, D])
        shared8k = sb("shared8k", [P, 2048])
        xn = shared8k[:, :].rearrange("p (t d) -> p t d", t=TT)
        sc1 = shared8k[:, :].rearrange("p (m k) -> p m k", m=MAPS)
        merged = shared8k[:, :].rearrange("p (k t) -> p k t", k=KT)
        hT = sb("hT", [P, KT, T])

        arena = sb("arena", [P, ARENA])
        taken = [0]

        def mix(*dims):
            n = int(np.prod(dims))
            v = arena[:, taken[0]:taken[0] + n]
            taken[0] += n
            assert taken[0] <= ARENA
            if len(dims) == 1:
                return v
            names = "abcd"[:len(dims)]
            spec = " ".join(names)
            return v.rearrange(f"p ({spec}) -> p {spec}", **dict(zip(names, dims)))

        gates = mix(4 * KT, T)
        junk = sb("junk", [P, D])
        eps = sb("eps", [P, 1])
        ssq = sb("ssq", [P, TT])
        rms = sb("rms", [P, TT])
        rstd = sb("rstd", [P, TT])
        const = sb("const", [P, C_N])
        par_rows = sb("par_rows", [PC, L, P])
        par = sb("par", [P, L, PC])
        router = sb("router", [P, KT, E])
        ident = const[:, C_ID:C_ID + P]
        tri = const[:, C_TRI:C_TRI + P]
        cos = const[:, C_COS:C_COS + 32].rearrange("p (t d) -> p t d", t=TT)
        sin = const[:, C_SIN:C_SIN + 32].rearrange("p (t d) -> p t d", t=TT)
        invcnt = const[:, C_INV:C_INV + 512].rearrange("p (c t) -> p c t", c=CT)

        qkg = sb("qkg", [P, L, 2, QK])
        lamv = sb("lamv", [P, L, 2, 2, QK])
        lamp = sb("lamp", [P, 2, QK])
        lams = sb("lams", [P, 2])
        lame = sb("lame", [P, 2])
        neglam = sb("neglam", [P, L])
        subg = sb("subg", [P, L, VD])
        qk_raw = sb("qk_raw", [P, TT, 2, BR])
        qk_n = sb("qk_n", [P, TT, 2, BR])
        att8k = mix(2048)
        qk_sq = att8k[:, 0:1024].rearrange("p (m d) -> p m d", d=QK)
        rot = att8k[:, 1024:2048].rearrange("p (t i c) -> p t i c", t=TT, i=2)
        aT = att8k[:, 0:12 * P].rearrange("p (n k) -> p n k", n=12)
        qk_ss = sb("qk_ss", [P, TT * 2 * MAPS])
        qk_rms = sb("qk_rms", [P, TT * 2 * MAPS])
        qk_rstd = sb("qk_rstd", [P, TT * 2 * MAPS])
        prod = sb("prod", [P, 2, 512])
        ra, rb = (prod[:, i, :].rearrange("p (t m d) -> p t m d", t=TT, m=16) for i in range(2))
        v_tok = mix(TT, BR)
        qT = mix(CT, T)
        kT = mix(CT, T)
        sc0 = mix(MAPS, P)
        smax = sb("smax", [P, 2, MAPS])
        nmax = sb("nmax", [P, 2, MAPS])
        esum = sb("esum", [P, 2, MAPS])
        erec = sb("erec", [P, 2, MAPS])
        elam = sb("elam", [P, 2, MAPS])
        osq = junk[:, 0:512].rearrange("p (m d) -> p m d", d=VD)
        oss = sb("oss", [P, MAPS])
        orms = sb("orms", [P, MAPS])
        orstd = sb("orstd", [P, MAPS])
        o_n = sb("o_n", [P, MAPS, VD])

        sig = mix(CT, T)
        u_pad = mix(CT, PAD + T)
        cy = mix(CT, T)
        csq = junk[:, 512:1024].rearrange("p (c t) -> p c t", c=CT)
        crms = sb("crms", [P, T])
        mean_w = sb("mean_w", [P, P])

        ws = sb("ws", [P, L, 4, P])
        wT = sb("wT", [P, L, 4, P])
        sgub = sb("sgub", [P, L, CT, P])
        slg = sb("slg", [P, L, BR])
        slb = sb("slb", [P, L, BR])
        zu = mix(CT, T)
        zv = sb("zv", [P, TT, BR])
        zsum = sb("zsum", [P, TT])
        znm = sb("znm", [P, TT])
        zss = sb("zss", [P, TT])
        zrms = sb("zrms", [P, TT])
        zrstd = sb("zrstd", [P, TT])

        pool_bd = sb("pool_bd", [P, L, CT, P])
        w1s, w2s, w4s, w8s, w16s = (mix(CT, PPAD + T) for _ in range(5))
        pooled = mix(CT, T)

        yT = [sb(f"yT{i}", [P, CT, T]) for i in range(4)]

        sil = qk_raw[:, :, :, :].rearrange("p t i c -> p t (i c)")
        act = qk_n[:, :, :, :].rearrange("p t i c -> p t (i c)")

        ring2 = arena[:, 0:2048 * MORE].rearrange("p (s c) -> p s c", s=MORE)
        taken[0] = 2048 * MORE
        xg = mix(KT, CAP)
        y_feat = mix(KT, CAP)
        y_slot = mix(D)
        gatesT = mix(TT, P)
        pick = mix(TT, CAP)
        pick_g = mix(TT, CAP)
        iota = const[:, C_IOTA:C_IOTA + CAP]
        ones = sb("ones", [P, P])

        chosen = sb("chosen", [P, TT, E + 2])
        place = sb("place", [P, TT, E + 2])
        most = sb("most", [P, 1])
        most_i = sb("most_i", [P, 1], I32)
        lg = sb("lg", [P, TT, E])
        top1 = sb("top1", [P, TT])
        top2 = sb("top2", [P, TT])
        eq = sb("eq", [P, TT, E])
        rank = sb("rank", [P, TT, E])
        best = sb("best", [P, TT])
        hot1 = sb("hot1", [P, TT, E])
        hot2 = sb("hot2", [P, TT, E])
        lg2 = sb("lg2", [P, TT, E])
        diff = sb("diff", [P, TT])
        ed = sb("ed", [P, TT])
        den = sb("den", [P, TT])
        wt1 = sb("wt1", [P, TT])
        wt2 = sb("wt2", [P, TT])
        gate = sb("gate", [P, TT, E + 2])

        loaded = [sem(f"slot{i}_loaded") for i in range(SLOTS)]
        loaded2 = [sem(f"slot{SLOTS + i}_loaded") for i in range(MORE)]
        ready = [sem(f"bank{b}_ready") for b in range(8)]
        drained = [sem(f"bank{b}_drained") for b in range(8)]
        acc_unit_used = sem("acc_unit_used")
        x_loaded = sem("x_loaded")
        const_loaded = sem("const_loaded")
        rows_loaded = sem("rows_loaded")
        bcast_loaded = sem("bcast_loaded")
        ws_loaded = sem("ws_loaded")
        bd_loaded = sem("bd_loaded")
        pool_step = sem("pool_step")
        dve_step = sem("dve_step")
        act_step = sem("act_step")
        pads_zero = sem("pads_zero")
        ones_set = sem("ones_set")
        eps_set = sem("eps_set")
        bd_zero = sem("bd_zero")
        ws_lower = sem("ws_lower")
        x_updated = sem("x_updated")
        rms_ready = sem("rms_ready")
        xn_ready = sem("xn_ready")
        qk_squared = sem("qk_squared")
        qk_summed = sem("qk_summed")
        qk_rooted = sem("qk_rooted")
        rot_ready = sem("rot_ready")
        z_shifted = sem("z_shifted")
        z_rooted = sem("z_rooted")
        z_normed = sem("z_normed")
        zu_ready = sem("zu_ready")
        lam_summed = sem("lam_summed")
        lam_exped = sem("lam_exped")
        nmax_ready = sem("nmax_ready")
        exp_ready = sem("exp_ready")
        a_ready = sem("a_ready")
        o_squared = sem("o_squared")
        o_summed = sem("o_summed")
        o_rooted = sem("o_rooted")
        o_normed = sem("o_normed")
        conv_ready = sem("conv_ready")
        c_shifted = sem("c_shifted")
        c_squared = sem("c_squared")
        c_normed = sem("c_normed")
        yc_ready = sem("yc_ready")
        pooled_ready = sem("pooled_ready")
        merged_ready = sem("merged_ready")
        diff_ready = sem("diff_ready")
        ed_ready = sem("ed_ready")
        gate_ready = sem("gate_ready")
        chosen_ready = sem("chosen_ready")
        most_ready = sem("most_ready")
        buffers_zero = sem("buffers_zero")
        pick_ready = sem("pick_ready")
        pick_g_ready = sem("pick_g_ready")
        x_final = sem("x_final")
        out_stored = sem("out_stored")

        def val(base, stride, e):
            return base if e is None else base + stride * e

        def wait_free(pe, key, e=None):
            b, n, stride = plan.jobs[key]
            if n > 0:
                pe.wait_ge(drained[b], val(n, stride, e))

        def wait_ready(eng, key, e=None):
            b, n, stride = plan.jobs[key]
            eng.wait_ge(ready[b], val(n + 1, stride, e))

        def wait_drained(eng, key, e=None):
            b, n, stride = plan.jobs[key]
            eng.wait_ge(drained[b], val(n + 1, stride, e))

        def bank_of(key):
            return bank[plan.jobs[key][0]]

        def signals(ins, sems, key):
            ins.then_inc(sems[plan.jobs[key][0]], 1)

        def slot_of(n):
            i = n - plan.moe_base
            if i < 0:
                return ring[:, n % SLOTS, :], loaded[n % SLOTS], 16 * (n // SLOTS + 1), 0
            turn, j = divmod(i, SLOTS + MORE)
            stride = 16 * (plan.moe_units // (SLOTS + MORE))
            if j >= SLOTS:
                return ring2[:, j - SLOTS, :], loaded2[j - SLOTS], 16 * (turn + 1), stride
            slot = (plan.moe_base + j) % SLOTS
            before = len(range(slot, plan.moe_base, SLOTS))
            return ring[:, slot, :], loaded[slot], 16 * (before + turn + 1), stride

        def wait_unit(pe, key, e=None):
            slot, sem_, count, stride = slot_of(plan.index[key])
            pe.wait_ge(sem_, val(count, stride, e))
            return slot

        def drams(key, e=None):
            kind = key[0]
            if kind == "in":
                _, l, w = key
                return w_in[l].rearrange("(k p) c -> p k c", p=P)[:, :, IN_COL[w]:IN_COL[w] + US]
            if kind == "gate":
                _, l, g = key
                return w_gate[l].rearrange("(k p) c -> p k c", p=P)[:, :, US * g:US * g + US]
            if kind == "branch":
                _, l, i = key
                return w_branch[l, i].rearrange("(k p) d -> p k d", p=P)
            if kind == "out":
                _, l, u = key
                return w_out[l, US * u:US * u + US, :].rearrange("(k p) d -> p k d", p=P)
            _, which, s = key
            w = {"dense": {"h1": ffn_w1, "h3": ffn_w3, "w2": ffn_w2},
                 "moe": {"h1": moe_w1, "h3": moe_w3, "w2": moe_w2}}[which][kind]
            if which == "dense":
                w = w[0:1]
            else:
                w = w[0, bass.ds(e, 1)]
            if kind == "w2":
                return w[:, US * s:US * s + US, :].rearrange("e (k p) d -> p (e k) d", p=P)
            return w[:, :, US * s:US * s + US].rearrange("e (k p) f -> p (e k) f", p=P)

        BCASTS = 1 + L * (2 + 4 + 1 + 2 + 4)

        block = ctx.enter_context(nc.Block())

        @block.sync
        def _(sp):
            def wait_used(n, e=None):
                _, freed = plan.units[n]
                if freed[0] == "ready":
                    wait_ready(sp, freed[1], e)
                else:
                    sp.wait_ge(acc_unit_used, val(freed[1], freed[2], e))

            def load(n, e=None):
                key, _ = plan.units[n]
                src = drams(key, e)
                slot, sem_, _, _ = slot_of(n)
                sp.dma_start(slot.rearrange("p (k c) -> p k c", k=src.shape[1]), src).then_inc(sem_, 16)

            for t in range(TT):
                sp.dma_start(x_tok[:, t, :], x[0, P * t:P * t + P, :]).then_inc(x_loaded, 16)
            for n in range(plan.moe_base):
                if n >= SLOTS:
                    wait_used(n - SLOTS)
                load(n)
            base, per, both = plan.moe_base, plan.moe_units, SLOTS + MORE
            for i in range(per):
                if i < SLOTS:
                    wait_used(base + i - SLOTS)
                elif i == SLOTS:
                    sp.wait_ge(x_updated, TT * (L + 1))
                elif i >= both:
                    wait_used(base + i - both, 0)
                load(base + i, 0)
            with sp.Fori(1, E) as e:
                for i in range(per):
                    if i < both:
                        wait_used(base + per + i - both, e - 1)
                    else:
                        wait_used(base + i - both, e)
                    load(base + i, e)
            sp.wait_ge(x_final, 1)
            for t in range(TT):
                sp.dma_start(out[0, P * t:P * t + P, :], x_tok[:, t, :]).then_inc(out_stored, 16)
            sp.wait_ge(out_stored, 16 * TT)

        @block.gpsimd
        def _(pool):
            steps = [0]

            def step(ins):
                steps[0] += 1
                ins.then_inc(pool_step, 1)
                pool.wait_ge(pool_step, steps[0])

            pool.memset(u_pad[:, :, 0:PAD], 0.0)
            for w in (w1s, w2s, w4s, w8s):
                pool.memset(w[:, :, 0:PPAD], 0.0)
            pool.memset(mean_w[:, :], 1.0 / BR).then_inc(pads_zero, 1)
            pool.memset(pool_bd[:, :, :, :], 0.0).then_inc(bd_zero, 1)
            pool.memset(ones[:, :], 1.0).then_inc(ones_set, 1)
            pool.wait_ge(pads_zero, 1)
            pool.wait_ge(ws_loaded, 16 * L)
            for l in range(L):
                pool.affine_select(out=ws[:, l, :, :], in_=ws[:, l, :, :], compare_op=ALU.is_ge, fill=0.0, base=0,
                                   pattern=[[0, 4], [-1, P]], channel_multiplier=1).then_inc(ws_lower, 1)
            pool.wait_ge(const_loaded, 16)
            now = slice(PPAD, PPAD + T)
            for l in range(L):
                wait_drained(pool, ("pa", l))
                for a, b, back in ((w1s, w2s, 1), (w2s, w4s, 2), (w4s, w8s, 4), (w8s, w16s, 8)):
                    step(pool.tensor_tensor(b[:, :, now], a[:, :, now], a[:, :, PPAD - back:PPAD - back + T], ALU.add))
                for g, w in enumerate((w2s, w4s, w8s, w16s)):
                    rows = slice(64 * (g % 2), 64 * (g % 2) + 64)
                    last = pool.tensor_tensor(pooled[rows, g // 2, :], w[rows, g // 2, now], invcnt[rows, g // 2, :], ALU.mult)
                step(last)
                pool.tensor_tensor(pooled[:, :, :], pooled[:, :, :], w1s[:, :, now], ALU.subtract).then_inc(pooled_ready, 1)

        @block.tensor
        def _(pe):
            def transposes(key, pairs):
                wait_free(pe, key)
                for o, i in pairs:
                    n = i.shape[0]
                    last = pe.transpose(o, i, ident[0:n, 0:n])
                signals(last, ready, key)

            def norm_transposes(l, which):
                for t in range(TT):
                    pe.wait_ge(xn_ready, TT * (2 * l + (which == "n2")) + t + 1)
                    for j in range(4):
                        if t == 0:
                            wait_free(pe, (which, l, j))
                        for k in (2 * j, 2 * j + 1):
                            last = pe.transpose(bank_of((which, l, j))[:, T * (k % 2) + P * t:T * (k % 2) + P * t + P],
                                                xn[:, t, P * k:P * k + P], ident)
                        if t == TT - 1:
                            signals(last, ready, (which, l, j))

            def feat_unit(key, ukey, k_guard=None, e=None):
                w = wait_unit(pe, ukey, e).rearrange("p (k c) -> p k c", k=KT)
                wait_free(pe, key, e)
                for c in range(2):
                    for k in range(KT):
                        if k_guard and c == 0 and k % 2 == 0:
                            wait_drained(pe, (*k_guard, k // 2))
                        last = pe.matmul(bank_of(key)[:, T * c:T * c + T], w[:, k, P * c:P * c + P], hT[:, k, :],
                                         start=(k == 0), stop=(k == KT - 1))
                signals(last, ready, key)

            def tok_unit(key, ukey, k_guard=None):
                w = wait_unit(pe, ukey).rearrange("p (k c) -> p k c", k=KT)
                wait_free(pe, key)
                for t in range(TT):
                    for k in range(KT):
                        if k_guard and t == 0 and k % 2 == 0:
                            wait_drained(pe, (*k_guard, k // 2))
                        last = pe.matmul(bank_of(key)[:, T * t:T * t + US], hT[:, k, P * t:P * t + P], w[:, k, :],
                                         start=(k == 0), stop=(k == KT - 1))
                signals(last, ready, key)

            def acc_unit(ukey, ykey, lhs, first, final, e=None):
                w = wait_unit(pe, ukey, e).rearrange("p (k d) -> p k d", k=2)
                for t in range(TT):
                    for n in range(2):
                        b = 2 * t + n
                        if first:
                            wait_free(pe, ("y", ykey, b), e)
                        for k in range(2):
                            last = pe.matmul(bank[b][:, :], lhs(k, t), w[:, k, 512 * n:512 * n + 512],
                                             start=(first and k == 0), stop=(final and k == 1))
                        if final and ykey != "moe":
                            signals(last, ready, ("y", ykey, b))
                if not final or ykey == "moe":
                    last.then_inc(acc_unit_used, 1)

            def ffn(key, steps, e=None, k_guard=None):
                for s in range(steps + 1):
                    if s < steps:
                        feat_unit(("h1", key, s), ("h1", key, s), k_guard if s == 0 else None, e)
                        feat_unit(("h3", key, s), ("h3", key, s), None, e)
                    if s >= 1:
                        wait_drained(pe, ("h3", key, s - 1), e)
                        acc_unit(("w2", key, s - 1), key,
                                 lambda k, t: act[:, (s - 1) % 2, T * k + P * t:T * k + P * t + P],
                                 s == 1, s == steps, e)

            def scores(l, qb):
                for b in range(4):
                    wait_free(pe, ("s", l, qb, b))
                keys = P * (qb + 1)
                for c in range(CT):
                    for b in range(4):
                        rows = slice(QK * b, QK * b + QK)
                        last = pe.matmul(bank[b][:, T * c:T * c + keys], qT[rows, c, P * qb:P * qb + P],
                                         kT[rows, c, 0:keys], start=True, stop=True)
                        if c == CT - 1:
                            signals(last, ready, ("s", l, qb, b))

            def hooks(l, g):
                if g == -1:
                    pe.wait_ge(rot_ready, l + 1)
                    for i, dst in enumerate(("qT", "kT")):
                        transposes((dst, l), [(bank_of((dst, l))[:, T * c + P * t:T * c + P * t + P],
                                               rot[:, t, i, P * c:P * c + P]) for c in range(CT) for t in range(TT)])
                if g == 0:
                    wait_drained(pe, ("qT", l))
                    wait_drained(pe, ("kT", l))
                    scores(l, 1)
                if g == 1:
                    scores(l, 0)
                if g == 3:
                    pe.wait_ge(pooled_ready, l + 1)
                    pe.wait_ge(bd_loaded, 16 * 4 * L)
                    wait_free(pe, ("pool", l))
                    for c in range(CT):
                        last = pe.matmul(bank_of(("pool", l))[:, T * c:T * c + T], pool_bd[:, l, c, :], pooled[:, c, :],
                                         start=True, stop=True)
                    signals(last, ready, ("pool", l))
                if g == 4:
                    pe.wait_ge(z_normed, l + 1)
                    wait_drained(pe, ("wsT", l))
                    wait_free(pe, ("sv", l))
                    for c in range(CT):
                        for n in range(TT):
                            for half in range(2):
                                grp = 2 * c + half
                                last = pe.matmul(bank_of(("sv", l))[64 * half:64 * half + 64, T * c + P * n:T * c + P * n + P],
                                                 zv[:, n, 64 * grp:64 * grp + 64], wT[:, l, grp, :],
                                                 start=True, stop=True, skip_group_check=True)
                    signals(last, ready, ("sv", l))
                if g == 8:
                    pe.wait_ge(conv_ready, l + 1)
                    pe.wait_ge(pads_zero, 1)
                    wait_free(pe, ("mean", l))
                    for c in range(CT):
                        last = pe.matmul(bank_of(("mean", l))[:, 0:T], mean_w[:, :], cy[:, c, :], start=(c == 0), stop=(c == CT - 1))
                    signals(last, ready, ("mean", l))
                if g == 9:
                    pe.wait_ge(c_squared, l + 1)
                    wait_free(pe, ("var", l))
                    for c in range(CT):
                        last = pe.matmul(bank_of(("var", l))[:, 0:T], mean_w[:, :], csq[:, c, :], start=(c == 0), stop=(c == CT - 1))
                    signals(last, ready, ("var", l))
                if g == 10:
                    pe.wait_ge(a_ready, l + 1)
                    for b in range(2):
                        transposes(("aT", l, b), [(bank[b][:, P * (2 * h + kb):P * (2 * h + kb) + P],
                                                   sc1[:, 2 * (2 * b + h), P * kb:P * kb + P]) for h in range(2) for kb in range(2)])
                    transposes(("aT", l, 2), [(bank[2][:, P * h:P * h + P], sc0[:, 2 * h, :]) for h in range(HEADS)])
                if g == 11:
                    for b in range(3):
                        wait_drained(pe, ("aT", l, b))
                    wait_free(pe, ("o", l))
                    for qb in range(2):
                        for h in range(HEADS):
                            for kb in range(qb + 1):
                                a = aT[:, 2 * h + kb if qb else 8 + h, :]
                                last = pe.matmul(bank_of(("o", l))[:, VD * (4 * qb + h):VD * (4 * qb + h) + VD], a,
                                                 v_tok[:, kb, VD * h:VD * h + VD], start=(kb == 0), stop=(kb == qb))
                    signals(last, ready, ("o", l))
                if g == 14:
                    pe.wait_ge(o_normed, l + 1)
                    flat = o_n[:, :, :].rearrange("p m d -> p (m d)")
                    transposes(("ybT", l), [(bank_of(("ybT", l))[:, T * c + P * t:T * c + P * t + P],
                                             flat[:, BR * t + P * c:BR * t + P * c + P]) for c in range(CT) for t in range(TT)])

            def branch(l, i):
                if i == 0:
                    wait_drained(pe, ("pool", l))
                elif i == 1:
                    wait_drained(pe, ("ybT", l))
                elif i == 2:
                    pe.wait_ge(yc_ready, l + 1)
                else:
                    wait_drained(pe, ("sv", l))
                w = wait_unit(pe, ("branch", l, i)).rearrange("p (k d) -> p k d", k=CT)
                for q in range(4):
                    key = ("br", l, i, q)
                    wait_free(pe, key)
                    for half in range(2):
                        d = 2 * q + half
                        for c in range(CT):
                            last = pe.matmul(bank_of(key)[:, T * half:T * half + T], w[:, c, P * d:P * d + P], yT[i][:, c, :],
                                             start=(c == 0), stop=(c == CT - 1))
                    signals(last, ready, key)

            pe.wait_ge(const_loaded, 16)
            pe.wait_ge(rows_loaded, 16 * 8 * L)
            for l in range(L):
                transposes(("par", l), [(bank_of(("par", l))[:, 0:PC], par_rows[:, l, :])])
            for l in range(L):
                norm_transposes(l, "n1")
                for i, w in enumerate(IN_ORDER):
                    (tok_unit if w in TOK_PARTS else feat_unit)((w, l), ("in", l, w), ("n1", l) if i == 0 else None)
                    if l == 0 and i == 0:
                        pe.wait_ge(ws_lower, L)
                        for j in range(L):
                            transposes(("wsT", j), [(bank_of(("wsT", j))[:, P * g:P * g + P], ws[:, j, g, :]) for g in range(4)])
                hooks(l, -1)
                for g in range(16):
                    feat_unit(("g", l, g), ("gate", l, g))
                    hooks(l, g)
                for i in BR_ORDER:
                    branch(l, i)
                for u in range(4):
                    pe.wait_ge(merged_ready, 4 * l + u + 1)
                    acc_unit(("out", l, u), ("out", l), lambda k, t: merged[:, 2 * u + k, P * t:P * t + P], u == 0, u == 3)
                norm_transposes(l, "n2")
                if l == 0:
                    ffn("dense", S_DENSE, k_guard=("n2", 0))
            for j in range(4):
                wait_drained(pe, ("n2", 1, j))
            pe.wait_ge(bcast_loaded, 16 * BCASTS)
            wait_free(pe, "logits")
            for t in range(TT):
                for k in range(KT):
                    last = pe.matmul(bank_of("logits")[:, E * t:E * t + E], hT[:, k, P * t:P * t + P], router[:, k, :],
                                     start=(k == 0), stop=(k == KT - 1))
            signals(last, ready, "logits")
            pe.wait_ge(chosen_ready, 1)
            pe.wait_ge(ones_set, 1)
            wait_free(pe, "places")
            now = slice(1, E + 1)
            spot = bank_of("places")
            pe.matmul(spot[:, 0:E], tri, chosen[:, 0, now], start=True, stop=True)
            pe.matmul(spot[:, E:2 * E], tri, chosen[:, 1, now], start=True, stop=False)
            pe.matmul(spot[:, E:2 * E], ones[:, :], chosen[:, 0, now], start=False, stop=True)
            pe.matmul(spot[:, 2 * E:3 * E], ones[:, :], chosen[:, 0, now], start=True, stop=False)
            signals(pe.matmul(spot[:, 2 * E:3 * E], ones[:, :], chosen[:, 1, now], start=False, stop=True), ready, "places")

            def gather(which, e=None):
                pe.wait_ge(pick_ready, 1 if e is None else e + 2)
                for b in (2, 3):
                    wait_free(pe, ("gather", which, b), e)
                    for j in range(4):
                        k = 4 * (b - 2) + j
                        for t in range(TT):
                            last = pe.matmul(bank[b][:, CAP * j:CAP * j + CAP], xn[:, t, P * k:P * k + P], pick[:, t, :],
                                             start=(t == 0), stop=(t == TT - 1))
                    signals(last, ready, ("gather", which, b))

            def turn(e=None, tail=()):
                for i in range(2):
                    wait_free(pe, ("turn", i, *tail), e)
                    for j in range(4):
                        last = pe.transpose(bank[2 + i][0:CAP, P * j:P * j + P], y_feat[:, 4 * i + j, :], ident)
                    signals(last, ready, ("turn", i, *tail))

            def spread(t, e=None, tail=()):
                for i in range(2):
                    wait_drained(pe, ("turn", i, *tail), e)
                for n in range(2):
                    wait_free(pe, ("spread", t, n, *tail), e)
                    signals(pe.matmul(bank[2 + n][:, :], gatesT[0:CAP, t, :], y_slot[0:CAP, 512 * n:512 * n + 512],
                                      start=True, stop=True), ready, ("spread", t, n, *tail))

            def gathered_expert(e):
                for i in range(2):
                    wait_free(pe, ("turn", i), e)
                for s in range(S_MOE + 1):
                    if s < S_MOE:
                        for w in ("h1", "h3"):
                            key = (w, "moe", s)
                            wu = wait_unit(pe, key, e).rearrange("p (k c) -> p k c", k=KT)
                            wait_free(pe, key, e)
                            for c in range(2):
                                for k in range(KT):
                                    last = pe.matmul(bank_of(key)[:, CAP * c:CAP * c + CAP], wu[:, k, P * c:P * c + P], xg[:, k, :],
                                                     start=(k == 0), stop=(k == KT - 1))
                            signals(last, ready, key)
                    if s == 0:
                        for b in range(2):
                            wait_free(pe, ("yT", b), e)
                        turn(e)
                    if s == S_MOE:
                        gather("next", e)
                    if s >= 1:
                        wait_drained(pe, ("h3", "moe", s - 1), e)
                        wu = wait_unit(pe, ("w2", "moe", s - 1), e).rearrange("p (k d) -> p k d", k=2)
                        for d in range(KT):
                            for k in range(2):
                                last = pe.matmul(bank[d // 4][:, CAP * (d % 4):CAP * (d % 4) + CAP], wu[:, k, P * d:P * d + P],
                                                 act[:, (s - 1) % 2, CAP * k:CAP * k + CAP],
                                                 start=(s == 1 and d % 4 == 0 and k == 0), stop=(s == S_MOE and k == 1),
                                                 skip_group_check=True)
                        last.then_inc(acc_unit_used, 1)
                    if s in (1, 2):
                        spread(s - 1, e)
                    if s == 2:
                        pe.wait_ge(pick_g_ready, e + 1)
                        wait_free(pe, ("gates", "T"), e)
                        for t in range(TT):
                            last = pe.transpose(bank[2][0:CAP, P * t:P * t + P], pick_g[:, t, :], ident)
                        signals(last, ready, ("gates", "T"))

            pe.wait_ge(most_ready, 1)
            most_tokens = pe.value_load(most_i[0:1, 0:1])
            with pe.If(most_tokens > CAP):
                with pe.Fori(0, E) as e:
                    ffn("moe", S_MOE, e)
            with pe.Else():
                pe.wait_ge(buffers_zero, 1)
                gather("first")
                with pe.Fori(0, E) as e:
                    gathered_expert(e)
                for b in range(2):
                    wait_drained(pe, ("yT", b), E - 1)
                turn(None, ("end",))
                for t in range(TT):
                    spread(t, None, ("end",))

        @block.scalar
        def _(act_e):
            steps = [0]

            def step(ins):
                steps[0] += 1
                ins.then_inc(act_step, 1)
                act_e.wait_ge(act_step, steps[0])

            fn = act_e.activation
            act_e.dma_start(const[:, :], table).then_inc(const_loaded, 16)
            for l in range(L):
                for c0, n, src in ((PC_N1, 8, norm1_g[l].rearrange("(k p) -> k p", p=P)),
                                   (PC_N2, 8, norm2_g[l].rearrange("(k p) -> k p", p=P)),
                                   (PC_BG, 32, b_gate[l].rearrange("(k p) -> k p", p=P)),
                                   (PC_PS, 2, pool_scale[l].rearrange("(k p) -> k p", p=P)),
                                   (PC_CB, 2, conv_b[l].rearrange("(k p) -> k p", p=P)),
                                   (PC_CG, 2, conv_ln_g[l].rearrange("(k p) -> k p", p=P)),
                                   (PC_CBB, 2, conv_ln_b[l].rearrange("(k p) -> k p", p=P)),
                                   (PC_CW, 2 * TAPS, conv_w[l].rearrange("t (h p) -> (t h) p", p=P))):
                    act_e.dma_start(par_rows[c0:c0 + n, l, :], src).then_inc(rows_loaded, 16)
            for l in range(L):
                act_e.dma_start(ws[:, l, :, :], sgu_w[l].rearrange("g t s -> t g s")).then_inc(ws_loaded, 16)

            act_e.dma_start(router[:, :, :], moe_router[0].rearrange("(k p) e -> p k e", p=P)).then_inc(bcast_loaded, 16)
            for l in range(L):
                for dst, src in ((qkg[:, l, 0, :], attn_qn_g[l]), (qkg[:, l, 1, :], attn_kn_g[l]),
                                 (lamv[:, l, 0, 0, :], lam_q1[l]), (lamv[:, l, 0, 1, :], lam_k1[l]),
                                 (lamv[:, l, 1, 0, :], lam_q2[l]), (lamv[:, l, 1, 1, :], lam_k2[l]),
                                 (subg[:, l, :], attn_subln_g[l]), (slg[:, l, :], sgu_ln_g[l]), (slb[:, l, :], sgu_ln_b[l])):
                    act_e.dma_start(dst, src.partition_broadcast(P)).then_inc(bcast_loaded, 16)
                for g in range(4):
                    h = 64 * (g % 2)
                    act_e.dma_start(sgub[h:h + 64, l, g // 2, :], sgu_b[l, g].partition_broadcast(64)).then_inc(bcast_loaded, 16)
            act_e.wait_ge(bd_zero, 1)
            for l in range(L):
                for g in range(4):
                    h = 64 * (g % 2)
                    act_e.dma_start(pool_bd[h:h + 64, l, g // 2, h:h + 64], pool_w[l, g]).then_inc(bd_loaded, 16)

            def copy_out(key, dst, func=ACT.Identity, **kw):
                wait_ready(act_e, key)
                signals(fn(dst, bank_of(key)[:, 0:dst.free_size()] if len(dst.shape) == 2 else
                           bank_of(key)[:, 0:dst.shape[1] * dst.shape[2]].rearrange("p (a b) -> p a b", a=dst.shape[1]),
                           func, **kw), drained, key)

            def norm(l, which):
                n = 2 * l + (which == "n2")
                for t in range(TT):
                    if n == 0:
                        act_e.wait_ge(x_loaded, 16 * TT)
                    else:
                        act_e.wait_ge(x_updated, TT * (n - 1) + t + 1)
                    step(fn(junk[:, :], x_tok[:, t, :], ACT.Square, accum_out=ssq[:, t:t + 1]))
                    fn(rms[:, t:t + 1], ssq[:, t:t + 1], ACT.Sqrt, scale=1.0 / D, bias=eps[:, :]).then_inc(rms_ready, 1)
                for j in (0, 2):
                    norm_out(act_e, l, which, j)

            def norm_out(eng, l, which, j):
                wait_ready(eng, (which, l, j))
                for k in (2 * j, 2 * j + 1):
                    c = (PC_N1 if which == "n1" else PC_N2) + k
                    last = fn(hT[:, k, :], bank_of((which, l, j))[:, T * (k % 2):T * (k % 2) + T], ACT.Copy,
                              scale=par[:, l, c:c + 1])
                signals(last, drained, (which, l, j))

            def hooks(l, g):
                if g == -1:
                    act_e.wait_ge(z_shifted, l + 1)
                    for t in range(TT):
                        last = fn(junk[:, BR * t:BR * t + BR], zv[:, t, :], ACT.Square, accum_out=zss[:, t:t + 1])
                    step(last)
                    fn(zrms[:, :], zss[:, :], ACT.Sqrt, scale=1.0 / BR, bias=eps[:, :]).then_inc(z_rooted, 1)
                    act_e.wait_ge(lam_summed, l + 1)
                    fn(lame[:, :], lams[:, :], ACT.Exp).then_inc(lam_exped, 1)
                    copy_out(("qT", l), qT[:, :, :])
                if g == 0:
                    for b in range(4):
                        copy_out(("s", l, 1, b), sc1[:, b::4, :])
                if g == 1:
                    for b in range(4):
                        wait_ready(act_e, ("s", l, 0, b))
                        signals(fn(sc0[:, b::4, :], bank[b][:, :].rearrange("p (c k) -> p c k", c=CT)[:, :, 0:P], ACT.Identity),
                                drained, ("s", l, 0, b))
                if g in (2, 3):
                    qb = 3 - g
                    sc = sc1 if qb else sc0
                    act_e.wait_ge(nmax_ready, 2 * l + g - 1)
                    for m in range(MAPS):
                        last = fn(sc[:, m, :], sc[:, m, :], ACT.Exp, scale=SCALE, bias=nmax[:, qb, m:m + 1],
                                  accum_out=esum[:, qb, m:m + 1])
                    last.then_inc(exp_ready, 1)
                if g == 3:
                    wait_ready(act_e, ("pool", l))
                    for c in range(CT):
                        last = fn(yT[0][:, c, :], bank_of(("pool", l))[:, T * c:T * c + T], ACT.Copy,
                                  scale=par[:, l, PC_PS + c:PC_PS + c + 1])
                    signals(last, drained, ("pool", l))
                if g == 9 - 1:
                    act_e.wait_ge(c_shifted, l + 1)
                    fn(csq[:, :, :], cy[:, :, :], ACT.Square).then_inc(c_squared, 1)
                if g == 9:
                    wait_ready(act_e, ("var", l))
                    signals(fn(crms[:, :], bank_of(("var", l))[:, 0:T], ACT.Sqrt, bias=eps[:, :]), drained, ("var", l))
                if g == 10:
                    for b in (0, 2):
                        copy_out(("aT", l, b), aT[:, 4 * b:4 * b + 4, :])
                    act_e.wait_ge(c_normed, l + 1)
                    for c in range(CT):
                        last = fn(yT[2][:, c, :], cy[:, c, :], ACT.Silu, scale=par[:, l, PC_CG + c:PC_CG + c + 1],
                                  bias=par[:, l, PC_CBB + c:PC_CBB + c + 1])
                    last.then_inc(yc_ready, 1)
                if g == 11:
                    wait_ready(act_e, ("o", l))
                    fn(osq[:, :, :], bank_of(("o", l))[:, :].rearrange("p (m d) -> p m d", m=MAPS), ACT.Square).then_inc(o_squared, 1)
                    act_e.wait_ge(o_summed, l + 1)
                    fn(orms[:, :], oss[:, :], ACT.Sqrt, scale=1.0 / VD, bias=eps[:, :]).then_inc(o_rooted, 1)
                if g == 14:
                    copy_out(("ybT", l), yT[1][:, :, :])

            def ffn(key, nsteps, e=None):
                for s in range(nsteps):
                    wait_ready(act_e, ("h1", key, s), e)
                    if s >= 2:
                        wait_drained(act_e, ("h3", key, s - 2), e)
                    signals(fn(sil[:, s % 2, :], bank_of(("h1", key, s))[:, :], ACT.Silu), drained, ("h1", key, s))

            act_e.wait_ge(eps_set, 1)
            for l in range(L):
                copy_out(("par", l), par[:, l, :], ACT.Identity)
            for l in range(L):
                wait_drained(act_e, ("par", l))
            for l in range(L):
                norm(l, "n1")
                for w in IN_ORDER:
                    key = (w, l)
                    if w in ("q", "k"):
                        copy_out(key, qk_raw[:, :, int(w == "k"), :])
                        if w == "k":
                            wait_drained(act_e, key)
                            wait_drained(act_e, ("q", l))
                            fn(qk_sq[:, :, :].rearrange("p m d -> p (m d)"), qk_raw[:, :, :, :].rearrange("p t i c -> p (t i c)"),
                               ACT.Square).then_inc(qk_squared, 1)
                    elif w == "v":
                        copy_out(key, v_tok[:, :, :])
                        act_e.wait_ge(qk_summed, l + 1)
                        fn(qk_rms[:, :], qk_ss[:, :], ACT.Sqrt, scale=1.0 / QK, bias=eps[:, :]).then_inc(qk_rooted, 1)
                        if l == 0:
                            for j in range(L):
                                copy_out(("wsT", j), wT[:, j, :, :])
                    elif w == "cg":
                        copy_out(key, sig[:, :, :], ACT.Sigmoid)
                    elif w == "dv":
                        wait_ready(act_e, key)
                        for t in range(TT):
                            last = fn(zv[:, t, :], bank_of(key)[:, T * t:T * t + BR], ACT.Gelu, accum_out=zsum[:, t:t + 1])
                        signals(last, drained, key)
                    elif w == "du":
                        copy_out(key, zu[:, :, :], ACT.Gelu)
                    elif w == "pa":
                        copy_out(key, w1s[:, :, PPAD:PPAD + T])
                hooks(l, -1)
                for g in range(16):
                    wait_ready(act_e, ("g", l, g))
                    for c in range(2):
                        d = 2 * g + c
                        last = fn(gates[:, d, :], bank_of(("g", l, g))[:, T * c:T * c + T], ACT.Sigmoid,
                                  bias=par[:, l, PC_BG + d:PC_BG + d + 1])
                    signals(last, drained, ("g", l, g))
                    hooks(l, g)
                norm(l, "n2")
                if l == 0:
                    ffn("dense", S_DENSE)
            act_e.wait_ge(diff_ready, 1)
            fn(ed[:, :], diff[:, :], ACT.Exp).then_inc(ed_ready, 1)

            def turned(e=None, tail=()):
                for i in range(2):
                    key = ("turn", i, *tail)
                    wait_ready(act_e, key, e)
                    signals(fn(y_slot[0:CAP, 512 * i:512 * i + 512], bank_of(key)[0:CAP, :], ACT.Copy), drained, key)

            def gathered_expert(e):
                for s in range(S_MOE):
                    key = ("h1", "moe", s)
                    wait_ready(act_e, key, e)
                    if s >= 2:
                        wait_drained(act_e, ("h3", "moe", s - 2), e)
                    signals(fn(sil[:, s % 2, 0:2 * CAP], bank_of(key)[:, 0:2 * CAP], ACT.Silu), drained, key)
                    if s == 0:
                        turned(e)
                    if s == 2:
                        wait_ready(act_e, ("gates", "T"), e)
                        signals(fn(gatesT[0:CAP, :, :], bank[2][0:CAP, 0:TT * P].rearrange("p (t n) -> p t n", t=TT), ACT.Copy),
                                drained, ("gates", "T"))

            act_e.wait_ge(most_ready, 1)
            most_tokens = act_e.value_load(most_i[0:1, 0:1])
            with act_e.If(most_tokens > CAP):
                with act_e.Fori(0, E) as e:
                    ffn("moe", S_MOE, e)
            with act_e.Else():
                act_e.wait_ge(buffers_zero, 1)
                with act_e.Fori(0, E) as e:
                    gathered_expert(e)
                turned(None, ("end",))

        @block.vector
        def _(dve):
            steps = [0]
            tt, ts, stt = dve.tensor_tensor, dve.tensor_scalar, dve.scalar_tensor_tensor

            def step(ins):
                steps[0] += 1
                ins.then_inc(dve_step, 1)
                dve.wait_ge(dve_step, steps[0])

            def norm(l, which):
                n = 2 * l + (which == "n2")
                for t in range(TT):
                    dve.wait_ge(rms_ready, TT * n + t + 1)
                    step(dve.reciprocal(rstd[:, t:t + 1], rms[:, t:t + 1]))
                    ts(xn[:, t, :], x_tok[:, t, :], rstd[:, t:t + 1], None, ALU.mult).then_inc(xn_ready, 1)
                for j in (1, 3):
                    wait_ready(dve, (which, l, j))
                    for k in (2 * j, 2 * j + 1):
                        c = (PC_N1 if which == "n1" else PC_N2) + k
                        last = ts(hT[:, k, :], bank_of((which, l, j))[:, T * (k % 2):T * (k % 2) + T], par[:, l, c:c + 1], None, ALU.mult)
                    signals(last, drained, (which, l, j))

            def add_y(key, e=None, scale=None):
                for t in range(TT):
                    for n in range(2):
                        k = ("y", key, 2 * t + n)
                        xs = x_tok[:, t, 512 * n:512 * n + 512]
                        if key == "moe":
                            dve.wait_ge(acc_unit_used, acc_at("moe", S_MOE - 1, e))
                        else:
                            wait_ready(dve, k, e)
                        if scale is None:
                            tt(xs, bank_of(k)[:, :], xs, ALU.add).then_inc(drained[2 * t + n], 1)
                        else:
                            stt(out=xs, in0=bank_of(k)[:, :], scalar=scale(t), in1=xs, op0=ALU.mult, op1=ALU.add)\
                                .then_inc(drained[2 * t + n], 1)
                    if key != "moe":
                        wait_drained(dve, ("y", key, 2 * t), e)
                        wait_drained(dve, ("y", key, 2 * t + 1), e)
                        dve.sem_inc(x_updated, 1)

            def rope(l):
                dve.wait_ge(qk_squared, l + 1)
                dve.tensor_reduce(qk_ss[:, :], qk_sq[:, :, :], AX, ALU.add).then_inc(qk_summed, 1)
                dve.wait_ge(qk_rooted, l + 1)
                step(dve.reciprocal(qk_rstd[:, :], qk_rms[:, :]))
                flat = "p t i (m d) -> p (t i m) d"
                step(tt(qk_n[:, :, :, :].rearrange(flat, d=QK), qk_raw[:, :, :, :].rearrange(flat, d=QK),
                        qk_rstd[:, :].unsqueeze(2).to_broadcast([P, TT * 2 * MAPS, QK]), ALU.mult))
                for i in range(2):
                    v = qk_n[:, :, i, :].rearrange("p t (m d) -> p t m d", d=QK)
                    last = tt(v, v, qkg[:, l, i, :].unsqueeze(1).unsqueeze(1).to_broadcast([P, TT, MAPS, QK]), ALU.mult)
                step(last)
                v = qk_n[:, :, :, :].rearrange("p t i (m d) -> p t (i m) d", d=QK)
                r = rot[:, :, :, :].rearrange("p t i (m d) -> p t (i m) d", d=QK)
                lo, hi = slice(0, 16), slice(16, 32)
                c = cos.unsqueeze(2).to_broadcast([P, TT, 16, 16])
                s = sin.unsqueeze(2).to_broadcast([P, TT, 16, 16])
                tt(ra[:, :, :, :], v[:, :, :, lo], c, ALU.mult)
                step(tt(rb[:, :, :, :], v[:, :, :, hi], s, ALU.mult))
                step(tt(r[:, :, :, lo], ra[:, :, :, :], rb[:, :, :, :], ALU.subtract))
                tt(ra[:, :, :, :], v[:, :, :, hi], c, ALU.mult)
                step(tt(rb[:, :, :, :], v[:, :, :, lo], s, ALU.mult))
                tt(r[:, :, :, hi], ra[:, :, :, :], rb[:, :, :, :], ALU.add).then_inc(rot_ready, 1)

            def lam(l):
                step(tt(lamp[:, :, :], lamv[:, l, :, 0, :], lamv[:, l, :, 1, :], ALU.mult))
                dve.tensor_reduce(lams[:, :], lamp[:, :, :], AX, ALU.add).then_inc(lam_summed, 1)

            def z_norm_shift(l):
                wait_drained(dve, ("dv", l))
                step(ts(znm[:, :], zsum[:, :], -1.0 / BR, None, ALU.mult))
                for t in range(TT):
                    last = ts(zv[:, t, :], zv[:, t, :], znm[:, t:t + 1], None, ALU.add)
                last.then_inc(z_shifted, 1)

            def z_norm_scale(l):
                dve.wait_ge(z_rooted, l + 1)
                step(dve.reciprocal(zrstd[:, :], zrms[:, :]))
                for t in range(TT):
                    last = stt(out=zv[:, t, :], in0=zv[:, t, :], scalar=zrstd[:, t:t + 1], in1=slg[:, l, :],
                               op0=ALU.mult, op1=ALU.mult)
                step(last)
                tt(zv[:, :, :], zv[:, :, :], slb[:, l, :].unsqueeze(1).to_broadcast([P, TT, BR]), ALU.add).then_inc(z_normed, 1)

            def row_max(l, qb):
                sc = sc1 if qb else sc0
                keys = P * (qb + 1)
                for b in range(4):
                    wait_drained(dve, ("s", l, qb, b))
                step(dve.memset(sc[0:64, :, keys - 64:keys], MASKED))
                step(dve.tensor_reduce(smax[:, qb, :], sc[:, :, :], AX, ALU.max))
                ts(nmax[:, qb, :], smax[:, qb, :], -SCALE, None, ALU.mult).then_inc(nmax_ready, 1)

            def conv(l):
                for k in range(TAPS):
                    for c in range(CT):
                        col = PC_CW + 2 * k + c
                        if k == 0:
                            ins = ts(cy[:, c, :], u_pad[:, c, 0:T], par[:, l, col:col + 1],
                                     par[:, l, PC_CB + c:PC_CB + c + 1], ALU.mult, ALU.add)
                        else:
                            dve.wait_ge(dve_step, steps[0] - 1)
                            ins = stt(out=cy[:, c, :], in0=u_pad[:, c, k:k + T], scalar=par[:, l, col:col + 1],
                                      in1=cy[:, c, :], op0=ALU.mult, op1=ALU.add)
                        if k == TAPS - 1 and c == CT - 1:
                            ins.then_inc(conv_ready, 1)
                        else:
                            steps[0] += 1
                            ins.then_inc(dve_step, 1)

            def combine(l):
                dve.wait_ge(exp_ready, 2 * l + 2)
                step(dve.reciprocal(erec[:, :, :], esum[:, :, :]))
                step(ts(elam[:, :, :], erec[:, :, :], neglam[:, l:l + 1], None, ALU.mult))
                for sc, qb in ((sc1, 1), (sc0, 0)):
                    for h in range(HEADS):
                        last = ts(sc[:, 2 * h + 1, :], sc[:, 2 * h + 1, :], elam[:, qb, 2 * h + 1:2 * h + 2], None, ALU.mult)
                step(last)
                for sc, qb in ((sc1, 1), (sc0, 0)):
                    for h in range(HEADS):
                        last = stt(out=sc[:, 2 * h, :], in0=sc[:, 2 * h, :], scalar=erec[:, qb, 2 * h:2 * h + 1],
                                   in1=sc[:, 2 * h + 1, :], op0=ALU.mult, op1=ALU.add)
                last.then_inc(a_ready, 1)

            def o_norm(l):
                dve.wait_ge(o_squared, l + 1)
                dve.tensor_reduce(oss[:, :], osq[:, :, :], AX, ALU.add).then_inc(o_summed, 1)
                dve.wait_ge(o_rooted, l + 1)
                step(dve.reciprocal(orstd[:, :], orms[:, :]))
                wait_ready(dve, ("o", l))
                signals(tt(o_n[:, :, :], bank_of(("o", l))[:, :].rearrange("p (m d) -> p m d", m=MAPS),
                           orstd[:, :].unsqueeze(2).to_broadcast([P, MAPS, VD]), ALU.mult), drained, ("o", l))
                wait_drained(dve, ("o", l))
                tt(o_n[:, :, :], o_n[:, :, :], subg[:, l, :].unsqueeze(1).to_broadcast([P, MAPS, VD]), ALU.mult)\
                    .then_inc(o_normed, 1)

            def ffn(key, nsteps, e=None):
                for s in range(nsteps):
                    wait_drained(dve, ("h1", key, s), e)
                    wait_ready(dve, ("h3", key, s), e)
                    if s >= 3:
                        dve.wait_ge(acc_unit_used, acc_at(key, s - 2, e))
                    elif s == 2:
                        dve.wait_ge(acc_unit_used, acc_at(key, 0, e))
                    signals(tt(act[:, s % 2, :], bank_of(("h3", key, s))[:, :], sil[:, s % 2, :], ALU.mult), drained, ("h3", key, s))

            def acc_at(key, s, e):
                freed = plan.units[plan.index[("w2", key, s)]][1]
                return val(freed[1], freed[2], e)

            dve.memset(eps[:, :], EPS).then_inc(eps_set, 1)
            dve.wait_ge(bcast_loaded, 16 * BCASTS)
            dve.wait_ge(const_loaded, 16)
            for l in range(L):
                step(ts(subg[:, l, :], subg[:, l, :], 1.0 - lam_init[l], None, ALU.mult))
            dve.wait_ge(x_loaded, 16 * TT)
            wait_drained(dve, ("par", 0))
            wait_drained(dve, ("par", 1))
            dve.wait_ge(pads_zero, 1)
            for l in range(L):
                norm(l, "n1")
                lam(l)
                rope(l)
                wait_ready(dve, ("ca", l))
                wait_drained(dve, ("cg", l))
                signals(tt(u_pad[:, :, PAD:PAD + T], bank_of(("ca", l))[:, :].rearrange("p (c t) -> p c t", c=CT), sig[:, :, :], ALU.mult),
                        drained, ("ca", l))
                z_norm_shift(l)
                z_norm_scale(l)
                dve.wait_ge(lam_exped, l + 1)
                step(stt(out=neglam[:, l:l + 1], in0=lame[:, 1:2], scalar=-lam_init[l], in1=lame[:, 0:1],
                         op0=ALU.add, op1=ALU.subtract))
                wait_ready(dve, ("kT", l))
                signals(dve.tensor_copy(kT[:, :, :], bank_of(("kT", l))[:, :].rearrange("p (c t) -> p c t", c=CT)), drained, ("kT", l))
                row_max(l, 1)
                row_max(l, 0)
                wait_drained(dve, ("ca", l))
                conv(l)
                combine(l)
                wait_ready(dve, ("sv", l))
                wait_drained(dve, ("du", l))
                step(tt(yT[3][:, :, :].rearrange("p c (n t) -> p c n t", n=TT),
                        bank_of(("sv", l))[:, :].rearrange("p (c n t) -> p c n t", c=CT, n=TT),
                        sgub[:, l, :, :].unsqueeze(2).to_broadcast([P, CT, TT, P]), ALU.add))
                signals(tt(yT[3][:, :, :], yT[3][:, :, :], zu[:, :, :], ALU.mult), drained, ("sv", l))
                wait_ready(dve, ("mean", l))
                dve.wait_ge(conv_ready, l + 1)
                mean = bank_of(("mean", l))[:, 0:T].unsqueeze(1).to_broadcast([P, CT, T])
                tt(cy[:, :, :], cy[:, :, :], mean, ALU.subtract).then_inc(c_shifted, 1)
                dve.wait_ge(c_shifted, l + 1)
                dve.sem_inc(drained[plan.jobs[("mean", l)][0]], 1)
                wait_drained(dve, ("var", l))
                step(dve.reciprocal(crms[:, :], crms[:, :]))
                tt(cy[:, :, :], cy[:, :, :], crms[:, :].unsqueeze(1).to_broadcast([P, CT, T]), ALU.mult).then_inc(c_normed, 1)
                wait_ready(dve, ("aT", l, 1))
                signals(dve.tensor_copy(aT[:, 4:8, :], bank[1][:, :].rearrange("p (a b) -> p a b", a=4)), drained, ("aT", l, 1))
                o_norm(l)
                for n, i in enumerate(BR_ORDER):
                    for q in range(4):
                        key = ("br", l, i, q)
                        wait_ready(dve, key)
                        m = merged[:, 2 * q:2 * q + 2, :].rearrange("p k t -> p (k t)")
                        gt = gates[:, KT * i + 2 * q:KT * i + 2 * q + 2, :].rearrange("p k t -> p (k t)")
                        if n == 0:
                            signals(tt(m, bank_of(key)[:, :], gt, ALU.mult), drained, key)
                        else:
                            signals(tt(prod[:, q % 2, :], bank_of(key)[:, :], gt, ALU.mult), drained, key)
                            wait_drained(dve, key)
                            ins = tt(m, m, prod[:, q % 2, :], ALU.add)
                            if n == 3:
                                ins.then_inc(merged_ready, 1)
                            else:
                                step(ins)
                add_y(("out", l))
                norm(l, "n2")
                if l == 0:
                    ffn("dense", S_DENSE)
                    add_y("dense")

            wait_ready(dve, "logits")
            signals(dve.tensor_copy(lg[:, :, :], bank_of("logits")[:, 0:TT * E].rearrange("p (t e) -> p t e", t=TT)), drained, "logits")
            wait_drained(dve, "logits")
            now = slice(1, E + 1)
            dve.memset(chosen[:, :, :], 0.0)
            dve.memset(place[:, :, :], 0.0)
            dve.memset(gate[:, :, :], 0.0)
            for e in range(E):
                last = dve.memset(rank[:, :, e:e + 1], float(E - e))
            step(last)

            def wide(col):
                return col.unsqueeze(2).to_broadcast([P, TT, E])

            def first_max(src, top, hot):
                step(dve.tensor_reduce(top[:, :], src[:, :, :], AX, ALU.max))
                step(tt(eq[:, :, :], src[:, :, :], wide(top[:, :]), ALU.is_equal))
                step(tt(eq[:, :, :], eq[:, :, :], rank[:, :, :], ALU.mult))
                step(dve.tensor_reduce(best[:, :], eq[:, :, :], AX, ALU.max))
                step(tt(hot[:, :, :], rank[:, :, :], wide(best[:, :]), ALU.is_equal))

            first_max(lg, top1, hot1)
            step(stt(out=lg2[:, :, :].rearrange("p t e -> p (t e)"), in0=hot1[:, :, :].rearrange("p t e -> p (t e)"), scalar=-3e38,
                     in1=lg[:, :, :].rearrange("p t e -> p (t e)"), op0=ALU.mult, op1=ALU.add))
            first_max(lg2, top2, hot2)
            tt(chosen[:, :, now], hot1[:, :, :], hot2[:, :, :], ALU.add).then_inc(chosen_ready, 1)
            tt(diff[:, :], top2[:, :], top1[:, :], ALU.subtract).then_inc(diff_ready, 1)
            dve.wait_ge(ed_ready, 1)
            step(ts(den[:, :], ed[:, :], 1.0, None, ALU.add))
            step(dve.reciprocal(wt1[:, :], den[:, :]))
            step(tt(wt2[:, :], ed[:, :], wt1[:, :], ALU.mult))
            step(tt(hot1[:, :, :], hot1[:, :, :], wide(wt1[:, :]), ALU.mult))
            step(tt(hot2[:, :, :], hot2[:, :, :], wide(wt2[:, :]), ALU.mult))
            tt(gate[:, :, now], hot1[:, :, :], hot2[:, :, :], ALU.add).then_inc(gate_ready, 1)

            wait_ready(dve, "places")
            dve.tensor_copy(place[:, :, now], bank_of("places")[:, 0:TT * E].rearrange("p (t e) -> p t e", t=TT))
            signals(dve.tensor_reduce(most[:, :], bank_of("places")[:, 2 * E:3 * E], AX, ALU.max), drained, "places")
            wait_drained(dve, "places")
            dve.tensor_copy(most_i[:, :], most[:, :]).then_inc(most_ready, 1)
            dve.wait_ge(gate_ready, 1)
            dve.wait_ge(most_ready, 1)

            def choose(dst, weight, col):
                for t in range(TT):
                    last = ts(dst[:, t, :], iota, place[:, t, col], weight[:, t, col], ALU.is_equal, ALU.mult)
                return last

            def gathered_out(which, e=None):
                for b in (2, 3):
                    key = ("gather", which, b)
                    wait_ready(dve, key, e)
                    c = PC_N2 + 4 * (b - 2)
                    signals(tt(xg[:, 4 * (b - 2):4 * (b - 2) + 4, :], bank[b][:, 0:4 * CAP].rearrange("p (k n) -> p k n", k=4),
                               par[:, L - 1, c:c + 4].unsqueeze(2).to_broadcast([P, 4, CAP]), ALU.mult), drained, key)

            def add_spread(t, e=None, tail=()):
                for n in range(2):
                    key = ("spread", t, n, *tail)
                    xs = x_tok[:, t, 512 * n:512 * n + 512]
                    wait_ready(dve, key, e)
                    signals(tt(xs, bank_of(key)[:, :], xs, ALU.add), drained, key)

            def gathered_expert(e):
                choose(pick_g, gate, bass.ds(e + 1, 1)).then_inc(pick_g_ready, 1)
                choose(pick, chosen, bass.ds(e + 2, 1)).then_inc(pick_ready, 1)
                for s in range(S_MOE):
                    key = ("h3", "moe", s)
                    wait_drained(dve, ("h1", "moe", s), e)
                    wait_ready(dve, key, e)
                    if s >= 2:
                        dve.wait_ge(acc_unit_used, acc_at("moe", s - 2, e))
                    signals(tt(act[:, s % 2, 0:2 * CAP], bank_of(key)[:, 0:2 * CAP], sil[:, s % 2, 0:2 * CAP], ALU.mult), drained, key)
                    if s in (1, 2):
                        add_spread(s - 1, e)
                gathered_out("next", e)
                dve.wait_ge(acc_unit_used, acc_at("moe", S_MOE - 1, e))
                for b in range(2):
                    signals(dve.tensor_copy(y_feat[:, 4 * b:4 * b + 4, :], bank[b][:, 0:4 * CAP].rearrange("p (k n) -> p k n", k=4)),
                            drained, ("yT", b))

            most_tokens = dve.value_load(most_i[0:1, 0:1])
            with dve.If(most_tokens > CAP):
                with dve.Fori(0, E) as e:
                    ffn("moe", S_MOE, e)
                    add_y("moe", e, lambda t: gate[:, t, bass.ds(e + 1, 1)])
                for b in range(4):
                    wait_drained(dve, ("y", "moe", b), E - 1)
                dve.sem_inc(x_final, 1)
            with dve.Else():
                dve.memset(y_feat[:, :, :], 0.0)
                dve.memset(gatesT[:, :, :], 0.0).then_inc(buffers_zero, 1)
                dve.wait_ge(buffers_zero, 1)
                choose(pick, chosen, slice(1, 2)).then_inc(pick_ready, 1)
                gathered_out("first")
                with dve.Fori(0, E) as e:
                    gathered_expert(e)
                for t in range(TT):
                    add_spread(t, None, ("end",))
                for n in range(2):
                    wait_drained(dve, ("spread", TT - 1, n, "end"))
                dve.sem_inc(x_final, 1)


_INS = ['x', 'norm1_g', 'w_in', 'w_gate', 'b_gate', 'w_branch', 'w_out', 'pool_w', 'pool_scale', 'attn_qn_g', 'attn_kn_g',
        'lam_q1', 'lam_k1', 'lam_q2', 'lam_k2', 'attn_subln_g', 'conv_w', 'conv_b', 'conv_ln_g', 'conv_ln_b', 'sgu_ln_g',
        'sgu_ln_b', 'sgu_w', 'sgu_b', 'norm2_g', 'ffn_w1', 'ffn_w3', 'ffn_w2', 'moe_router', 'moe_w1', 'moe_w3', 'moe_w2']


def kernel(**inputs):
    import concourse.bacc as _bacc
    from concourse.bass_utils import run_bass_kernel_spmd as _run

    nc = _bacc.Bacc("TRN2", target_bir_lowering=False, num_devices=1)
    arrays, args = {}, []
    for name in _INS:
        a = np.ascontiguousarray(inputs[name])
        arrays[f"in_{name}"] = a
        args.append(nc.dram_tensor(f"in_{name}", a.shape, mybir.dt.from_np(a.dtype), kind="ExternalInput").ap())
    arrays["in_table"] = shape_constants()
    args.append(nc.dram_tensor("in_table", (P, C_N), F32, kind="ExternalInput").ap())
    args.append(nc.dram_tensor("out_y", (1, T, D), F32, kind="ExternalOutput").ap())
    trunk_kernel(nc, *args)
    r = _run(nc, [arrays], core_ids=[0])
    return r.results[0]["out_y"]
```

```python
import math
from contextlib import ExitStack

import numpy as np
import concourse.bass as bass
from concourse import mybir

F32 = mybir.dt.float32
F32R = mybir.dt.float32r
I32 = mybir.dt.int32
ALU = mybir.AluOpType
ACT = mybir.ActivationFunctionType
AX = mybir.AxisListType.X

P = 128
D = 1024
T = 256
TT = T // P
KT = D // P
L = 2
BR = D // 4
CT = BR // P
HEADS = 4
QK = 32
MAPS = 2 * HEADS
VD = 64
TAPS = 31
PAD = TAPS - 1
PPAD = 16
NGATE = 4
FF = 2816
FE = 3584
E = 8
US = 256
S_DENSE = FF // US
S_MOE = FE // US
SLOTS = 3
MORE = 4
HI = 3
LO = 3
LO_AHEAD = 2
CAP = 128
EPS = 1e-6
MASKED = -1e30
SCALE = QK ** -0.5

IN_COL = {"pa": 0, "q": 256, "k": 512, "v": 768, "ca": 1024, "cg": 1280, "du": 1536, "dv": 1792}
IN_ORDER = ["q", "k", "v", "cg", "ca", "dv", "du", "pa"]
TOK_PARTS = ("q", "k", "v", "dv")
BR_ORDER = [0, 3, 2, 1]

PC_N1, PC_N2, PC_BG, PC_PS, PC_CB, PC_CG, PC_CBB, PC_CW = 0, 8, 16, 48, 50, 52, 54, 56
PC = PC_CW + 2 * TAPS

C_ID, C_TRI, C_COS, C_SIN, C_INV, C_IOTA = 0, 128, 256, 288, 320, 832
C_N = C_IOTA + 128

ARENA = 15456


def shape_constants():
    c = np.zeros((P, C_N), np.float32)
    c[:, C_ID:C_ID + P] = np.eye(P, dtype=np.float32)
    c[:, C_TRI:C_TRI + P] = np.triu(np.ones((P, P), np.float32), 1)
    pos = np.arange(T, dtype=np.float32)
    inv = (1.0 / (np.float32(10000.0) ** (np.arange(0, QK, 2, dtype=np.float32) / np.float32(QK)))).astype(np.float32)
    ang = (pos[:, None] * inv[None, :]).astype(np.float32)
    for t in range(TT):
        c[:, C_COS + 16 * t:C_COS + 16 * t + 16] = np.cos(ang[P * t:P * t + P])
        c[:, C_SIN + 16 * t:C_SIN + 16 * t + 16] = np.sin(ang[P * t:P * t + P])
    for g, w in enumerate((2, 4, 8, 16)):
        row = 1.0 / np.minimum(np.arange(T) + 1, w).astype(np.float32)
        c[64 * (g % 2):64 * (g % 2) + 64, C_INV + T * (g // 2):C_INV + T * (g // 2) + T] = row
    c[:, C_IOTA:C_IOTA + P] = np.arange(P)
    return c


class Plan:

    def __init__(self):
        self.jobs, self.uses = {}, [0] * 8
        self.units, self.index = [], {}
        self.split, self.splits = {}, []
        self.acc_units = 0

    def job(self, key, bank, stride=0):
        self.jobs[key] = (bank, self.uses[bank], stride)
        self.uses[bank] += 1

    def unit(self, key, used):
        n = len(self.units)
        self.index[key] = n
        self.units.append((key, used))
        if key[0] != "out":
            self.split[n] = len(self.splits)
            self.splits.append(n)

    def acc(self, stride=0):
        self.acc_units += 1
        return ("acc", self.acc_units, stride)


def make_plan():
    p = Plan()
    for l in range(L):
        p.job(("par", l), 1 + l)
    p.job(("wsT", 0), 0)
    p.job(("wsT", 1), 3)

    def ffn(key, steps):
        for b in range(4):
            p.job(("y", key, b), b)
        for s in range(steps + 1):
            if s < steps:
                for j, w in enumerate(("h1", "h3")):
                    p.job((w, key, s), 4 + 2 * (s % 2) + j)
                    p.unit((w, key, s), ("ready", (w, key, s)))
            if s >= 1:
                p.unit(("w2", key, s - 1), ("ready", ("y", key, 3)) if s == steps else p.acc())

    for l in range(L):
        for j in range(4):
            p.job(("n1", l, j), 4 + j)
        for i, w in enumerate(IN_ORDER):
            p.job((w, l), 4 + i % 4)
            p.unit(("in", l, w), ("ready", (w, l)))
        p.job(("qT", l), 0)
        p.job(("kT", l), 1)
        for g in range(16):
            p.job(("g", l, g), 4 + g % 4)
            p.unit(("gate", l, g), ("ready", ("g", l, g)))
        for qb in (1, 0):
            for b in range(4):
                p.job(("s", l, qb, b), b)
        p.job(("pool", l), 0)
        p.job(("sv", l), 1)
        p.job(("mean", l), 2)
        p.job(("var", l), 3)
        for b in range(3):
            p.job(("aT", l, b), b)
        p.job(("o", l), 3)
        p.job(("ybT", l), 0)
        for i in BR_ORDER:
            for q in range(4):
                p.job(("br", l, i, q), 4 + q)
            p.unit(("branch", l, i), ("ready", ("br", l, i, 3)))
        for b in range(4):
            p.job(("y", ("out", l), b), b)
        for u in range(4):
            p.unit(("out", l, u), ("ready", ("y", ("out", l), 3)) if u == 3 else p.acc())
        for j in range(4):
            p.job(("n2", l, j), 4 + j)
        if l == 0:
            ffn("dense", S_DENSE)
    p.job("logits", 0)
    p.job("places", 1)

    p.moe_base = len(p.units)
    for s in range(S_MOE + 1):
        if s < S_MOE:
            for j, w in enumerate(("h1", "h3")):
                p.job((w, "moe", s), 4 + 2 * (s % 2) + j, S_MOE // 2)
                p.unit((w, "moe", s), ("ready", (w, "moe", s)))
        if s >= 1:
            p.unit(("w2", "moe", s - 1), p.acc(S_MOE))
    p.moe_units = len(p.units) - p.moe_base
    assert p.moe_units % (SLOTS + MORE) == 0
    before = list(p.uses)

    for b in range(4):
        p.job(("y", "moe", b), b, 1)

    p.uses = before
    for b in (2, 3):
        p.job(("gather", "first", b), b)
    for b in range(2):
        p.job(("ys", b), b, 1)
    before = list(p.uses)
    inside = []
    for s in range(S_MOE + 1):
        if s >= 1:
            inside.append((("turn", s - 1), 2 + s % 2))
        if s in (2, 3):
            inside += [(("spread", s - 2, n), 2 + n) for n in range(2)]
        if s == 4:
            inside.append(("gates", 2))
        if s == 6:
            inside += [(("gather", "next", b), b) for b in (2, 3)]
    per = {b: sum(1 for _, x in inside if x == b) for b in (2, 3)}
    for key, b in inside:
        p.job(key, b, per[b])
    for t in range(TT):
        for n in range(2):
            p.jobs[("spread", t, n, "end")] = (2 + n, before[2 + n] + E * per[2 + n] + t, 0)
    return p


def trunk_kernel(nc, x, norm1_g, w_in, w_gate, b_gate, w_branch, w_out, pool_w, pool_scale,
                 attn_qn_g, attn_kn_g, lam_q1, lam_k1, lam_q2, lam_k2, attn_subln_g,
                 conv_w, conv_b, conv_ln_g, conv_ln_b, sgu_ln_g, sgu_ln_b, sgu_w, sgu_b,
                 norm2_g, ffn_w1, ffn_w3, ffn_w2, moe_router, moe_w1, moe_w3, moe_w2, table, out):
    plan = make_plan()
    lam_init = [0.8 - 0.6 * math.exp(-0.3 * l) for l in range(L)]

    with ExitStack() as ctx:
        def sb(name, shape, dt=F32):
            return ctx.enter_context(nc.sbuf_tensor(name, shape, dt))

        def sem(name):
            return ctx.enter_context(nc.semaphore(name))

        bank = [ctx.enter_context(nc.psum_tensor(f"bank{b}", [P, 512], F32)) for b in range(8)]

        ring = sb("ring", [P, SLOTS, 2048])
        x_tok = sb("x_tok", [P, TT, D])
        shared8k = sb("shared8k", [P, 2048])
        xn = shared8k[:, :].rearrange("p (t d) -> p t d", t=TT)
        sc1 = shared8k[:, :].rearrange("p (m k) -> p m k", m=MAPS)
        merged = shared8k[:, :].rearrange("p (k t) -> p k t", k=KT)
        h_hi = sb("h_hi", [P, KT, T], F32R)
        h_lo = sb("h_lo", [P, KT, T], F32R)
        w_hi = sb("w_hi", [P, HI, 2048], F32R)
        w_lo = sb("w_lo", [P, LO, 2048], F32R)
        act_hi = sb("act_hi", [P, 2, 512], F32R)
        act_lo = sb("act_lo", [P, 2, 512], F32R)
        router_hi = sb("router_hi", [P, KT, E], F32R)
        router_lo = sb("router_lo", [P, KT, E], F32R)

        arena = sb("arena", [P, ARENA])
        taken = [0]

        def mix(*dims):
            n = int(np.prod(dims))
            v = arena[:, taken[0]:taken[0] + n]
            taken[0] += n
            assert taken[0] <= ARENA
            if len(dims) == 1:
                return v
            names = "abcd"[:len(dims)]
            spec = " ".join(names)
            return v.rearrange(f"p ({spec}) -> p {spec}", **dict(zip(names, dims)))

        gates = mix(4 * KT, T)
        eps = sb("eps", [P, 1])
        ssq = sb("ssq", [P, TT])
        rms = sb("rms", [P, TT])
        rstd = sb("rstd", [P, TT])
        const = sb("const", [P, C_N])
        par_rows = sb("par_rows", [PC, L, P])
        par = sb("par", [P, L, PC])
        router = sb("router", [P, KT, E])
        ident = const[:, C_ID:C_ID + P]
        tri = const[:, C_TRI:C_TRI + P]
        cos = const[:, C_COS:C_COS + 32].rearrange("p (t d) -> p t d", t=TT)
        sin = const[:, C_SIN:C_SIN + 32].rearrange("p (t d) -> p t d", t=TT)
        invcnt = const[:, C_INV:C_INV + 512].rearrange("p (c t) -> p c t", c=CT)

        qkg = sb("qkg", [P, L, 2, QK])
        lamv = sb("lamv", [P, L, 2, 2, QK])
        lamp = sb("lamp", [P, 2, QK])
        lams = sb("lams", [P, 2])
        lame = sb("lame", [P, 2])
        neglam = sb("neglam", [P, L])
        subg = sb("subg", [P, L, VD])
        qk_raw = sb("qk_raw", [P, TT, 2, BR])
        att8k = mix(2048)
        qk_sq = att8k[:, 0:1024].rearrange("p (m d) -> p m d", d=QK)
        rot = att8k[:, 1024:2048].rearrange("p (t i c) -> p t i c", t=TT, i=2)
        aT = att8k[:, 0:12 * P].rearrange("p (n k) -> p n k", n=12)
        qk_ss = sb("qk_ss", [P, TT * 2 * MAPS])
        qk_rms = sb("qk_rms", [P, TT * 2 * MAPS])
        qk_rstd = sb("qk_rstd", [P, TT * 2 * MAPS])
        prod = sb("prod", [P, 2, 512])
        junk = prod[:, :, :].rearrange("p a b -> p (a b)")
        ra, rb = (prod[:, i, :].rearrange("p (t m d) -> p t m d", t=TT, m=16) for i in range(2))
        v_tok = mix(TT, BR)
        qT = mix(CT, T)
        kT = mix(CT, T)
        sc0 = mix(MAPS, P)
        smax = sb("smax", [P, 2, MAPS])
        nmax = sb("nmax", [P, 2, MAPS])
        esum = sb("esum", [P, 2, MAPS])
        erec = sb("erec", [P, 2, MAPS])
        elam = sb("elam", [P, 2, MAPS])
        osq = junk[:, 0:512].rearrange("p (m d) -> p m d", d=VD)
        oss = sb("oss", [P, MAPS])
        orms = sb("orms", [P, MAPS])
        orstd = sb("orstd", [P, MAPS])
        o_n = qT.rearrange("p c t -> p (c t)").rearrange("p (m d) -> p m d", d=VD)

        u_pad = mix(CT, PAD + T)
        cy = mix(CT, T)
        sig = cy
        csq = junk[:, 512:1024].rearrange("p (c t) -> p c t", c=CT)
        crms = sb("crms", [P, T])
        mean_w = sb("mean_w", [P, P])

        ws = sc0.rearrange("p m k -> p (m k)").rearrange("p (l g s) -> p l g s", l=L, g=4)
        wT = sb("wT", [P, L, 4, P])
        sgub = sb("sgub", [P, L, CT, P])
        slg = sb("slg", [P, L, BR])
        slb = sb("slb", [P, L, BR])
        zu = mix(CT, T)
        zv = sb("zv", [P, TT, BR])
        zsum = sb("zsum", [P, TT])
        znm = sb("znm", [P, TT])
        zss = sb("zss", [P, TT])
        zrms = sb("zrms", [P, TT])
        zrstd = sb("zrstd", [P, TT])

        pool_bd = sb("pool_bd", [P, L, CT, P])
        w1s = mix(CT, PPAD + T)
        w2s, w4s = (att8k[:, (PPAD + T) * CT * i:(PPAD + T) * CT * (i + 1)].rearrange("p (c t) -> p c t", c=CT) for i in range(2))
        pooled = mix(CT, T)

        yT = [pooled, kT, cy, zv]

        sil = qk_raw[:, :, :, :].rearrange("p t i c -> p t (i c)")

        ring2 = arena[:, 0:2048 * MORE].rearrange("p (s c) -> p s c", s=MORE)
        taken[0] = 2048 * MORE
        xg = mix(KT, CAP)
        y_slot = mix(D)
        gatesT = mix(TT, P)
        pick = mix(TT, CAP)
        pick_g = mix(TT, CAP)
        iota = const[:, C_IOTA:C_IOTA + CAP]
        ones = sb("ones", [P, P])

        chosen = sb("chosen", [P, TT, E + 2])
        place = sb("place", [P, TT, E + 2])
        most = sb("most", [P, 1])
        most_i = sb("most_i", [P, 1], I32)
        lg = sb("lg", [P, TT, E])
        top1 = sb("top1", [P, TT])
        top2 = sb("top2", [P, TT])
        eq = sb("eq", [P, TT, E])
        rank = sb("rank", [P, TT, E])
        best = sb("best", [P, TT])
        hot1 = sb("hot1", [P, TT, E])
        hot2 = sb("hot2", [P, TT, E])
        lg2 = sb("lg2", [P, TT, E])
        diff = sb("diff", [P, TT])
        ed = sb("ed", [P, TT])
        den = sb("den", [P, TT])
        wt1 = sb("wt1", [P, TT])
        wt2 = sb("wt2", [P, TT])
        gate = sb("gate", [P, TT, E + 2])

        loaded = [sem(f"slot{i}_loaded") for i in range(SLOTS)]
        loaded2 = [sem(f"slot{SLOTS + i}_loaded") for i in range(MORE)]
        ready = [sem(f"bank{b}_ready") for b in range(8)]
        drained = [sem(f"bank{b}_drained") for b in range(8)]
        acc_unit_used = sem("acc_unit_used")
        x_loaded = sem("x_loaded")
        const_loaded = sem("const_loaded")
        rows_loaded = sem("rows_loaded")
        bcast_loaded = sem("bcast_loaded")
        ws_loaded = sem("ws_loaded")
        bd_loaded = sem("bd_loaded")
        dve_step = sem("dve_step")
        act_step = sem("act_step")
        pads_zero = sem("pads_zero")
        ones_set = sem("ones_set")
        eps_set = sem("eps_set")
        bd_zero = sem("bd_zero")
        ws_lower = sem("ws_lower")
        x_updated = sem("x_updated")
        rms_ready = sem("rms_ready")
        hi_ready = [sem(f"w_hi{i}_ready") for i in range(HI)]
        lo_ready = [sem(f"w_lo{i}_ready") for i in range(LO)]
        h_hi_ready = sem("h_hi_ready")
        router_split_hi = sem("router_split_hi")
        router_split = sem("router_split")
        act_ready = sem("act_ready")
        y_hi_ready = sem("y_hi_ready")
        y_ready = sem("y_ready")
        act_hi_dve = sem("act_hi_dve")
        act_hi_ready = sem("act_hi_ready")
        xg_hi_ready = sem("xg_hi_ready")
        xg_ready = sem("xg_ready")
        xg_taken = sem("xg_taken")
        xn_ready = sem("xn_ready")
        qk_squared = sem("qk_squared")
        qk_summed = sem("qk_summed")
        qk_rooted = sem("qk_rooted")
        rot_ready = sem("rot_ready")
        z_shifted = sem("z_shifted")
        z_rooted = sem("z_rooted")
        z_normed = sem("z_normed")
        zu_ready = sem("zu_ready")
        lam_summed = sem("lam_summed")
        lam_exped = sem("lam_exped")
        nmax_ready = sem("nmax_ready")
        exp_ready = sem("exp_ready")
        a_ready = sem("a_ready")
        o_squared = sem("o_squared")
        o_summed = sem("o_summed")
        o_rooted = sem("o_rooted")
        o_normed = sem("o_normed")
        conv_ready = sem("conv_ready")
        c_shifted = sem("c_shifted")
        c_squared = sem("c_squared")
        c_normed = sem("c_normed")
        yc_ready = sem("yc_ready")
        pooled_ready = sem("pooled_ready")
        merged_ready = sem("merged_ready")
        diff_ready = sem("diff_ready")
        ed_ready = sem("ed_ready")
        gate_ready = sem("gate_ready")
        chosen_ready = sem("chosen_ready")
        most_ready = sem("most_ready")
        buffers_zero = sem("buffers_zero")
        pick_ready = sem("pick_ready")
        pick_g_ready = sem("pick_g_ready")
        x_final = sem("x_final")
        out_stored = sem("out_stored")

        def val(base, stride, e):
            return base if e is None else base + stride * e

        def wait_free(pe, key, e=None):
            b, n, stride = plan.jobs[key]
            if n > 0:
                pe.wait_ge(drained[b], val(n, stride, e))

        def wait_ready(eng, key, e=None):
            b, n, stride = plan.jobs[key]
            eng.wait_ge(ready[b], val(n + 1, stride, e))

        def wait_drained(eng, key, e=None):
            b, n, stride = plan.jobs[key]
            eng.wait_ge(drained[b], val(n + 1, stride, e))

        def bank_of(key):
            return bank[plan.jobs[key][0]]

        def signals(ins, sems, key):
            ins.then_inc(sems[plan.jobs[key][0]], 1)

        def slot_of(n):
            i = n - plan.moe_base
            if i < 0:
                return ring[:, n % SLOTS, :], loaded[n % SLOTS], 16 * (n // SLOTS + 1), 0
            turn, j = divmod(i, SLOTS + MORE)
            stride = 16 * (plan.moe_units // (SLOTS + MORE))
            if j >= SLOTS:
                return ring2[:, j - SLOTS, :], loaded2[j - SLOTS], 16 * (turn + 1), stride
            slot = (plan.moe_base + j) % SLOTS
            before = len(range(slot, plan.moe_base, SLOTS))
            return ring[:, slot, :], loaded[slot], 16 * (before + turn + 1), stride

        def wait_raw(eng, n, e=None):
            slot, sem_, count, stride = slot_of(n)
            eng.wait_ge(sem_, val(count, stride, e))
            return slot

        def wait_used(eng, n, e=None):
            _, used = plan.units[n]
            if used[0] == "ready":
                wait_ready(eng, used[1], e)
            else:
                eng.wait_ge(acc_unit_used, val(used[1], used[2], e))

        def wait_split_used(eng, m, e):
            if e is not None and m < m_moe:
                if isinstance(e, int) and e == 0:
                    wait_used(eng, plan.splits[m])
                else:
                    wait_used(eng, plan.splits[m + plan.moe_units], e - 1)
            else:
                wait_used(eng, plan.splits[m], e)

        per3, per2 = plan.moe_units // HI, plan.moe_units // LO

        def wait_hi(eng, m, e=None):
            eng.wait_ge(hi_ready[m % HI], val(m // HI + 1, per3, e))

        def wait_lo(eng, m, e=None):
            eng.wait_ge(lo_ready[m % LO], val(m // LO + 1, per2, e))

        def split_hi(m, e=None):
            n = plan.splits[m]
            raw = wait_raw(nc.scalar, n, e)
            if m >= HI:
                wait_split_used(nc.scalar, m - HI, e)
            nc.scalar.activation(w_hi[:, m % HI, :], raw, ACT.Copy).then_inc(hi_ready[m % HI], 1)

        def split_lo(eng, m, e=None):
            n = plan.splits[m]
            wait_hi(eng, m, e)
            if m >= LO:
                wait_split_used(eng, m - LO, e)
            eng.tensor_tensor(w_lo[:, m % LO, :], slot_of(n)[0], w_hi[:, m % HI, :].bitcast(F32), ALU.subtract)\
                .then_inc(lo_ready[m % LO], 1)

        def lo_engine(m):
            kind, *where = plan.units[plan.splits[m]][0]
            if kind in ("in", "gate", "branch"):
                return "pool"
            return "dve"

        m_moe = plan.split[plan.moe_base]

        def parts(pe, key, pattern, k, e=None):
            m = plan.split[plan.index[key]]
            wait_lo(pe, m, e)
            return (w_hi[:, m % HI, :].rearrange(pattern, k=k), w_lo[:, m % LO, :].rearrange(pattern, k=k))

        def acc_at(key, s, e):
            used = plan.units[plan.index[("w2", key, s)]][1]
            return val(used[1], used[2], e)

        def act_count(key, s, e=None):
            return s + 1 if key == "dense" else val(S_DENSE + s + 1, S_MOE, e)

        def drams(key, e=None):
            kind = key[0]
            if kind == "in":
                _, l, w = key
                return w_in[l].rearrange("(k p) c -> p k c", p=P)[:, :, IN_COL[w]:IN_COL[w] + US]
            if kind == "gate":
                _, l, g = key
                return w_gate[l].rearrange("(k p) c -> p k c", p=P)[:, :, US * g:US * g + US]
            if kind == "branch":
                _, l, i = key
                return w_branch[l, i].rearrange("(k p) d -> p k d", p=P)
            if kind == "out":
                _, l, u = key
                return w_out[l, US * u:US * u + US, :].rearrange("(k p) d -> p k d", p=P)
            _, which, s = key
            w = {"dense": {"h1": ffn_w1, "h3": ffn_w3, "w2": ffn_w2},
                 "moe": {"h1": moe_w1, "h3": moe_w3, "w2": moe_w2}}[which][kind]
            if which == "dense":
                w = w[0:1]
            else:
                w = w[0, bass.ds(e, 1)]
            if kind == "w2":
                return w[:, US * s:US * s + US, :].rearrange("e (k p) d -> p (e k) d", p=P)
            return w[:, :, US * s:US * s + US].rearrange("e (k p) f -> p (e k) f", p=P)

        BCASTS = 1 + 2 + 4 + 1 + 2 + 4

        block = ctx.enter_context(nc.Block())

        @block.sync
        def _(sp):
            def wait_freed(n, e=None):
                if n in plan.split:
                    wait_lo(sp, plan.split[n], e)
                else:
                    wait_used(sp, n, e)

            def load(n, e=None):
                key, _ = plan.units[n]
                src = drams(key, e)
                slot, sem_, _, _ = slot_of(n)
                sp.dma_start(slot.rearrange("p (k c) -> p k c", k=src.shape[1]), src).then_inc(sem_, 16)

            for t in range(TT):
                sp.dma_start(x_tok[:, t, :], x[0, P * t:P * t + P, :]).then_inc(x_loaded, 16)
            for n in range(plan.moe_base):
                if n >= SLOTS:
                    wait_freed(n - SLOTS)
                load(n)
            base, per, both = plan.moe_base, plan.moe_units, SLOTS + MORE
            for i in range(per):
                if i < SLOTS:
                    wait_freed(base + i - SLOTS)
                elif i == SLOTS:
                    sp.wait_ge(x_updated, TT * (L + 1))
                elif i >= both:
                    wait_freed(base + i - both, 0)
                load(base + i, 0)
            with sp.Fori(1, E) as e:
                for i in range(per):
                    if i < both:
                        wait_freed(base + per + i - both, e - 1)
                    else:
                        wait_freed(base + i - both, e)
                    load(base + i, e)
            sp.wait_ge(x_final, 1)
            for t in range(TT):
                sp.dma_start(out[0, P * t:P * t + P, :], x_tok[:, t, :]).then_inc(out_stored, 16)
            sp.wait_ge(out_stored, 16 * TT)

        @block.gpsimd
        def _(pool):
            for l in range(L):
                pool.dma_start(ws[:, l, :, :], sgu_w[l].rearrange("g t s -> t g s")).then_inc(ws_loaded, 16)
            pool.dma_start(router[:, :, :], moe_router[0].rearrange("(k p) e -> p k e", p=P)).then_inc(bcast_loaded, 16)
            for dst, src in ((qkg[:, :, 0, :], attn_qn_g), (qkg[:, :, 1, :], attn_kn_g),
                             (lamv[:, :, 0, 0, :], lam_q1), (lamv[:, :, 0, 1, :], lam_k1),
                             (lamv[:, :, 1, 0, :], lam_q2), (lamv[:, :, 1, 1, :], lam_k2),
                             (subg[:, :, :], attn_subln_g), (slg[:, :, :], sgu_ln_g), (slb[:, :, :], sgu_ln_b)):
                pool.dma_start(dst, src.partition_broadcast(P)).then_inc(bcast_loaded, 16)
            for g in range(4):
                h = 64 * (g % 2)
                pool.dma_start(sgub[h:h + 64, :, g // 2, :], sgu_b[:, g].partition_broadcast(64)).then_inc(bcast_loaded, 16)
            pool.memset(u_pad[:, :, 0:PAD], 0.0)
            pool.memset(w1s[:, :, 0:PPAD], 0.0)
            pool.memset(mean_w[:, :], 1.0 / BR).then_inc(pads_zero, 1)
            pool.memset(pool_bd[:, :, :, :], 0.0).then_inc(bd_zero, 1)
            pool.wait_ge(bd_zero, 1)
            for g in range(4):
                h = 64 * (g % 2)
                pool.dma_start(pool_bd[h:h + 64, :, g // 2, h:h + 64], pool_w[:, g].rearrange("l c d -> c l d")).then_inc(bd_loaded, 16)
            pool.memset(ones[:, :], 1.0).then_inc(ones_set, 1)
            pool.wait_ge(ws_loaded, 16 * L)
            for l in range(L):
                pool.affine_select(out=ws[:, l, :, :], in_=ws[:, l, :, :], compare_op=ALU.is_ge, fill=0.0, base=0,
                                   pattern=[[0, 4], [-1, P]], channel_multiplier=1).then_inc(ws_lower, 1)
            for m in range(m_moe):
                if lo_engine(m) == "pool":
                    split_lo(pool, m)

            pool.wait_ge(most_ready, 1)
            most_tokens = pool.value_load(most_i[0:1, 0:1])
            with pool.If(most_tokens < CAP + 1):
                with pool.Fori(0, E + 1) as e:
                    pool.wait_ge(xg_hi_ready, e + 1)
                    pool.tensor_tensor(h_lo[:, :, 0:CAP], xg, h_hi[:, :, 0:CAP].bitcast(F32), ALU.subtract).then_inc(xg_ready, 1)

        @block.tensor
        def _(pe):
            def transposes(key, pairs):
                wait_free(pe, key)
                for o, i in pairs:
                    n = i.shape[0]
                    last = pe.transpose(o, i, ident[0:n, 0:n])
                signals(last, ready, key)

            def norm_transposes(l, which):
                for t in range(TT):
                    pe.wait_ge(xn_ready, TT * (2 * l + (which == "n2")) + t + 1)
                    for j in range(4):
                        if t == 0:
                            wait_free(pe, (which, l, j))
                        for k in (2 * j, 2 * j + 1):
                            last = pe.transpose(bank_of((which, l, j))[:, T * (k % 2) + P * t:T * (k % 2) + P * t + P],
                                                xn[:, t, P * k:P * k + P], ident)
                        if t == TT - 1:
                            signals(last, ready, (which, l, j))

            def three(out_, a, b, start, stop):
                pe.matmul(out_, a[0], b[0], start=start, stop=False)
                pe.matmul(out_, a[0], b[1], start=False, stop=False)
                return pe.matmul(out_, a[1], b[0], start=False, stop=stop)

            def feat_unit(key, ukey, k_guard=None, e=None):
                w, wl = parts(pe, ukey, "p (k c) -> p k c", KT, e)
                wait_free(pe, key, e)
                for c in range(2):
                    for k in range(KT):
                        if k_guard and c == 0 and k % 2 == 0:
                            wait_drained(pe, (*k_guard, k // 2))
                        cols = slice(P * c, P * c + P)
                        last = three(bank_of(key)[:, T * c:T * c + T], (w[:, k, cols], wl[:, k, cols]),
                                     (h_hi[:, k, :], h_lo[:, k, :]), k == 0, k == KT - 1)
                signals(last, ready, key)

            def tok_unit(key, ukey, k_guard=None):
                w, wl = parts(pe, ukey, "p (k c) -> p k c", KT)
                wait_free(pe, key)
                for t in range(TT):
                    for k in range(KT):
                        if k_guard and t == 0 and k % 2 == 0:
                            wait_drained(pe, (*k_guard, k // 2))
                        toks = slice(P * t, P * t + P)
                        last = three(bank_of(key)[:, T * t:T * t + US], (h_hi[:, k, toks], h_lo[:, k, toks]),
                                     (w[:, k, :], wl[:, k, :]), k == 0, k == KT - 1)
                signals(last, ready, key)

            def acc_unit(ukey, ykey, lhs, first, final, e=None):
                if ukey[0] == "out":
                    w = wait_raw(pe, plan.index[ukey]).rearrange("p (k d) -> p k d", k=2)
                else:
                    w, wl = parts(pe, ukey, "p (k d) -> p k d", 2, e)
                for t in range(TT):
                    for n in range(2):
                        b = 2 * t + n
                        cols = slice(512 * n, 512 * n + 512)
                        if first:
                            wait_free(pe, ("y", ykey, b), e)
                        for k in range(2):
                            start, stop = first and k == 0, final and k == 1
                            if ukey[0] == "out":
                                last = pe.matmul(bank[b][:, :], lhs(k, t), w[:, k, cols], start=start, stop=stop)
                            else:
                                last = three(bank[b][:, :], lhs(k, t), (w[:, k, cols], wl[:, k, cols]), start, stop)
                        if final and ykey != "moe":
                            signals(last, ready, ("y", ykey, b))
                if not final or ykey == "moe":
                    last.then_inc(acc_unit_used, 1)

            def ffn(key, steps, e=None, k_guard=None):
                for s in range(steps + 1):
                    if s < steps:
                        feat_unit(("h1", key, s), ("h1", key, s), k_guard if s == 0 else None, e)
                        feat_unit(("h3", key, s), ("h3", key, s), None, e)
                    if s >= 1:
                        pe.wait_ge(act_ready, act_count(key, s - 1, e))
                        acc_unit(("w2", key, s - 1), key,
                                 lambda k, t: tuple(a[:, (s - 1) % 2, T * k + P * t:T * k + P * t + P] for a in (act_hi, act_lo)),
                                 s == 1, s == steps, e)

            def scores(l, qb):
                for b in range(4):
                    wait_free(pe, ("s", l, qb, b))
                keys = P * (qb + 1)
                for c in range(CT):
                    for b in range(4):
                        rows = slice(QK * b, QK * b + QK)
                        last = pe.matmul(bank[b][:, T * c:T * c + keys], qT[rows, c, P * qb:P * qb + P],
                                         kT[rows, c, 0:keys], start=True, stop=True)
                        if c == CT - 1:
                            signals(last, ready, ("s", l, qb, b))

            def hooks(l, g):
                if g == -1:
                    pe.wait_ge(rot_ready, l + 1)
                    for i, dst in enumerate(("qT", "kT")):
                        transposes((dst, l), [(bank_of((dst, l))[:, T * c + P * t:T * c + P * t + P],
                                               rot[:, t, i, P * c:P * c + P]) for c in range(CT) for t in range(TT)])
                if g == 0:
                    wait_drained(pe, ("qT", l))
                    wait_drained(pe, ("kT", l))
                    scores(l, 1)
                if g == 1:
                    scores(l, 0)
                if g == 3:
                    pe.wait_ge(pooled_ready, l + 1)
                    pe.wait_ge(bd_loaded, 16 * 4)
                    wait_free(pe, ("pool", l))
                    for c in range(CT):
                        last = pe.matmul(bank_of(("pool", l))[:, T * c:T * c + T], pool_bd[:, l, c, :], pooled[:, c, :],
                                         start=True, stop=True)
                    signals(last, ready, ("pool", l))
                if g == 4:
                    pe.wait_ge(z_normed, l + 1)
                    wait_drained(pe, ("wsT", l))
                    wait_free(pe, ("sv", l))
                    for c in range(CT):
                        for n in range(TT):
                            for half in range(2):
                                grp = 2 * c + half
                                last = pe.matmul(bank_of(("sv", l))[64 * half:64 * half + 64, T * c + P * n:T * c + P * n + P],
                                                 zv[:, n, 64 * grp:64 * grp + 64], wT[:, l, grp, :],
                                                 start=True, stop=True, skip_group_check=True)
                    signals(last, ready, ("sv", l))
                if g == 8:
                    pe.wait_ge(conv_ready, l + 1)
                    pe.wait_ge(pads_zero, 1)
                    wait_free(pe, ("mean", l))
                    for c in range(CT):
                        last = pe.matmul(bank_of(("mean", l))[:, 0:T], mean_w[:, :], cy[:, c, :], start=(c == 0), stop=(c == CT - 1))
                    signals(last, ready, ("mean", l))
                if g == 9:
                    pe.wait_ge(c_squared, l + 1)
                    wait_free(pe, ("var", l))
                    for c in range(CT):
                        last = pe.matmul(bank_of(("var", l))[:, 0:T], mean_w[:, :], csq[:, c, :], start=(c == 0), stop=(c == CT - 1))
                    signals(last, ready, ("var", l))
                if g == 10:
                    pe.wait_ge(a_ready, l + 1)
                    for b in range(2):
                        transposes(("aT", l, b), [(bank[b][:, P * (2 * h + kb):P * (2 * h + kb) + P],
                                                   sc1[:, 2 * (2 * b + h), P * kb:P * kb + P]) for h in range(2) for kb in range(2)])
                    transposes(("aT", l, 2), [(bank[2][:, P * h:P * h + P], sc0[:, 2 * h, :]) for h in range(HEADS)])
                if g == 11:
                    for b in range(3):
                        wait_drained(pe, ("aT", l, b))
                    wait_free(pe, ("o", l))
                    for qb in range(2):
                        for h in range(HEADS):
                            for kb in range(qb + 1):
                                a = aT[:, 2 * h + kb if qb else 8 + h, :]
                                last = pe.matmul(bank_of(("o", l))[:, VD * (4 * qb + h):VD * (4 * qb + h) + VD], a,
                                                 v_tok[:, kb, VD * h:VD * h + VD], start=(kb == 0), stop=(kb == qb))
                    signals(last, ready, ("o", l))
                if g == 14:
                    pe.wait_ge(o_normed, l + 1)
                    flat = o_n[:, :, :].rearrange("p m d -> p (m d)")
                    transposes(("ybT", l), [(bank_of(("ybT", l))[:, T * c + P * t:T * c + P * t + P],
                                             flat[:, BR * t + P * c:BR * t + P * c + P]) for c in range(CT) for t in range(TT)])

            def branch(l, n, i):
                pe.wait_ge(y_ready, 4 * l + n + 1)
                w, wl = parts(pe, ("branch", l, i), "p (k d) -> p k d", CT)
                for q in range(4):
                    key = ("br", l, i, q)
                    wait_free(pe, key)
                    for half in range(2):
                        cols = slice(P * (2 * q + half), P * (2 * q + half) + P)
                        for c in range(CT):
                            toks = slice(T * c, T * c + T)
                            last = three(bank_of(key)[:, T * half:T * half + T], (w[:, c, cols], wl[:, c, cols]),
                                         (act_hi[:, n % 2, toks], act_lo[:, n % 2, toks]), c == 0, c == CT - 1)
                    signals(last, ready, key)

            pe.wait_ge(const_loaded, 16)
            pe.wait_ge(rows_loaded, 16 * 8)
            for l in range(L):
                transposes(("par", l), [(bank_of(("par", l))[:, 0:PC], par_rows[:, l, :])])
            for l in range(L):
                norm_transposes(l, "n1")
                for i, w in enumerate(IN_ORDER):
                    (tok_unit if w in TOK_PARTS else feat_unit)((w, l), ("in", l, w), ("n1", l) if i == 0 else None)
                    if l == 0 and i == 0:
                        pe.wait_ge(ws_lower, L)
                        for j in range(L):
                            transposes(("wsT", j), [(bank_of(("wsT", j))[:, P * g:P * g + P], ws[:, j, g, :]) for g in range(4)])
                hooks(l, -1)
                for g in range(16):
                    feat_unit(("g", l, g), ("gate", l, g))
                    hooks(l, g)
                for n, i in enumerate(BR_ORDER):
                    branch(l, n, i)
                for u in range(4):
                    pe.wait_ge(merged_ready, 4 * l + u + 1)
                    acc_unit(("out", l, u), ("out", l), lambda k, t: merged[:, 2 * u + k, P * t:P * t + P], u == 0, u == 3)
                norm_transposes(l, "n2")
                if l == 0:
                    ffn("dense", S_DENSE, k_guard=("n2", 0))
            for j in range(4):
                wait_drained(pe, ("n2", 1, j))
            pe.wait_ge(router_split, 1)
            wait_free(pe, "logits")
            for t in range(TT):
                toks = slice(P * t, P * t + P)
                for k in range(KT):
                    last = three(bank_of("logits")[:, E * t:E * t + E], (h_hi[:, k, toks], h_lo[:, k, toks]),
                                 (router_hi[:, k, :], router_lo[:, k, :]), k == 0, k == KT - 1)
            signals(last, ready, "logits")
            pe.wait_ge(chosen_ready, 1)
            pe.wait_ge(ones_set, 1)
            wait_free(pe, "places")
            now = slice(1, E + 1)
            spot = bank_of("places")
            pe.matmul(spot[:, 0:E], tri, chosen[:, 0, now], start=True, stop=True)
            pe.matmul(spot[:, E:2 * E], tri, chosen[:, 1, now], start=True, stop=False)
            pe.matmul(spot[:, E:2 * E], ones[:, :], chosen[:, 0, now], start=False, stop=True)
            pe.matmul(spot[:, 2 * E:3 * E], ones[:, :], chosen[:, 0, now], start=True, stop=False)
            signals(pe.matmul(spot[:, 2 * E:3 * E], ones[:, :], chosen[:, 1, now], start=False, stop=True), ready, "places")

            def gather(which, e=None):
                pe.wait_ge(pick_ready, 1 if e is None else e + 2)
                for b in (2, 3):
                    wait_free(pe, ("gather", which, b), e)
                    for j in range(4):
                        k = 4 * (b - 2) + j
                        for t in range(TT):
                            last = pe.matmul(bank[b][:, CAP * j:CAP * j + CAP], xn[:, t, P * k:P * k + P], pick[:, t, :],
                                             start=(t == 0), stop=(t == TT - 1))
                    signals(last, ready, ("gather", which, b))

            def spread(t, e=None, tail=()):
                for n in range(2):
                    wait_free(pe, ("spread", t, n, *tail), e)
                    signals(pe.matmul(bank[2 + n][:, :], gatesT[:, t, :], y_slot[:, 512 * n:512 * n + 512],
                                      start=True, stop=True), ready, ("spread", t, n, *tail))

            def turn(s, e):
                wait_drained(pe, ("h3", "moe", s), e)
                wait_free(pe, ("turn", s), e)
                for c in range(2):
                    last = pe.transpose(bank_of(("turn", s))[:, CAP * c:CAP * c + CAP],
                                        sil[:, s % 2, P * c:P * c + P], ident)
                signals(last, ready, ("turn", s))

            def gathered_expert(e):
                pe.wait_ge(xg_ready, e + 1)
                for s in range(S_MOE + 1):
                    for w in ("h1", "h3"):
                        if s < S_MOE:
                            key = (w, "moe", s)
                            wu, wl = parts(pe, key, "p (k c) -> p k c", KT, e)
                            wait_free(pe, key, e)
                            for k in range(KT):
                                last = three(bank_of(key)[:, 0:US], (h_hi[:, k, 0:CAP], h_lo[:, k, 0:CAP]),
                                             (wu[:, k, :], wl[:, k, :]), k == 0, k == KT - 1)
                            signals(last, ready, key)
                        if w == "h1" and 1 <= s < S_MOE:
                            turn(s - 1, e)
                    if s >= 1:
                        wait_drained(pe, ("turn", s - 1), e)
                        wu, wl = parts(pe, ("w2", "moe", s - 1), "p (k d) -> p k d", 2, e)
                        for n in range(2):
                            if s == 1:
                                wait_free(pe, ("ys", n), e)
                            if s == S_MOE - 1 and n == 1:
                                turn(s, e)
                            cols = slice(512 * n, 512 * n + 512)
                            for k in range(2):
                                rows = slice(CAP * k, CAP * k + CAP)
                                last = three(bank[n][:, :], (act_hi[:, (s - 1) % 2, rows], act_lo[:, (s - 1) % 2, rows]),
                                             (wu[:, k, cols], wl[:, k, cols]), s == 1 and k == 0, s == S_MOE and k == 1)
                        last.then_inc(acc_unit_used, 1)
                    if s in (2, 3):
                        wait_drained(pe, ("ys", 1), e - 1)
                        spread(s - 2, e)
                    if s == 4:
                        pe.wait_ge(pick_g_ready, e + 1)
                        wait_free(pe, "gates", e)
                        for t in range(TT):
                            last = pe.transpose(bank[2][:, P * t:P * t + P], pick_g[:, t, :], ident)
                        signals(last, ready, "gates")
                    if s == 6:
                        gather("next", e)

            pe.wait_ge(most_ready, 1)
            most_tokens = pe.value_load(most_i[0:1, 0:1])
            with pe.If(most_tokens > CAP):
                with pe.Fori(0, E) as e:
                    ffn("moe", S_MOE, e)
            with pe.Else():
                pe.wait_ge(buffers_zero, 1)
                gather("first")
                with pe.Fori(0, E) as e:
                    gathered_expert(e)
                wait_drained(pe, ("ys", 1), E - 1)
                for t in range(TT):
                    spread(t, None, ("end",))

        @block.scalar
        def _(act_e):
            steps = [0]

            def step(ins):
                steps[0] += 1
                ins.then_inc(act_step, 1)
                act_e.wait_ge(act_step, steps[0])

            fn = act_e.activation
            done = [0]

            def hi_until(m):
                while done[0] <= min(m, m_moe - 1):
                    split_hi(done[0])
                    done[0] += 1

            def after(key):
                hi_until(plan.split[plan.index[key]] + HI)
            act_e.dma_start(const[:, :], table).then_inc(const_loaded, 16)
            for c0, n, src in ((PC_N1, 8, norm1_g), (PC_N2, 8, norm2_g), (PC_BG, 32, b_gate), (PC_PS, 2, pool_scale),
                               (PC_CB, 2, conv_b), (PC_CG, 2, conv_ln_g), (PC_CBB, 2, conv_ln_b)):
                act_e.dma_start(par_rows[c0:c0 + n, :, :], src.rearrange("l (k p) -> k l p", p=P)).then_inc(rows_loaded, 16)
            act_e.dma_start(par_rows[PC_CW:PC, :, :], conv_w.rearrange("l t (h p) -> (t h) l p", p=P)).then_inc(rows_loaded, 16)

            def copy_out(key, dst, func=ACT.Identity, **kw):
                wait_ready(act_e, key)
                signals(fn(dst, bank_of(key)[:, 0:dst.free_size()] if len(dst.shape) == 2 else
                           bank_of(key)[:, 0:dst.shape[1] * dst.shape[2]].rearrange("p (a b) -> p a b", a=dst.shape[1]),
                           func, **kw), drained, key)

            def norm(l, which):
                n = 2 * l + (which == "n2")
                for t in range(TT):
                    if n == 0:
                        act_e.wait_ge(x_loaded, 16 * TT)
                    else:
                        act_e.wait_ge(x_updated, TT * (n - 1) + t + 1)
                    step(fn(junk[:, :], x_tok[:, t, :], ACT.Square, accum_out=ssq[:, t:t + 1]))
                    fn(rms[:, t:t + 1], ssq[:, t:t + 1], ACT.Sqrt, scale=1.0 / D, bias=eps[:, :]).then_inc(rms_ready, 1)
                if n < 3:
                    first = {0: ("in", 0, "q"), 1: ("h1", "dense", 0), 2: ("in", 1, "q")}[n]
                    hi_until(plan.split[plan.index[first]] + (SLOTS - 1 if n == 1 else HI - 1))
                for j in range(4):
                    wait_ready(act_e, (which, l, j))
                    for k in (2 * j, 2 * j + 1):
                        c = (PC_N1 if which == "n1" else PC_N2) + k
                        last = fn(h_hi[:, k, :], bank_of((which, l, j))[:, T * (k % 2):T * (k % 2) + T], ACT.Copy,
                                  scale=par[:, l, c:c + 1])
                    last.then_inc(h_hi_ready, 1)

            def hooks(l, g):
                if g == -1:
                    act_e.wait_ge(z_shifted, l + 1)
                    for t in range(TT):
                        last = fn(junk[:, BR * t:BR * t + BR], zv[:, t, :], ACT.Square, accum_out=zss[:, t:t + 1])
                    step(last)
                    fn(zrms[:, :], zss[:, :], ACT.Sqrt, scale=1.0 / BR, bias=eps[:, :]).then_inc(z_rooted, 1)
                    act_e.wait_ge(lam_summed, l + 1)
                    fn(lame[:, :], lams[:, :], ACT.Exp).then_inc(lam_exped, 1)
                    copy_out(("qT", l), qT[:, :, :])
                if g == 0:
                    for b in range(4):
                        copy_out(("s", l, 1, b), sc1[:, b::4, :])
                if g == 1:
                    for b in range(4):
                        wait_ready(act_e, ("s", l, 0, b))
                        signals(fn(sc0[:, b::4, :], bank[b][:, :].rearrange("p (c k) -> p c k", c=CT)[:, :, 0:P], ACT.Identity),
                                drained, ("s", l, 0, b))
                if g in (2, 3):
                    qb = 3 - g
                    sc = sc1 if qb else sc0
                    act_e.wait_ge(nmax_ready, 2 * l + g - 1)
                    for m in range(MAPS):
                        last = fn(sc[:, m, :], sc[:, m, :], ACT.Exp, scale=SCALE, bias=nmax[:, qb, m:m + 1],
                                  accum_out=esum[:, qb, m:m + 1])
                    last.then_inc(exp_ready, 1)
                if g == 3:
                    wait_ready(act_e, ("pool", l))
                    for c in range(CT):
                        last = fn(yT[0][:, c, :], bank_of(("pool", l))[:, T * c:T * c + T], ACT.Copy,
                                  scale=par[:, l, PC_PS + c:PC_PS + c + 1])
                    signals(last, drained, ("pool", l))
                if g == 9 - 1:
                    act_e.wait_ge(c_shifted, l + 1)
                    fn(csq[:, :, :], cy[:, :, :], ACT.Square).then_inc(c_squared, 1)
                if g == 9:
                    wait_ready(act_e, ("var", l))
                    signals(fn(crms[:, :], bank_of(("var", l))[:, 0:T], ACT.Sqrt, bias=eps[:, :]), drained, ("var", l))
                if g == 10:
                    for b in (0, 2):
                        copy_out(("aT", l, b), aT[:, 4 * b:4 * b + 4, :])
                    act_e.wait_ge(c_normed, l + 1)
                    for c in range(CT):
                        last = fn(yT[2][:, c, :], cy[:, c, :], ACT.Silu, scale=par[:, l, PC_CG + c:PC_CG + c + 1],
                                  bias=par[:, l, PC_CBB + c:PC_CBB + c + 1])
                    last.then_inc(yc_ready, 1)
                if g == 11:
                    wait_ready(act_e, ("o", l))
                    fn(osq[:, :, :], bank_of(("o", l))[:, :].rearrange("p (m d) -> p m d", m=MAPS), ACT.Square).then_inc(o_squared, 1)
                    act_e.wait_ge(o_summed, l + 1)
                    fn(orms[:, :], oss[:, :], ACT.Sqrt, scale=1.0 / VD, bias=eps[:, :]).then_inc(o_rooted, 1)
                if g == 14:
                    copy_out(("ybT", l), yT[1][:, :, :])

            def ffn(key, nsteps, e=None):
                if key == "dense":
                    hi_until(plan.split[plan.index[("h1", key, 0)]] + HI - 1)
                for s in range(nsteps + 1):
                    for w in ("h1", "h3", "w2"):
                        ukey = (w, key, s - (w == "w2"))
                        if ukey not in plan.index:
                            continue
                        if w == "h1":
                            wait_ready(act_e, ukey, e)
                            if s >= 2:
                                act_e.wait_ge(act_ready, act_count(key, s - 2, e))
                            signals(fn(sil[:, s % 2, :], bank_of(ukey)[:, :], ACT.Silu), drained, ukey)
                        if key == "dense":
                            after(ukey)
                        else:
                            expert_hi(ukey, e)

            def expert_hi(ukey, e):
                i = plan.index[ukey] - plan.moe_base + HI
                if i < plan.moe_units:
                    split_hi(m_moe + i, e)
                else:
                    with act_e.If(e < E - 1):
                        split_hi(m_moe + i - plan.moe_units, e + 1)

            def y_hi(l, n):
                i = BR_ORDER[n]
                if i == 0:
                    wait_drained(act_e, ("pool", l))
                elif i == 1:
                    wait_drained(act_e, ("ybT", l))
                elif i == 2:
                    act_e.wait_ge(yc_ready, l + 1)
                else:
                    wait_drained(act_e, ("sv", l))
                if n >= 2:
                    wait_ready(act_e, ("br", l, BR_ORDER[n - 2], 3))
                fn(act_hi[:, n % 2, :], yT[i].rearrange("p c t -> p (c t)"), ACT.Copy).then_inc(y_hi_ready, 1)

            act_e.wait_ge(eps_set, 1)
            for l in range(L):
                copy_out(("par", l), par[:, l, :], ACT.Identity)
            for l in range(L):
                wait_drained(act_e, ("par", l))
            for l in range(L):
                norm(l, "n1")
                for w in IN_ORDER:
                    key = (w, l)
                    if w in ("q", "k"):
                        copy_out(key, qk_raw[:, :, int(w == "k"), :])
                        if w == "k":
                            wait_drained(act_e, key)
                            wait_drained(act_e, ("q", l))
                            fn(qk_sq[:, :, :].rearrange("p m d -> p (m d)"), qk_raw[:, :, :, :].rearrange("p t i c -> p (t i c)"),
                               ACT.Square).then_inc(qk_squared, 1)
                    elif w == "v":
                        copy_out(key, v_tok[:, :, :])
                        act_e.wait_ge(qk_summed, l + 1)
                        fn(qk_rms[:, :], qk_ss[:, :], ACT.Sqrt, scale=1.0 / QK, bias=eps[:, :]).then_inc(qk_rooted, 1)
                        if l == 0:
                            for j in range(L):
                                copy_out(("wsT", j), wT[:, j, :, :])
                    elif w == "cg":
                        copy_out(key, sig[:, :, :], ACT.Sigmoid)
                    elif w == "dv":
                        wait_ready(act_e, key)
                        for t in range(TT):
                            last = fn(zv[:, t, :], bank_of(key)[:, T * t:T * t + BR], ACT.Gelu, accum_out=zsum[:, t:t + 1])
                        signals(last, drained, key)
                    elif w == "du":
                        copy_out(key, zu[:, :, :], ACT.Gelu)
                    elif w == "pa":
                        copy_out(key, w1s[:, :, PPAD:PPAD + T])
                    elif w == "ca":
                        pass
                    after(("in", l, w))
                hooks(l, -1)
                for g in range(16):
                    wait_ready(act_e, ("g", l, g))
                    for c in range(2):
                        d = 2 * g + c
                        last = fn(gates[:, d, :], bank_of(("g", l, g))[:, T * c:T * c + T], ACT.Sigmoid,
                                  bias=par[:, l, PC_BG + d:PC_BG + d + 1])
                    signals(last, drained, ("g", l, g))
                    after(("gate", l, g))
                    hooks(l, g)
                    if g == 12:
                        y_hi(l, 0)
                        y_hi(l, 1)
                y_hi(l, 2)
                after(("branch", l, BR_ORDER[0]))
                y_hi(l, 3)
                if l == 0:
                    act_e.wait_ge(bcast_loaded, 16 * BCASTS)
                    fn(router_hi[:, :, :], router[:, :, :], ACT.Copy).then_inc(router_split_hi, 1)
                norm(l, "n2")
                if l == 0:
                    ffn("dense", S_DENSE)
            act_e.wait_ge(diff_ready, 1)
            fn(ed[:, :], diff[:, :], ACT.Exp).then_inc(ed_ready, 1)

            def turned_hi(s, e):
                wait_ready(act_e, ("turn", s), e)
                fn(act_hi[:, s % 2, 0:2 * CAP], bank_of(("turn", s))[:, 0:2 * CAP], ACT.Copy).then_inc(act_hi_ready, 1)

            def gathered_expert(e):
                for s in range(S_MOE + 1):
                    if s < S_MOE:
                        wait_ready(act_e, ("h1", "moe", s), e)
                    if 1 <= s < S_MOE:
                        turned_hi(s - 1, e)
                    if s < S_MOE:
                        key = ("h1", "moe", s)
                        signals(fn(sil[:, s % 2, 0:US], bank_of(key)[:, 0:US], ACT.Silu), drained, key)
                        expert_hi(key, e)
                        if s == S_MOE - 1:
                            wait_ready(act_e, ("h3", "moe", s), e)
                            act_e.wait_ge(xg_taken, e + 2)
                            fn(h_hi[:, :, 0:CAP], xg, ACT.Copy).then_inc(xg_hi_ready, 1)
                            turned_hi(s, e)
                        expert_hi(("h3", "moe", s), e)
                    if s >= 1:
                        expert_hi(("w2", "moe", s - 1), e)
                    if s == 4:
                        wait_ready(act_e, "gates", e)
                        signals(fn(gatesT, bank[2][:, 0:TT * P].rearrange("p (t n) -> p t n", t=TT), ACT.Copy), drained, "gates")
                act_e.wait_ge(acc_unit_used, acc_at("moe", S_MOE - 1, e))
                for n in range(2):
                    signals(fn(y_slot[:, 512 * n:512 * n + 512], bank[n][:, :], ACT.Copy), drained, ("ys", n))

            for i in range(HI):
                split_hi(m_moe + i, 0)
            act_e.wait_ge(most_ready, 1)
            most_tokens = act_e.value_load(most_i[0:1, 0:1])
            with act_e.If(most_tokens > CAP):
                with act_e.Fori(0, E) as e:
                    ffn("moe", S_MOE, e)
            with act_e.Else():
                act_e.wait_ge(buffers_zero, 1)
                act_e.wait_ge(xg_taken, 1)
                fn(h_hi[:, :, 0:CAP], xg, ACT.Copy).then_inc(xg_hi_ready, 1)
                with act_e.Fori(0, E) as e:
                    gathered_expert(e)

        @block.vector
        def _(dve):
            steps = [0]
            tt, ts, stt = dve.tensor_tensor, dve.tensor_scalar, dve.scalar_tensor_tensor

            def step(ins):
                steps[0] += 1
                ins.then_inc(dve_step, 1)
                dve.wait_ge(dve_step, steps[0])

            def norm(l, which):
                n = 2 * l + (which == "n2")
                for t in range(TT):
                    dve.wait_ge(rms_ready, TT * n + t + 1)
                    step(dve.reciprocal(rstd[:, t:t + 1], rms[:, t:t + 1]))
                    ts(xn[:, t, :], x_tok[:, t, :], rstd[:, t:t + 1], None, ALU.mult).then_inc(xn_ready, 1)
                if n == 1:
                    first_lo(("h1", "dense", 0), range(LO_AHEAD))
                for j in range(4):
                    dve.wait_ge(h_hi_ready, 4 * n + j + 1)
                    for k in (2 * j, 2 * j + 1):
                        c = (PC_N1 if which == "n1" else PC_N2) + k
                        last = stt(out=h_lo[:, k, :], in0=bank_of((which, l, j))[:, T * (k % 2):T * (k % 2) + T],
                                   scalar=par[:, l, c:c + 1], in1=h_hi[:, k, :].bitcast(F32), op0=ALU.mult, op1=ALU.subtract)
                    signals(last, drained, (which, l, j))

            def add_y(key, e=None, scale=None):
                for t in range(TT):
                    for n in range(2):
                        k = ("y", key, 2 * t + n)
                        xs = x_tok[:, t, 512 * n:512 * n + 512]
                        if key == "moe":
                            dve.wait_ge(acc_unit_used, acc_at("moe", S_MOE - 1, e))
                        else:
                            wait_ready(dve, k, e)
                        if scale is None:
                            tt(xs, bank_of(k)[:, :], xs, ALU.add).then_inc(drained[2 * t + n], 1)
                        else:
                            stt(out=xs, in0=bank_of(k)[:, :], scalar=scale(t), in1=xs, op0=ALU.mult, op1=ALU.add)\
                                .then_inc(drained[2 * t + n], 1)
                    if key != "moe":
                        wait_drained(dve, ("y", key, 2 * t), e)
                        wait_drained(dve, ("y", key, 2 * t + 1), e)
                        dve.sem_inc(x_updated, 1)

            def rope(l):
                dve.wait_ge(qk_squared, l + 1)
                dve.tensor_reduce(qk_ss[:, :], qk_sq[:, :, :], AX, ALU.add).then_inc(qk_summed, 1)
                dve.wait_ge(qk_rooted, l + 1)
                step(dve.reciprocal(qk_rstd[:, :], qk_rms[:, :]))
                flat = "p t i (m d) -> p (t i m) d"
                step(tt(qk_raw[:, :, :, :].rearrange(flat, d=QK), qk_raw[:, :, :, :].rearrange(flat, d=QK),
                        qk_rstd[:, :].unsqueeze(2).to_broadcast([P, TT * 2 * MAPS, QK]), ALU.mult))
                for i in range(2):
                    v = qk_raw[:, :, i, :].rearrange("p t (m d) -> p t m d", d=QK)
                    last = tt(v, v, qkg[:, l, i, :].unsqueeze(1).unsqueeze(1).to_broadcast([P, TT, MAPS, QK]), ALU.mult)
                step(last)
                v = qk_raw[:, :, :, :].rearrange("p t i (m d) -> p t (i m) d", d=QK)
                r = rot[:, :, :, :].rearrange("p t i (m d) -> p t (i m) d", d=QK)
                lo, hi = slice(0, 16), slice(16, 32)
                c = cos.unsqueeze(2).to_broadcast([P, TT, 16, 16])
                s = sin.unsqueeze(2).to_broadcast([P, TT, 16, 16])
                tt(ra[:, :, :, :], v[:, :, :, lo], c, ALU.mult)
                step(tt(rb[:, :, :, :], v[:, :, :, hi], s, ALU.mult))
                step(tt(r[:, :, :, lo], ra[:, :, :, :], rb[:, :, :, :], ALU.subtract))
                tt(ra[:, :, :, :], v[:, :, :, hi], c, ALU.mult)
                step(tt(rb[:, :, :, :], v[:, :, :, lo], s, ALU.mult))
                tt(r[:, :, :, hi], ra[:, :, :, :], rb[:, :, :, :], ALU.add).then_inc(rot_ready, 1)

            def pooling(l):
                now = slice(PPAD, PPAD + T)
                wait_drained(dve, ("pa", l))
                dve.memset(w2s[:, :, 0:PPAD], 0.0)
                step(dve.memset(w4s[:, :, 0:PPAD], 0.0))
                for g, (a, b, back) in enumerate(((w1s, w2s, 1), (w2s, w4s, 2), (w4s, w2s, 4), (w2s, w4s, 8))):
                    rows = slice(64 * (g % 2), 64 * (g % 2) + 64)
                    step(tt(b[:, :, now], a[:, :, now], a[:, :, PPAD - back:PPAD - back + T], ALU.add))
                    step(tt(pooled[rows, g // 2, :], b[rows, g // 2, now], invcnt[rows, g // 2, :], ALU.mult))
                tt(pooled[:, :, :], pooled[:, :, :], w1s[:, :, now], ALU.subtract).then_inc(pooled_ready, 1)

            def lam(l):
                step(tt(lamp[:, :, :], lamv[:, l, :, 0, :], lamv[:, l, :, 1, :], ALU.mult))
                dve.tensor_reduce(lams[:, :], lamp[:, :, :], AX, ALU.add).then_inc(lam_summed, 1)

            def z_norm_shift(l):
                wait_drained(dve, ("dv", l))
                step(ts(znm[:, :], zsum[:, :], -1.0 / BR, None, ALU.mult))
                for t in range(TT):
                    last = ts(zv[:, t, :], zv[:, t, :], znm[:, t:t + 1], None, ALU.add)
                last.then_inc(z_shifted, 1)

            def z_norm_scale(l):
                dve.wait_ge(z_rooted, l + 1)
                step(dve.reciprocal(zrstd[:, :], zrms[:, :]))
                for t in range(TT):
                    last = stt(out=zv[:, t, :], in0=zv[:, t, :], scalar=zrstd[:, t:t + 1], in1=slg[:, l, :],
                               op0=ALU.mult, op1=ALU.mult)
                step(last)
                tt(zv[:, :, :], zv[:, :, :], slb[:, l, :].unsqueeze(1).to_broadcast([P, TT, BR]), ALU.add).then_inc(z_normed, 1)

            def row_max(l, qb):
                sc = sc1 if qb else sc0
                keys = P * (qb + 1)
                for b in range(4):
                    wait_drained(dve, ("s", l, qb, b))
                step(dve.memset(sc[0:64, :, keys - 64:keys], MASKED))
                step(dve.tensor_reduce(smax[:, qb, :], sc[:, :, :], AX, ALU.max))
                ts(nmax[:, qb, :], smax[:, qb, :], -SCALE, None, ALU.mult).then_inc(nmax_ready, 1)

            def conv(l):
                for k in range(TAPS):
                    for c in range(CT):
                        col = PC_CW + 2 * k + c
                        if k == 0:
                            ins = ts(cy[:, c, :], u_pad[:, c, 0:T], par[:, l, col:col + 1],
                                     par[:, l, PC_CB + c:PC_CB + c + 1], ALU.mult, ALU.add)
                        else:
                            dve.wait_ge(dve_step, steps[0] - 1)
                            ins = stt(out=cy[:, c, :], in0=u_pad[:, c, k:k + T], scalar=par[:, l, col:col + 1],
                                      in1=cy[:, c, :], op0=ALU.mult, op1=ALU.add)
                        if k == TAPS - 1 and c == CT - 1:
                            ins.then_inc(conv_ready, 1)
                        else:
                            steps[0] += 1
                            ins.then_inc(dve_step, 1)

            def combine(l):
                dve.wait_ge(exp_ready, 2 * l + 2)
                step(dve.reciprocal(erec[:, :, :], esum[:, :, :]))
                step(ts(elam[:, :, :], erec[:, :, :], neglam[:, l:l + 1], None, ALU.mult))
                for sc, qb in ((sc1, 1), (sc0, 0)):
                    for h in range(HEADS):
                        last = ts(sc[:, 2 * h + 1, :], sc[:, 2 * h + 1, :], elam[:, qb, 2 * h + 1:2 * h + 2], None, ALU.mult)
                step(last)
                for sc, qb in ((sc1, 1), (sc0, 0)):
                    for h in range(HEADS):
                        last = stt(out=sc[:, 2 * h, :], in0=sc[:, 2 * h, :], scalar=erec[:, qb, 2 * h:2 * h + 1],
                                   in1=sc[:, 2 * h + 1, :], op0=ALU.mult, op1=ALU.add)
                last.then_inc(a_ready, 1)

            def y_lo(l, n):
                dve.wait_ge(y_hi_ready, 4 * l + n + 1)
                tt(act_lo[:, n % 2, :], yT[BR_ORDER[n]].rearrange("p c t -> p (c t)"), act_hi[:, n % 2, :].bitcast(F32),
                   ALU.subtract).then_inc(y_ready, 1)

            def o_norm(l):
                dve.wait_ge(o_squared, l + 1)
                dve.tensor_reduce(oss[:, :], osq[:, :, :], AX, ALU.add).then_inc(o_summed, 1)
                dve.wait_ge(o_rooted, l + 1)
                step(dve.reciprocal(orstd[:, :], orms[:, :]))
                wait_ready(dve, ("o", l))
                signals(tt(o_n[:, :, :], bank_of(("o", l))[:, :].rearrange("p (m d) -> p m d", m=MAPS),
                           orstd[:, :].unsqueeze(2).to_broadcast([P, MAPS, VD]), ALU.mult), drained, ("o", l))
                wait_drained(dve, ("o", l))
                tt(o_n[:, :, :], o_n[:, :, :], subg[:, l, :].unsqueeze(1).to_broadcast([P, MAPS, VD]), ALU.mult)\
                    .then_inc(o_normed, 1)

            def lo_after(ukey, e=None):
                n = plan.index[ukey]
                m = plan.split[n] + LO_AHEAD
                if e is None:
                    if m < m_moe and lo_engine(m) == "dve":
                        split_lo(dve, m)
                elif m < m_moe + plan.moe_units:
                    split_lo(dve, m, e)
                else:
                    with dve.If(e < E - 1):
                        split_lo(dve, m - plan.moe_units, e + 1)

            def first_lo(ukey, which, e=None):
                m = plan.split[plan.index[ukey]]
                for i in which:
                    if lo_engine(m + i) == "dve":
                        split_lo(dve, m + i, e)

            def ffn(key, nsteps, e=None):
                for s in range(nsteps + 1):
                    for w in ("h1", "h3", "w2"):
                        ukey = (w, key, s - (w == "w2"))
                        if ukey not in plan.index:
                            continue
                        lo_after(ukey, e)
                        if w != "h3":
                            continue
                        wait_drained(dve, ("h1", key, s), e)
                        wait_ready(dve, ukey, e)
                        if s >= 2:
                            dve.wait_ge(acc_unit_used, acc_at(key, s - 2, e))
                        g = sil[:, s % 2, :]
                        signals(tt(g, bank_of(ukey)[:, :], g, ALU.mult), drained, ukey)
                        wait_drained(dve, ukey, e)
                        dve.tensor_copy(act_hi[:, s % 2, :], g).then_inc(act_hi_dve, 1)
                        dve.wait_ge(act_hi_dve, act_count(key, s, e))
                        tt(act_lo[:, s % 2, :], g, act_hi[:, s % 2, :].bitcast(F32), ALU.subtract).then_inc(act_ready, 1)

            dve.memset(eps[:, :], EPS).then_inc(eps_set, 1)
            dve.wait_ge(const_loaded, 16)
            dve.wait_ge(x_loaded, 16 * TT)
            wait_drained(dve, ("par", 0))
            wait_drained(dve, ("par", 1))
            dve.wait_ge(pads_zero, 1)
            for l in range(L):
                norm(l, "n1")
                if l == 0:
                    dve.wait_ge(bcast_loaded, 16 * BCASTS)
                    for j in range(L):
                        step(ts(subg[:, j, :], subg[:, j, :], 1.0 - lam_init[j], None, ALU.mult))
                lam(l)
                rope(l)
                wait_ready(dve, ("ca", l))
                wait_drained(dve, ("cg", l))
                signals(tt(u_pad[:, :, PAD:PAD + T], bank_of(("ca", l))[:, :].rearrange("p (c t) -> p c t", c=CT), sig[:, :, :], ALU.mult),
                        drained, ("ca", l))
                z_norm_shift(l)
                z_norm_scale(l)
                dve.wait_ge(lam_exped, l + 1)
                step(stt(out=neglam[:, l:l + 1], in0=lame[:, 1:2], scalar=-lam_init[l], in1=lame[:, 0:1],
                         op0=ALU.add, op1=ALU.subtract))
                wait_ready(dve, ("kT", l))
                signals(dve.tensor_copy(kT[:, :, :], bank_of(("kT", l))[:, :].rearrange("p (c t) -> p c t", c=CT)), drained, ("kT", l))
                row_max(l, 1)
                row_max(l, 0)
                pooling(l)
                wait_drained(dve, ("ca", l))
                conv(l)
                combine(l)
                wait_ready(dve, ("sv", l))
                wait_drained(dve, ("du", l))
                step(tt(yT[3][:, :, :].rearrange("p c (n t) -> p c n t", n=TT),
                        bank_of(("sv", l))[:, :].rearrange("p (c n t) -> p c n t", c=CT, n=TT),
                        sgub[:, l, :, :].unsqueeze(2).to_broadcast([P, CT, TT, P]), ALU.add))
                signals(tt(yT[3][:, :, :], yT[3][:, :, :], zu[:, :, :], ALU.mult), drained, ("sv", l))
                wait_ready(dve, ("mean", l))
                dve.wait_ge(conv_ready, l + 1)
                mean = bank_of(("mean", l))[:, 0:T].unsqueeze(1).to_broadcast([P, CT, T])
                tt(cy[:, :, :], cy[:, :, :], mean, ALU.subtract).then_inc(c_shifted, 1)
                dve.wait_ge(c_shifted, l + 1)
                dve.sem_inc(drained[plan.jobs[("mean", l)][0]], 1)
                wait_drained(dve, ("var", l))
                step(dve.reciprocal(crms[:, :], crms[:, :]))
                tt(cy[:, :, :], cy[:, :, :], crms[:, :].unsqueeze(1).to_broadcast([P, CT, T]), ALU.mult).then_inc(c_normed, 1)
                wait_ready(dve, ("aT", l, 1))
                signals(dve.tensor_copy(aT[:, 4:8, :], bank[1][:, :].rearrange("p (a b) -> p a b", a=4)), drained, ("aT", l, 1))
                o_norm(l)
                y_lo(l, 0)
                y_lo(l, 1)
                for n, i in enumerate(BR_ORDER):
                    if n >= 1 and n + 1 < NGATE:
                        y_lo(l, n + 1)
                    for q in range(4):
                        key = ("br", l, i, q)
                        wait_ready(dve, key)
                        m = merged[:, 2 * q:2 * q + 2, :].rearrange("p k t -> p (k t)")
                        gt = gates[:, KT * i + 2 * q:KT * i + 2 * q + 2, :].rearrange("p k t -> p (k t)")
                        if n == 0:
                            signals(tt(m, bank_of(key)[:, :], gt, ALU.mult), drained, key)
                        else:
                            signals(tt(prod[:, q % 2, :], bank_of(key)[:, :], gt, ALU.mult), drained, key)
                            wait_drained(dve, key)
                            ins = tt(m, m, prod[:, q % 2, :], ALU.add)
                            if n == 3:
                                ins.then_inc(merged_ready, 1)
                            else:
                                step(ins)
                add_y(("out", l))
                norm(l, "n2")
                if l == 0:
                    ffn("dense", S_DENSE)
                    add_y("dense")

            dve.wait_ge(router_split_hi, 1)
            tt(router_lo[:, :, :], router[:, :, :], router_hi[:, :, :].bitcast(F32), ALU.subtract).then_inc(router_split, 1)
            wait_ready(dve, "logits")
            signals(dve.tensor_copy(lg[:, :, :], bank_of("logits")[:, 0:TT * E].rearrange("p (t e) -> p t e", t=TT)), drained, "logits")
            wait_drained(dve, "logits")
            now = slice(1, E + 1)
            dve.memset(chosen[:, :, :], 0.0)
            dve.memset(place[:, :, :], 0.0)
            dve.memset(gate[:, :, :], 0.0)
            for e in range(E):
                last = dve.memset(rank[:, :, e:e + 1], float(E - e))
            step(last)

            def wide(col):
                return col.unsqueeze(2).to_broadcast([P, TT, E])

            def first_max(src, top, hot):
                step(dve.tensor_reduce(top[:, :], src[:, :, :], AX, ALU.max))
                step(tt(eq[:, :, :], src[:, :, :], wide(top[:, :]), ALU.is_equal))
                step(tt(eq[:, :, :], eq[:, :, :], rank[:, :, :], ALU.mult))
                step(dve.tensor_reduce(best[:, :], eq[:, :, :], AX, ALU.max))
                step(tt(hot[:, :, :], rank[:, :, :], wide(best[:, :]), ALU.is_equal))

            first_max(lg, top1, hot1)
            step(stt(out=lg2[:, :, :].rearrange("p t e -> p (t e)"), in0=hot1[:, :, :].rearrange("p t e -> p (t e)"), scalar=-3e38,
                     in1=lg[:, :, :].rearrange("p t e -> p (t e)"), op0=ALU.mult, op1=ALU.add))
            first_max(lg2, top2, hot2)
            tt(chosen[:, :, now], hot1[:, :, :], hot2[:, :, :], ALU.add).then_inc(chosen_ready, 1)
            tt(diff[:, :], top2[:, :], top1[:, :], ALU.subtract).then_inc(diff_ready, 1)
            dve.wait_ge(ed_ready, 1)
            step(ts(den[:, :], ed[:, :], 1.0, None, ALU.add))
            step(dve.reciprocal(wt1[:, :], den[:, :]))
            step(tt(wt2[:, :], ed[:, :], wt1[:, :], ALU.mult))
            step(tt(hot1[:, :, :], hot1[:, :, :], wide(wt1[:, :]), ALU.mult))
            step(tt(hot2[:, :, :], hot2[:, :, :], wide(wt2[:, :]), ALU.mult))
            tt(gate[:, :, now], hot1[:, :, :], hot2[:, :, :], ALU.add).then_inc(gate_ready, 1)

            wait_ready(dve, "places")
            dve.tensor_copy(place[:, :, now], bank_of("places")[:, 0:TT * E].rearrange("p (t e) -> p t e", t=TT))
            signals(dve.tensor_reduce(most[:, :], bank_of("places")[:, 2 * E:3 * E], AX, ALU.max), drained, "places")
            wait_drained(dve, "places")
            dve.tensor_copy(most_i[:, :], most[:, :]).then_inc(most_ready, 1)
            dve.wait_ge(gate_ready, 1)
            dve.wait_ge(most_ready, 1)

            def choose(dst, weight, col):
                for t in range(TT):
                    last = ts(dst[:, t, :], iota, place[:, t, col], weight[:, t, col], ALU.is_equal, ALU.mult)
                return last

            def gathered_out(which, e=None):
                if e is not None:
                    dve.wait_ge(xg_ready, e + 1)
                for b in (2, 3):
                    key = ("gather", which, b)
                    wait_ready(dve, key, e)
                    c = PC_N2 + 4 * (b - 2)
                    signals(tt(xg[:, 4 * (b - 2):4 * (b - 2) + 4, :], bank[b][:, 0:4 * CAP].rearrange("p (k n) -> p k n", k=4),
                               par[:, L - 1, c:c + 4].unsqueeze(2).to_broadcast([P, 4, CAP]), ALU.mult), drained, key)
                    wait_drained(dve, key, e)
                dve.sem_inc(xg_taken, 1)

            def add_spread(t, e=None, tail=()):
                for n in range(2):
                    key = ("spread", t, n, *tail)
                    xs = x_tok[:, t, 512 * n:512 * n + 512]
                    wait_ready(dve, key, e)
                    signals(tt(xs, bank_of(key)[:, :], xs, ALU.add), drained, key)

            def turned_lo(s, e):
                dve.wait_ge(act_hi_ready, S_MOE * e + s + 1)
                signals(tt(act_lo[:, s % 2, 0:2 * CAP], bank_of(("turn", s))[:, 0:2 * CAP],
                           act_hi[:, s % 2, 0:2 * CAP].bitcast(F32), ALU.subtract), drained, ("turn", s))

            def gathered_expert(e):
                choose(pick_g, gate, bass.ds(e + 1, 1)).then_inc(pick_g_ready, 1)
                choose(pick, chosen, bass.ds(e + 2, 1)).then_inc(pick_ready, 1)
                for s in range(S_MOE + 1):
                    if s < S_MOE:
                        lo_after(("h1", "moe", s), e)
                    if 1 <= s < S_MOE:
                        turned_lo(s - 1, e)
                    if s < S_MOE:
                        key = ("h3", "moe", s)
                        lo_after(key, e)
                        wait_drained(dve, ("h1", "moe", s), e)
                        wait_ready(dve, key, e)
                        signals(tt(sil[:, s % 2, 0:US], bank_of(key)[:, 0:US], sil[:, s % 2, 0:US], ALU.mult), drained, key)
                    if s == S_MOE - 1:
                        turned_lo(s, e)
                    if s >= 1:
                        lo_after(("w2", "moe", s - 1), e)
                    if s in (2, 3):
                        add_spread(s - 2, e)
                    if s == 6:
                        gathered_out("next", e)

            first_lo(("h1", "moe", 0), range(LO_AHEAD), 0)
            most_tokens = dve.value_load(most_i[0:1, 0:1])
            with dve.If(most_tokens > CAP):
                with dve.Fori(0, E) as e:
                    ffn("moe", S_MOE, e)
                    add_y("moe", e, lambda t: gate[:, t, bass.ds(e + 1, 1)])
                for b in range(4):
                    wait_drained(dve, ("y", "moe", b), E - 1)
                dve.sem_inc(x_final, 1)
            with dve.Else():
                dve.memset(y_slot, 0.0)
                dve.memset(gatesT[:, :, :], 0.0).then_inc(buffers_zero, 1)
                dve.wait_ge(buffers_zero, 1)
                choose(pick, chosen, slice(1, 2)).then_inc(pick_ready, 1)
                gathered_out("first")
                with dve.Fori(0, E) as e:
                    gathered_expert(e)
                for t in range(TT):
                    add_spread(t, None, ("end",))
                for n in range(2):
                    wait_drained(dve, ("spread", TT - 1, n, "end"))
                dve.sem_inc(x_final, 1)


_INS = ['x', 'norm1_g', 'w_in', 'w_gate', 'b_gate', 'w_branch', 'w_out', 'pool_w', 'pool_scale', 'attn_qn_g', 'attn_kn_g',
        'lam_q1', 'lam_k1', 'lam_q2', 'lam_k2', 'attn_subln_g', 'conv_w', 'conv_b', 'conv_ln_g', 'conv_ln_b', 'sgu_ln_g',
        'sgu_ln_b', 'sgu_w', 'sgu_b', 'norm2_g', 'ffn_w1', 'ffn_w3', 'ffn_w2', 'moe_router', 'moe_w1', 'moe_w3', 'moe_w2']


def kernel(**inputs):
    import concourse.bacc as _bacc
    from concourse.bass_utils import run_bass_kernel_spmd as _run

    nc = _bacc.Bacc("TRN2", target_bir_lowering=False, num_devices=1)
    arrays, args = {}, []
    for name in _INS:
        a = np.ascontiguousarray(inputs[name])
        arrays[f"in_{name}"] = a
        args.append(nc.dram_tensor(f"in_{name}", a.shape, mybir.dt.from_np(a.dtype), kind="ExternalInput").ap())
    arrays["in_table"] = shape_constants()
    args.append(nc.dram_tensor("in_table", (P, C_N), F32, kind="ExternalInput").ap())
    args.append(nc.dram_tensor("out_y", (1, T, D), F32, kind="ExternalOutput").ap())
    trunk_kernel(nc, *args)
    r = _run(nc, [arrays], core_ids=[0])
    return r.results[0]["out_y"]
```
